# Optimizing a Trainium2 kernel written in Bass

```python
import math
import jax, jax.numpy as jnp
from jax import lax
import numpy as np

D_MODEL = 1024
BATCH = 1
SEQ = 256
DEPTH = 1

CHUNK = 64
Q_BLOCK = 128
EPS = 1e-6

DIFF_HEADS = 8
DIFF_DH = 64
DIFF_W = DIFF_HEADS * 2 * DIFF_DH

CH_HEADS = 8
CH_DH = 64
CH_W = CH_HEADS * CH_DH
CH_LEFT = 8
REL_CLIP = 128

PEER_HEADS = 8
PEER_NKEYS = 128
PEER_NEXP = PEER_NKEYS * PEER_NKEYS
PEER_DKEY = 128
PEER_TOPK = 16
PEER_BLOCK = 128

IN_SIZES = (DIFF_W, DIFF_W, DIFF_W, CH_W, CH_W, CH_W, D_MODEL, D_MODEL)
IN_COLS = sum(IN_SIZES)
IN_SPLITS = tuple(int(s) for s in np.cumsum(IN_SIZES)[:-1])


def rmsnorm(x, w):
    xf = x.astype(jnp.float32)
    y = xf * lax.rsqrt(jnp.mean(xf * xf, axis=-1, keepdims=True) + EPS)
    return (y * w.astype(jnp.float32)).astype(x.dtype)

def alibi_slopes(n_heads):
    return jnp.exp2(-8.0 * jnp.arange(1, n_heads + 1, dtype=jnp.float32) / n_heads)

def diff_attention(q, k, v, lq1, lk1, lq2, lk2, subln_w, lam_init):
    B, S = q.shape[0], q.shape[1]
    nqb = S // Q_BLOCK
    f32 = jnp.float32
    lam = (jnp.exp(jnp.sum(lq1.astype(f32) * lk1.astype(f32)))
           - jnp.exp(jnp.sum(lq2.astype(f32) * lk2.astype(f32))) + lam_init)
    k1, k2 = k[..., 0, :], k[..., 1, :]
    qb = jnp.moveaxis(q.reshape(B, nqb, Q_BLOCK, DIFF_HEADS, 2, DIFF_DH), 1, 0)
    slopes = alibi_slopes(DIFF_HEADS)
    kpos = jnp.arange(S, dtype=jnp.int32)
    scale = DIFF_DH ** -0.5

    def block(args):
        qblk, bi = args
        qpos = bi * Q_BLOCK + jnp.arange(Q_BLOCK, dtype=jnp.int32)
        dist = jnp.abs(qpos[:, None] - kpos[None, :]).astype(f32)
        bias = -slopes[:, None, None] * dist
        allowed = (kpos[None, :] // CHUNK) <= (qpos[:, None] // CHUNK)

        def probs(qq, kk):
            s = jnp.einsum('bqhd,bkhd->bhqk', qq, kk).astype(f32) * scale + bias
            return jax.nn.softmax(jnp.where(allowed, s, -jnp.inf), axis=-1)

        a = probs(qblk[..., 0, :], k1) - lam * probs(qblk[..., 1, :], k2)
        return jnp.einsum('bhqk,bkhe->bqhe', a.astype(v.dtype), v)

    o = lax.map(block, (qb, jnp.arange(nqb, dtype=jnp.int32)))
    o = jnp.moveaxis(o, 0, 1).reshape(B, S, DIFF_HEADS, 2 * DIFF_DH)
    o = rmsnorm(o, subln_w) * (1.0 - lam_init)
    return o.reshape(B, S, DIFF_W)

def chunk_attention(q, k, v, rel_table):
    B, S = q.shape[0], q.shape[1]
    nc = S // CHUNK
    band = (CH_LEFT + 1) * CHUNK
    f32 = jnp.float32
    qc = q.reshape(B, nc, CHUNK, CH_HEADS, CH_DH)
    pad = ((0, 0), (CH_LEFT * CHUNK, 0), (0, 0), (0, 0))
    kp = jnp.pad(k, pad).reshape(B, nc + CH_LEFT, CHUNK, CH_HEADS, CH_DH)
    vp = jnp.pad(v, pad).reshape(B, nc + CH_LEFT, CHUNK, CH_HEADS, CH_DH)
    kb = jnp.concatenate([kp[:, j:j + nc] for j in range(CH_LEFT + 1)], axis=2)
    vb = jnp.concatenate([vp[:, j:j + nc] for j in range(CH_LEFT + 1)], axis=2)
    r = jnp.arange(band, dtype=jnp.int32)
    qi = jnp.arange(CHUNK, dtype=jnp.int32)
    rel = qi[:, None] - r[None, :] + CH_LEFT * CHUNK
    bias = rel_table[:, jnp.clip(rel, -REL_CLIP, REL_CLIP) + REL_CLIP].astype(f32)
    valid = (jnp.arange(nc, dtype=jnp.int32)[:, None] * CHUNK - CH_LEFT * CHUNK + r[None, :]) >= 0
    s = jnp.einsum('bcqhd,bckhd->bhcqk', qc, kb).astype(f32) * (CH_DH ** -0.5) + bias[:, None]
    s = jnp.where(valid[:, None, :], s, -jnp.inf)
    p = jax.nn.softmax(s, axis=-1)
    o = jnp.einsum('bhcqk,bckhd->bcqhd', p.astype(v.dtype), vb)
    return o.reshape(B, S, CH_W)

def peer(xn, wq, keys, u, v):
    B, S, D = xn.shape
    xt = xn.reshape(-1, PEER_BLOCK, D)
    f32 = jnp.float32

    def block(xb):
        q = (xb @ wq).reshape(PEER_BLOCK, PEER_HEADS, 2, PEER_DKEY // 2)
        s1 = jnp.einsum('thd,hnd->thn', q[:, :, 0], keys[:, 0]).astype(f32)
        s2 = jnp.einsum('thd,hnd->thn', q[:, :, 1], keys[:, 1]).astype(f32)
        v1, i1 = lax.top_k(s1, PEER_TOPK)
        v2, i2 = lax.top_k(s2, PEER_TOPK)
        cand = (v1[..., :, None] + v2[..., None, :]).reshape(PEER_BLOCK, PEER_HEADS, PEER_TOPK * PEER_TOPK)
        sc, ci = lax.top_k(cand, PEER_TOPK)
        e = (jnp.take_along_axis(i1, ci // PEER_TOPK, axis=-1) * PEER_NKEYS
             + jnp.take_along_axis(i2, ci % PEER_TOPK, axis=-1))
        g = jax.nn.softmax(sc, axis=-1)
        ue = u[e]
        ve = v[e]
        hid = jnp.einsum('thkd,td->thk', ue, xb).astype(f32)
        a = (jax.nn.gelu(hid, approximate=False) * g).astype(xb.dtype)
        return jnp.einsum('thk,thkd->td', a, ve)

    return lax.map(block, xt).reshape(B, S, D)

def first_inputs(seed: int = 0) -> dict:
    key = jax.random.key(seed)
    ks = jax.random.split(key, 20)
    n = jax.random.normal
    f32 = jnp.float32
    L, D = DEPTH, D_MODEL
    return {
        "x": n(ks[0], (BATCH, SEQ, D), f32),
        "norm1_w": 1.0 + 0.02 * n(ks[1], (L, D), f32),
        "w_in": n(ks[2], (L, D, IN_COLS), f32) * D ** -0.5,
        "b_gate": 0.01 * n(ks[3], (L, 2 * D), f32),
        "diff_lq1": 0.1 * n(ks[4], (L, DIFF_DH), f32),
        "diff_lk1": 0.1 * n(ks[5], (L, DIFF_DH), f32),
        "diff_lq2": 0.1 * n(ks[6], (L, DIFF_DH), f32),
        "diff_lk2": 0.1 * n(ks[7], (L, DIFF_DH), f32),
        "diff_subln_w": 1.0 + 0.02 * n(ks[8], (L, 2 * DIFF_DH), f32),
        "chunk_rel_bias": 0.1 * n(ks[9], (L, CH_HEADS, 2 * REL_CLIP + 1), f32),
        "w_branch_diff": n(ks[10], (L, DIFF_W, D), f32) * DIFF_W ** -0.5,
        "w_branch_chunk": n(ks[11], (L, CH_W, D), f32) * CH_W ** -0.5,
        "w_out": n(ks[12], (L, D, D), f32) * D ** -0.5,
        "norm2_w": 1.0 + 0.02 * n(ks[13], (L, D), f32),
        "peer_wq": n(ks[14], (L, D, PEER_HEADS * PEER_DKEY), f32) * D ** -0.5,
        "peer_keys": n(ks[15], (L, PEER_HEADS, 2, PEER_NKEYS, PEER_DKEY // 2), f32) * (PEER_DKEY // 2) ** -0.5,
        "peer_u": n(ks[16], (L, PEER_NEXP, D), f32) * D ** -0.5,
        "peer_v": n(ks[17], (L, PEER_NEXP, D), f32) * D ** -0.5,
        "final_norm_w": 1.0 + 0.02 * n(ks[18], (D,), f32),
    }

def first_block(x, norm1_w, w_in, b_gate, diff_lq1, diff_lk1, diff_lq2, diff_lk2, diff_subln_w,
              chunk_rel_bias, w_branch_diff, w_branch_chunk, w_out, norm2_w, peer_wq, peer_keys,
              peer_u, peer_v, final_norm_w):
    B, S, D = x.shape
    h = x
    for l in range(DEPTH):
        lam_init = 0.8 - 0.6 * math.exp(-0.3 * l)
        xn = rmsnorm(h, norm1_w[l])
        proj = xn @ w_in[l]
        qd, kd, vd, qc, kc, vc, gd, gc = jnp.split(proj, IN_SPLITS, axis=-1)
        o_d = diff_attention(qd.reshape(B, S, DIFF_HEADS, 2, DIFF_DH),
                             kd.reshape(B, S, DIFF_HEADS, 2, DIFF_DH),
                             vd.reshape(B, S, DIFF_HEADS, 2 * DIFF_DH),
                             diff_lq1[l], diff_lk1[l], diff_lq2[l], diff_lk2[l], diff_subln_w[l], lam_init)
        o_c = chunk_attention(qc.reshape(B, S, CH_HEADS, CH_DH), kc.reshape(B, S, CH_HEADS, CH_DH),
                              vc.reshape(B, S, CH_HEADS, CH_DH), chunk_rel_bias[l])
        g_d = jax.nn.sigmoid(gd + b_gate[l, :D])
        g_c = jax.nn.sigmoid(gc + b_gate[l, D:])
        merged = g_d * (o_d @ w_branch_diff[l]) + g_c * (o_c @ w_branch_chunk[l])
        h = h + merged @ w_out[l]
        h = h + peer(rmsnorm(h, norm2_w[l]), peer_wq[l], peer_keys[l], peer_u[l], peer_v[l])
    return rmsnorm(h, final_norm_w)


D_MIX = D_MODEL
D_LRU = D_MIX // 2
LRU_BLOCKS = 8
LRU_BLOCK = D_LRU // LRU_BLOCKS
CONV_WIDTH = 4
LRU_C = 8.0
N_HEADS = 8
N_KV_HEADS = 2
GQA_GROUP = N_HEADS // N_KV_HEADS
HEAD_DIM = (D_MIX - D_LRU) // N_HEADS
D_ATTN = N_HEADS * HEAD_DIM
WINDOW = 128
BLOCK_Q = 128
D_FF = 2816
RMS_EPS = 1e-6
D_IN = 2 * D_LRU + (N_HEADS + 2 * N_KV_HEADS) * HEAD_DIM
MASK_VALUE = -1e30


def rms_norm(x, g):
    xf = x.astype(jnp.float32)
    y = xf * lax.rsqrt(jnp.mean(xf * xf, axis=-1, keepdims=True) + RMS_EPS)
    return (y * g.astype(jnp.float32)).astype(x.dtype)

def swiglu(x, w_gu, w_down):
    gate, up = jnp.split(x @ w_gu, 2, axis=-1)
    return (jax.nn.silu(gate) * up) @ w_down

def causal_depthwise_conv(x, w, b):
    c = x.shape[-1]
    rhs = w.astype(x.dtype)[:, None, :]
    y = lax.conv_general_dilated(x, rhs, window_strides=(1,), padding=[(CONV_WIDTH - 1, 0)],
                                 dimension_numbers=("NWC", "WIO", "NWC"), feature_group_count=c)
    return y + b.astype(x.dtype)

def block_diag(x, w, b):
    bsz, s, _ = x.shape
    xh = x.reshape(bsz, s, LRU_BLOCKS, LRU_BLOCK)
    y = jnp.einsum("bshi,hij->bshj", xh, w).reshape(bsz, s, D_LRU)
    return y + b

def rg_lru(x_in, conv_w, conv_b, w_rg, b_rg, w_ig, b_ig, lam):
    xc = causal_depthwise_conv(x_in, conv_w, conv_b)
    r = jax.nn.sigmoid(block_diag(xc, w_rg, b_rg).astype(jnp.float32))
    i = jax.nn.sigmoid(block_diag(xc, w_ig, b_ig).astype(jnp.float32))
    log_a = LRU_C * r * jax.nn.log_sigmoid(lam.astype(jnp.float32))
    a = jnp.exp(log_a)
    mult = jnp.sqrt(-jnp.expm1(2.0 * log_a))
    u = mult * (i * xc.astype(jnp.float32))

    def combine(left, right):
        a_l, u_l = left
        a_r, u_r = right
        return a_l * a_r, a_r * u_l + u_r

    _, h = lax.associative_scan(combine, (a, u), axis=1)
    return h.astype(x_in.dtype)

def sliding_window_sink_attention(q, k, v, sinks):
    bsz, s = q.shape[0], q.shape[1]
    nb = s // BLOCK_Q
    qb = q.reshape(bsz, nb, BLOCK_Q, N_KV_HEADS, GQA_GROUP, HEAD_DIM)
    kb = k.reshape(bsz, nb, BLOCK_Q, N_KV_HEADS, HEAD_DIM)
    vb = v.reshape(bsz, nb, BLOCK_Q, N_KV_HEADS, HEAD_DIM)
    k_band = jnp.concatenate([jnp.concatenate([jnp.zeros_like(kb[:, :1]), kb[:, :-1]], axis=1), kb], axis=2)
    v_band = jnp.concatenate([jnp.concatenate([jnp.zeros_like(vb[:, :1]), vb[:, :-1]], axis=1), vb], axis=2)
    scale = HEAD_DIM ** -0.5
    scores = jnp.einsum("bnqkgd,bnjkd->bnkgqj", qb, k_band).astype(jnp.float32) * scale
    qi = jnp.arange(BLOCK_Q)[:, None]
    kj = jnp.arange(2 * BLOCK_Q)[None, :]
    rel = qi + BLOCK_Q - kj
    band = (rel >= 0) & (rel < WINDOW)
    blk = jnp.arange(nb)[:, None, None]
    mask = band[None] & ((blk > 0) | (kj >= BLOCK_Q)[None])
    scores = jnp.where(mask[None, :, None, None], scores, MASK_VALUE)
    sink = sinks.astype(jnp.float32).reshape(1, 1, N_KV_HEADS, GQA_GROUP, 1, 1)
    m = jnp.maximum(jnp.max(scores, axis=-1, keepdims=True), sink)
    p = jnp.exp(scores - m)
    denom = jnp.sum(p, axis=-1, keepdims=True) + jnp.exp(sink - m)
    p = (p / denom).astype(v.dtype)
    out = jnp.einsum("bnkgqj,bnjkd->bnqkgd", p, v_band)
    return out.reshape(bsz, s, D_ATTN)

def hybrid_mixer(h, w_in, conv_w, conv_b, w_rg, b_rg, w_ig, b_ig, lam, sinks, g_lru_out, g_attn_out, w_o):
    bsz, s, _ = h.shape
    proj = h @ w_in
    o1 = D_LRU
    o2 = o1 + D_LRU
    o3 = o2 + D_ATTN
    o4 = o3 + N_KV_HEADS * HEAD_DIM
    x_lru = proj[..., :o1]
    gate_lru = proj[..., o1:o2]
    q = proj[..., o2:o3].reshape(bsz, s, N_HEADS, HEAD_DIM)
    k = proj[..., o3:o4].reshape(bsz, s, N_KV_HEADS, HEAD_DIM)
    v = proj[..., o4:].reshape(bsz, s, N_KV_HEADS, HEAD_DIM)
    y_lru = rg_lru(x_lru, conv_w, conv_b, w_rg, b_rg, w_ig, b_ig, lam) * jax.nn.gelu(gate_lru)
    y_attn = sliding_window_sink_attention(q, k, v, sinks)
    y = jnp.concatenate([rms_norm(y_lru, g_lru_out), rms_norm(y_attn, g_attn_out)], axis=-1)
    return y @ w_o

def second_inputs(seed: int = 0) -> dict:
    key = jax.random.key(seed)
    ks = jax.random.split(key, 32)
    f32 = jnp.float32

    def nrm(k, shape, scale):
        return jax.random.normal(k, shape, f32) * scale

    def gain(k, n):
        return 1.0 + 0.05 * jax.random.normal(k, (DEPTH, n), f32)

    u = jax.random.uniform(ks[13], (DEPTH, D_LRU), f32, 0.9, 0.999)
    return {
        "x": jax.random.normal(ks[0], (BATCH, SEQ, D_MODEL), f32),
        "ffn1_pre_g": gain(ks[1], D_MODEL),
        "ffn1_w_gu": nrm(ks[2], (DEPTH, D_MODEL, 2 * D_FF), D_MODEL ** -0.5),
        "ffn1_w_down": nrm(ks[3], (DEPTH, D_FF, D_MODEL), D_FF ** -0.5),
        "ffn1_post_g": gain(ks[4], D_MODEL),
        "mix_pre_g": gain(ks[5], D_MODEL),
        "w_in": nrm(ks[6], (DEPTH, D_MODEL, D_IN), D_MODEL ** -0.5),
        "conv_w": nrm(ks[7], (DEPTH, CONV_WIDTH, D_LRU), CONV_WIDTH ** -0.5),
        "conv_b": nrm(ks[8], (DEPTH, D_LRU), 0.01),
        "w_rg": nrm(ks[9], (DEPTH, LRU_BLOCKS, LRU_BLOCK, LRU_BLOCK), LRU_BLOCK ** -0.5),
        "b_rg": nrm(ks[10], (DEPTH, D_LRU), 0.01),
        "w_ig": nrm(ks[11], (DEPTH, LRU_BLOCKS, LRU_BLOCK, LRU_BLOCK), LRU_BLOCK ** -0.5),
        "b_ig": nrm(ks[12], (DEPTH, D_LRU), 0.01),
        "lru_lambda": jnp.log(u) - jnp.log1p(-u),
        "sinks": nrm(ks[14], (DEPTH, N_HEADS), 1.0),
        "g_lru_out": gain(ks[15], D_LRU),
        "g_attn_out": gain(ks[16], D_ATTN),
        "w_o": nrm(ks[17], (DEPTH, D_MIX, D_MODEL), D_MIX ** -0.5),
        "mix_post_g": gain(ks[18], D_MODEL),
        "ffn2_pre_g": gain(ks[19], D_MODEL),
        "ffn2_w_gu": nrm(ks[20], (DEPTH, D_MODEL, 2 * D_FF), D_MODEL ** -0.5),
        "ffn2_w_down": nrm(ks[21], (DEPTH, D_FF, D_MODEL), D_FF ** -0.5),
        "ffn2_post_g": gain(ks[22], D_MODEL),
    }

def second_block(x, ffn1_pre_g, ffn1_w_gu, ffn1_w_down, ffn1_post_g, mix_pre_g, w_in, conv_w, conv_b,
              w_rg, b_rg, w_ig, b_ig, lru_lambda, sinks, g_lru_out, g_attn_out, w_o, mix_post_g,
              ffn2_pre_g, ffn2_w_gu, ffn2_w_down, ffn2_post_g):
    for l in range(DEPTH):
        x = x + 0.5 * rms_norm(swiglu(rms_norm(x, ffn1_pre_g[l]), ffn1_w_gu[l], ffn1_w_down[l]), ffn1_post_g[l])
        y = hybrid_mixer(rms_norm(x, mix_pre_g[l]), w_in[l], conv_w[l], conv_b[l], w_rg[l], b_rg[l],
                         w_ig[l], b_ig[l], lru_lambda[l], sinks[l], g_lru_out[l], g_attn_out[l], w_o[l])
        x = x + rms_norm(y, mix_post_g[l])
        x = x + 0.5 * rms_norm(swiglu(rms_norm(x, ffn2_pre_g[l]), ffn2_w_gu[l], ffn2_w_down[l]), ffn2_post_g[l])
    return x


def setup_inputs(seed=0):
    out = dict(first_inputs(seed))
    for name, value in second_inputs(seed + 1).items():
        if name != "x":
            out[name + "_2"] = value
    return out


def reference(
    x, norm1_w, w_in, b_gate, diff_lq1, diff_lk1, diff_lq2, diff_lk2, diff_subln_w,
    chunk_rel_bias, w_branch_diff, w_branch_chunk, w_out, norm2_w, peer_wq, peer_keys, peer_u,
    peer_v, final_norm_w, ffn1_pre_g_2, ffn1_w_gu_2, ffn1_w_down_2, ffn1_post_g_2, mix_pre_g_2,
    w_in_2, conv_w_2, conv_b_2, w_rg_2, b_rg_2, w_ig_2, b_ig_2, lru_lambda_2, sinks_2,
    g_lru_out_2, g_attn_out_2, w_o_2, mix_post_g_2, ffn2_pre_g_2, ffn2_w_gu_2, ffn2_w_down_2,
    ffn2_post_g_2,
):
    x = first_block(
        x, norm1_w, w_in, b_gate, diff_lq1, diff_lk1, diff_lq2, diff_lk2, diff_subln_w,
        chunk_rel_bias, w_branch_diff, w_branch_chunk, w_out, norm2_w, peer_wq, peer_keys,
        peer_u, peer_v, final_norm_w,
    )
    return second_block(
        x, ffn1_pre_g_2, ffn1_w_gu_2, ffn1_w_down_2, ffn1_post_g_2, mix_pre_g_2, w_in_2,
        conv_w_2, conv_b_2, w_rg_2, b_rg_2, w_ig_2, b_ig_2, lru_lambda_2, sinks_2, g_lru_out_2,
        g_attn_out_2, w_o_2, mix_post_g_2, ffn2_pre_g_2, ffn2_w_gu_2, ffn2_w_down_2,
        ffn2_post_g_2,
    )


_drawn_inputs = setup_inputs


def setup_inputs(seed=0):
    import zlib

    import numpy as np

    out = dict(_drawn_inputs(seed))
    spreads = {}
    factors = {'b_gate': 8.0,
     'diff_lk1': 2.829,
     'diff_lq2': 2.92,
     'diff_subln_w': 4.194,
     'chunk_rel_bias': 5.658,
     'norm2_w': 8.0,
     'peer_wq': 2.976,
     'peer_keys': 2.977,
     'peer_u': 3.327,
     'peer_v': 2.956,
     'conv_b_2': 3.366,
     'b_rg_2': 42.749,
     'b_ig_2': 22.072,
     'sinks_2': 2.871,
     'ffn2_post_g_2': 3.737}
    for name, (base, spread) in spreads.items():
        noise = np.random.default_rng([zlib.crc32(name.encode()), seed]).standard_normal(out[name].shape)
        drawn = base * np.exp(spread * noise) if base else spread * noise
        out[name] = __import__('jax').numpy.asarray(drawn.astype(out[name].dtype))
    for name, factor in factors.items():
        out[name] = (out[name] * factor).astype(out[name].dtype)
    return out
```

```python
import numpy as np

import concourse.bass as bass
import concourse.mybir as mybir
from contextlib import ExitStack

F32 = mybir.dt.float32
F32R = mybir.dt.float32r
I32 = mybir.dt.int32
U32 = mybir.dt.uint32
ALU = mybir.AluOpType
ACT = mybir.ActivationFunctionType
AX = mybir.AxisListType

P = 128
T = 256
TT = T // P
D = 1024
KD = D // P
EPS = 1e-6
HEADS = 8
SUB = 64
PEER_H, NKEY, TOPK = 8, 128, 16
D_FF = 2816
FT = D_FF // P
LT = 4
CONV = 4
MASKED = -1e30
LAM_INIT = 0.8 - 0.6

CW = 2048
RAW = 2
RING = 4
AHEAD = RING - 1
_sizes = [("qk", 12), ("vd", 4), ("vc", 2), ("gate", 8), ("bd", 4), ("bc", 2), ("out", 4),
          ("wq", 4), ("peer", 128), ("gu1", 22), ("dn1", 11), ("in2", 7), ("wo", 4),
          ("gu2", 22), ("dn2", 11)]
CH = {}
NCH = 0
for _name, _n in _sizes:
    CH[_name] = NCH
    NCH += _n

_usizes = [("qk", 12), ("gate", 8), ("bd", 4), ("bc", 4), ("wq", 4), ("gu1", 22),
           ("in2", 7), ("gu2", 22)]
UN = {}
_n0 = 0
for _name, _n in _usizes:
    UN[_name] = _n0
    _n0 += _n

QG = 4
QW = NKEY // QG
GT = 8
GROUPS = T // GT

NORMS = ["norm1_w", "norm2_w", "final_norm_w", "ffn1_pre_g_2", "ffn1_post_g_2", "mix_pre_g_2",
         "g_attn", "mix_post_g_2", "ffn2_pre_g_2", "ffn2_post_g_2"]


def build_program(nc, A, out):
    ctx = ExitStack()
    with ctx:
        def sem(name):
            return ctx.enter_context(nc.semaphore(name))

        def sb(name, shape, dt=F32, at=ctx):
            return at.enter_context(nc.sbuf_tensor(name, shape, dt))

        raw = sb("raw", [P, RAW, CW])
        wh = sb("wh", [P, RING, CW], F32R)
        wl = sb("wl", [P, RING, CW], F32R)
        resid = sb("resid", [P, TT, D])
        xh = sb("xh", [P, KD, T], F32R)
        xl = sb("xl", [P, KD, T], F32R)
        wb = sb("wb", [P, 2, D])
        ident = sb("ident", [P, P])
        iota = sb("iota", [P, NKEY])
        i1T = sb("i1T", [P, T])
        i2T = sb("i2T", [P, T])
        gTh = sb("gTh", [P, T])
        gTl = sb("gTl", [P, T])
        ssq = sb("ssq", [P, TT])
        var = sb("var", [P, TT])
        nw_i = sb("nw_i", [P, TT], I32)
        nw_a = sb("nw_a", [P, TT])
        nw_b = sb("nw_b", [P, TT])
        rstd = sb("rstd", [P, TT])

        st = ExitStack()
        y = sb("y", [P, TT, D], at=st)
        junk = sb("junk", [P, D], at=st)
        st1 = ExitStack()
        gate = sb("gate", [P, 16, T], at=st1)
        oc = sb("oc", [P, TT, 4, P], at=st1)
        nd = sb("nd", [P, T], at=st1)
        ndi = i2T
        lq = gTh[:, :].rearrange("p (a b) -> p a b", a=4)
        lqj = sb("lqj", [P, SUB], at=st1)
        lams = sb("lams", [P, 8], at=st1)
        subw = sb("subw", [P, P], at=st1)
        bgate = sb("bgate", [P, 16], at=st1)
        sso = sb("sso", [P, 16], at=st1)
        so = [sb(f"so{k}", [P, 16], I32 if k == 0 else F32, at=st1) for k in range(5)]
        s_sb = sb("s_sb", [P, 2, 2, T], at=st1)
        p_sb = sb("p_sb", [P, 2, 2, T], at=st1)
        pT = sb("pT", [P, 2, 4, P], at=st1)
        smx = sb("smx", [P, 2, 2], at=st1)
        rs = sb("rs", [P, 2, 2], at=st1)
        rr = sb("rr", [P, 2, 2], at=st1)
        rc = sb("rc", [P, 2], at=st1)
        st2 = ExitStack()
        qkT = sb("qkT", [P, 24, T], at=st2)
        vd = sb("vd", [P, TT, D], at=st2)
        vc = sb("vc", [P, TT, 512], at=st2)
        rb = sb("rb", [P, HEADS, T], at=st2)
        st2.close()
        st2 = ExitStack()
        odh = sb("odh", [P, KD, T], F32R, at=st2)
        odl = sb("odl", [P, KD, T], F32R, at=st2)
        och = sb("och", [P, 4, T], F32R, at=st2)
        ocl = sb("ocl", [P, 4, T], F32R, at=st2)
        st2.close()
        st1.close()

        st1 = ExitStack()
        pqT = sb("pqT", [P, PEER_H, T], at=st1)
        keysT = sb("keysT", [P, PEER_H, NKEY], at=st1)
        sc12 = sb("sc12", [P, TT, PEER_H, 2, NKEY], at=st1)
        sc_w = sb("sc_w", [P, PEER_H, 2, NKEY], at=st1)
        v16 = sb("v16", [P, PEER_H, 2, TOPK], at=st1)
        i16 = sb("i16", [P, PEER_H, 2, TOPK], U32, at=st1)
        i16f = sb("i16f", [P, PEER_H, 2, TOPK], at=st1)
        cand = sb("cand", [P, PEER_H, TOPK * TOPK], at=st1)
        cand_w = sb("cand_w", [P, PEER_H, TOPK * TOPK], at=st1)
        cv = sb("cv", [P, PEER_H, TOPK], at=st1)
        ci = sb("ci", [P, PEER_H, TOPK], U32, at=st1)
        cab = sb("cab", [P, 2, PEER_H, TOPK], U32, at=st1)
        cabf = sb("cabf", [P, 2, PEER_H, TOPK], at=st1)
        esel = sb("esel", [P, 2, PEER_H * TOPK], at=st1)
        gate_t = sb("gate_t", [P, PEER_H, TOPK], at=st1)
        gsum = sb("gsum", [P, PEER_H], at=st1)
        grec = sb("grec", [P, PEER_H], at=st1)
        st1.close()
        st.close()

        st = ExitStack()
        G = sb("G", [P, 2, QW, T], at=st)
        hid = sb("hid", [P, 2, 2, T], at=st)
        ah = sb("ah", [P, 2, 2, T], F32R, at=st)
        al = sb("al", [P, 2, 2, T], F32R, at=st)
        one1 = sb("one1", [P, 2, GT, NKEY], F32R, at=st)
        one2 = sb("one2", [P, GT, QW], at=st)
        g2h = sb("g2h", [P, 2, GT, QW], F32R, at=st)
        g2l = sb("g2l", [P, 2, GT, QW], F32R, at=st)
        i1c = sb("i1c", [P, 4 * GT], at=st)
        st.close()

        st = ExitStack()
        y_again = sb("y_again", [P, TT, D], at=st)
        junk_again = sb("junk_again", [P, D], at=st)
        st1 = ExitStack()
        fh = sb("fh", [P, FT, T], F32R, at=st1)
        fl = sb("fl", [P, FT, T], F32R, at=st1)
        fs = sb("fs", [P, 2, T], at=st1)
        ff = sb("ff", [P, 2, T], at=st1)
        st1.close()
        st1 = ExitStack()
        xin = sb("xin", [P, LT, CONV - 1 + T], at=st1)
        gl = sb("gl", [P, LT, T], at=st1)
        q2T = sb("q2T", [P, 5, T], at=st1)
        v2 = sb("v2", [P, TT, P], at=st1)
        xc = sb("xc", [P, LT, T], at=st1)
        gr = sb("gr", [P, LT, T], at=st1)
        gi = sb("gi", [P, LT, T], at=st1)
        la = sb("la", [P, LT, T], at=st1)
        th = sb("th", [P, LT, T], at=st1)
        hs = sb("hs", [P, LT, T], at=st1)
        bd = sb("bd", [P, 2, LT, P], at=st1)
        cols = sb("cols", [P, 9, LT], at=st1)
        lsg = sb("lsg", [P, 6, LT], at=st1)
        ones = sb("ones", [P, P], at=st1)
        m2 = sb("m2", [P, T], at=st1)
        sinkb = sb("sinkb", [P, 4, 2], at=st1)
        o2 = sb("o2", [P, TT, 4, P], at=st1)
        wv = sb("wv", [P, T], at=st1)
        wi_ = sb("wi_", [P, T], I32, at=st1)
        wa_ = sb("wa_", [P, T], at=st1)
        wb_ = sb("wb_", [P, T], at=st1)
        wr_ = sb("wr_", [P, T], at=st1)
        s2_sb = sb("s2_sb", [P, 2, 2, T], at=st1)
        p2_sb = sb("p2_sb", [P, 2, 2, T], at=st1)
        p2T = sb("p2T", [P, 2, 4, P], at=st1)
        smx2 = sb("smx2", [P, 2, 2], at=st1)
        mx2 = sb("mx2", [P, 2, 2], at=st1)
        sd2 = sb("sd2", [P, 2, 2], at=st1)
        es2 = sb("es2", [P, 2, 2], at=st1)
        rs2 = sb("rs2", [P, 2, 2], at=st1)
        rr2 = sb("rr2", [P, 2, 2], at=st1)
        st1.close()
        st.close()

        acc = ctx.enter_context(nc.psum_tensor("acc", [P, 4, 512], F32))
        ub = ctx.enter_context(nc.psum_tensor("ub", [P, 2, 512], F32))
        mb = ctx.enter_context(nc.psum_tensor("mb", [P, 2, 512], F32))

        raw_in = [sem(f"raw_in{k}") for k in range(RAW)]
        w_high = sem("w_high")
        w_low = sem("w_low")
        c_done = sem("c_done")
        u_free = sem("u_free")
        c_read = sem("c_read")
        t_in = sem("t_in")
        t_ps = sem("t_ps")
        t_high = sem("t_high")
        t_low = sem("t_low")
        wb_in = [sem(f"wb_in{k}") for k in range(2)]
        wb_used = sem("wb_used")
        x_in = sem("x_in")
        x_out = sem("x_out")
        consts = sem("consts")
        par1 = sem("par1")
        rb_in = sem("rb_in")
        rb_ok = sem("rb_ok")
        keys_in = sem("keys_in")
        keys_go = sem("keys_go")
        par2 = sem("par2")
        par2_go = sem("par2_go")
        dve = sem("dve")
        at_sc = sem("at_sc")
        at_b = sem("at_b")
        at_sm = sem("at_sm")
        at_ex = sem("at_ex")
        at_a = sem("at_a")
        at_t = sem("at_t")
        at_v = sem("at_v")
        at_o = sem("at_o")
        at_d = sem("at_d")
        lam_s = sem("lam_s")
        lam_e = sem("lam_e")
        bt_done = sem("bt_done")
        sk_ps = sem("sk_ps")
        sk_sb = sem("sk_sb")
        tk_x = sem("tk_x")
        tk_e = sem("tk_e")
        ix_in = sem("ix_in")
        ix_ps = sem("ix_ps")
        ix_sb = sem("ix_sb")
        ix_l = sem("ix_l")
        g_one1 = sem("g_one1")
        rows_go = sem("rows_go")
        g_eq = sem("g_eq")
        g_two = sem("g_two")
        g_ps = sem("g_ps")
        g_sb = sem("g_sb")
        pool_c = sem("pool_c")
        hd_g = sem("hd_g")
        hd_m = sem("hd_m")
        a_h = sem("a_h")
        a_l = sem("a_l")
        f_s = sem("f_s")
        f_f = sem("f_f")
        f_h = sem("f_h")
        f_l = sem("f_l")
        v2_sb = sem("v2_sb")
        x2_sb = sem("x2_sb")
        ls_z = sem("ls_z")
        ls_e = sem("ls_e")
        xc_ok = sem("xc_ok")
        rg_ps = sem("rg_ps")
        rg_sb = sem("rg_sb")
        la_ok = sem("la_ok")
        la_e = sem("la_e")
        m2_ok = sem("m2_ok")
        mu_ok = sem("mu_ok")
        yq_ok = sem("yq_ok")
        ss_ps = sem("ss_ps")
        yl_ok = sem("yl_ok")
        done = sem("done")

        block = ctx.enter_context(nc.Block())

        @block.sync
        def _(sp):
            stream = A["wstream"]
            for c in range(RAW):
                sp.dma_start(raw[:, c, :], stream[c]).then_inc(raw_in[c % RAW], 16)

            def load(c, slot):
                sp.wait_ge(w_low, c - RAW + 1)
                sp.dma_start(raw[:, slot, :],
                             stream[bass.ds(c, 1)].rearrange("a p n -> p (a n)")).then_inc(raw_in[slot], 16)

            pairs = (NCH - RAW) // 2
            with sp.Fori(0, pairs) as i:
                for j in range(2):
                    load(i * 2 + (RAW + j), j)
            for c in range(RAW + 2 * pairs, NCH):
                load(c, c % RAW)
            sp.wait_ge(done, 1)
            sp.dma_start(out.rearrange("(a p) d -> p a d", p=P), resid[:, :, :]).then_inc(x_out, 16)
            sp.wait_ge(x_out, 16)

        @block.gpsimd
        def _(pool):
            pool.dma_start(resid[:, :, :], A["x"].rearrange("(a p) d -> p a d", p=P)).then_inc(x_in, 16)

            def load_wb(n):
                if n >= 2:
                    pool.wait_ge(wb_used, n - 1)
                a = A[NORMS[n]]
                w = a.shape[1]
                pool.dma_start(wb[:, n % 2, 0:w], a.to_broadcast([P, w])).then_inc(wb_in[n % 2], 16)

            load_wb(0)
            load_wb(1)
            pool.memset(ident[:, :], 0.0).then_inc(pool_c, 1)
            pool.iota(iota[:, :], [[1, NKEY]], base=0, channel_multiplier=0,
                      allow_small_or_imprecise_dtypes=True).then_inc(consts, 1)
            pool.iota(ndi[:, :], [[1, T]], base=-P, channel_multiplier=-1,
                      allow_small_or_imprecise_dtypes=True).then_inc(consts, 1)
            pool.wait_ge(pool_c, 1)
            pool.affine_select(out=ident[:, :], in_=ident[:, :], compare_op=ALU.not_equal, fill=1.0,
                               base=0, pattern=[[-1, P]], channel_multiplier=1).then_inc(consts, 1)
            pool.dma_start(lq[:, :, :], A["lq"].to_broadcast([P, 4 * SUB])
                           .rearrange("p (a b) -> p a b", a=4)).then_inc(par1, 16)
            pool.dma_start(subw[:, :], A["subln"].to_broadcast([P, P])).then_inc(par1, 16)
            pool.dma_start(bgate[:, :], A["b_gate"]).then_inc(par1, 16)
            pool.dma_start(rb[:, :, :], A["rel"]).then_inc(rb_in, 16)
            pool.wait_ge(rb_in, 16)
            pool.memset(rb[0:SUB, :, T - SUB:T], MASKED).then_inc(rb_ok, 1)
            load_wb(2)
            pool.wait_ge(keys_go, 1)
            pool.dma_start(keysT[:, :, :], A["keys"]).then_inc(keys_in, 16)

            def rows(n, j):
                pool.wait_ge(g_ps, n - 1)
                pool.sem_inc(rows_go, 1)
                for k in range(GT):
                    last = pool.tensor_scalar(one1[:, j % 2, k, :], iota[:, :],
                                              i1c[:, j * GT + k:j * GT + k + 1], None, ALU.is_equal)
                last.then_inc(g_one1, 1)

            ncopy = 0

            def rows4(q, i):
                base = (q - 1) * 8 + i
                pool.wait_ge(g_one1, GROUPS + base * 4)
                pool.tensor_copy(i1c[:, :], i1T[:, bass.ds(i * (4 * GT), 4 * GT)]).then_inc(pool_c, 1)
                pool.wait_ge(pool_c, base + 2)
                for j in range(4):
                    rows(q * GROUPS + i * 4 + j, j)

            pool.wait_ge(ix_l, 2)
            for q in range(1, QG):
                with pool.Fori(0, 8) as i:
                    rows4(q, i)

            for n in range(3, 6):
                load_wb(n)
            pool.wait_ge(par2_go, 1)
            pool.memset(xin[:, :, 0:CONV - 1], 0.0).then_inc(x2_sb, 1)
            pool.memset(ones[:, :], 1.0).then_inc(x2_sb, 1)
            pool.memset(bd[:, :, :, :], 0.0).then_inc(pool_c, 1)
            pool.memset(m2[:, :], 0.0).then_inc(pool_c, 1)
            pool.dma_start(cols[:, :, :], A["cols"]).then_inc(par2, 16)
            pool.dma_start(sinkb[:, :, :], A["sinks"].to_broadcast([P, 8])
                           .rearrange("p (a b) -> p a b", a=4)).then_inc(par2, 16)
            pool.wait_ge(pool_c, 1 + 8 * (QG - 1) + 2)
            for g, name in enumerate(("w_rg", "w_ig")):
                for r in range(2):
                    pool.dma_start(bd[SUB * r:SUB * r + SUB, g, :, SUB * r:SUB * r + SUB],
                                   A[name][r]).then_inc(par2, 16)
            pool.affine_select(out=m2[:, :], in_=m2[:, :], compare_op=ALU.is_ge, fill=MASKED,
                               base=P, pattern=[[-1, T]], channel_multiplier=1).then_inc(pool_c, 1)
            pool.wait_ge(pool_c, 1 + 8 * (QG - 1) + 3)
            pool.affine_select(out=m2[:, :], in_=m2[:, :], compare_op=ALU.is_gt, fill=MASKED,
                               base=0, pattern=[[1, T]], channel_multiplier=-1).then_inc(x2_sb, 1)
            for n in range(6, len(NORMS)):
                load_wb(n)

        @block.scalar
        def _(act):
            def split(c, slot):
                act.wait_ge(raw_in[slot % RAW], arrived(c, slot))
                if not isinstance(c, int) or c >= RING:
                    act.wait_ge(c_done, c - RING + 1)
                act.copy(wh[:, slot, :], raw[:, slot % RAW, :]).then_inc(w_high, 1)

            def arrived(c, slot):
                return ((c - slot % RAW) // RAW) * 16 + 16 if isinstance(c, int) else \
                    (c - slot % RAW) * (16 // RAW) + 16

            def ahead(c):
                if isinstance(c, int) and c + AHEAD < NCH:
                    split(c + AHEAD, (c + AHEAD) % RING)

            def ahead_at(c, cmod):
                split(c + AHEAD, (cmod + AHEAD) % RING)

            nt = [0]

            def transposed(dh, dl, tiles, to=0):
                for g in range(tiles // 2):
                    act.wait_ge(t_ps, nt[0] + 1)
                    act.copy(dh[:, to + 2 * g:to + 2 * g + 2, :],
                             acc[:, g, :].rearrange("p (a b) -> p a b", a=2)).then_inc(t_high, 1)
                    nt[0] += 1

            def read_acc(dst, stage, banks=4):
                act.wait_ge(c_done, CH[stage] + dict(_sizes)[stage])
                for b in range(banks):
                    tt, nb = (b // 2, b % 2) if banks == 4 else (b, 0)
                    last = act.copy(dst[:, tt, nb * 512:nb * 512 + 512], acc[:, b, :])
                last.then_inc(c_read, 1)

            for c in range(AHEAD):
                split(c, c)
            transposed(xh, xl, KD)
            for j in range(4):
                ahead(j)
                act.wait_ge(c_done, j + 1)
                act.copy(qkT[:, 2 * j:2 * j + 2, :],
                         ub[:, j % 2, :].rearrange("p (a b) -> p a b", a=2)).then_inc(u_free, 1)
            with act.Fori(1, 3) as i:
                for j in range(4):
                    ahead_at(i * 4 + j, j)
                    act.wait_ge(c_done, i * 4 + (j + 1))
                    act.copy(qkT[:, bass.ds(i * 8 + 2 * j, 2), :],
                             ub[:, j % 2, :].rearrange("p (a b) -> p a b", a=2)).then_inc(u_free, 1)
            for c in range(CH["vd"], CH["vd"] + 4):
                ahead(c)
            read_acc(vd, "vd")
            for c in range(CH["vc"], CH["vc"] + 2):
                ahead(c)
            read_acc(vc, "vc", banks=2)
            act.wait_ge(par1, 48)
            with act.Fori(0, 2) as i:
                for j in range(4):
                    ahead_at(i * 4 + (CH["gate"] + j), CH["gate"] + j)
                    act.wait_ge(c_done, i * 4 + (CH["gate"] + j + 1))
                    for k in range(2):
                        last = act.activation(gate[:, bass.ds(i * 8 + (2 * j + k), 1), :],
                                              ub[:, j % 2, k * T:k * T + T].rearrange("p (a b) -> p a b", a=1),
                                              ACT.Sigmoid, bias=bgate[:, bass.ds(i * 8 + (2 * j + k), 1)])
                    last.then_inc(u_free, 1)
            act.wait_ge(lam_s, 2)
            act.activation(lams[:, 2:4], lams[:, 0:2], ACT.Exp).then_inc(lam_e, 1)

            def attention(count, n0, sb_, pb_, pt_, mx_, r_, scale_of, blocks_of, nk_of, sink=None):
                def exps(n):
                    b = n % 2
                    nk = nk_of(n)
                    act.wait_ge(at_sm, n0 + n + 1)
                    for r in range(2):
                        act.activation(pb_[:, b, r, 0:nk], sb_[:, b, r, 0:nk], ACT.Exp,
                                       bias=mx_[:, b, r:r + 1], scale=scale_of(n),
                                       accum_out=r_[:, b, r:r + 1]).then_inc(at_ex, 1)
                    if sink is not None:
                        act.activation(es2[:, b, :], sd2[:, b, :], ACT.Exp).then_inc(la_e, 1)

                def turn(n):
                    b = n % 2
                    act.wait_ge(at_t, n0 + n + 1)
                    if n >= 2:
                        act.wait_ge(at_o, n0 + n - 1)
                    w = blocks_of(n)
                    act.copy(pt_[:, b, 0:w, :], ub[:, b, 0:w * P].rearrange("p (a b) -> p a b", a=w)
                             ).then_inc(at_v, 1)

                for n in range(count):
                    exps(n)
                    if n >= 1:
                        turn(n - 1)
                turn(count - 1)

            attention(24, 0, s_sb, p_sb, pT, smx, rs, lambda n: 0.125 if n < 16 else 1.0,
                      lambda n: (1 if n < 16 else 2) * (1 + n % 2), lambda n: P * (1 + n % 2))
            transposed(odh, odl, KD)
            transposed(och, ocl, 4)
            for c in range(CH["bd"], CH["bd"] + 6 + 4):
                ahead(c)
            read_acc(y, "out")
            transposed(xh, xl, KD)
            for u in range(4):
                ahead(CH["wq"] + u)
                act.wait_ge(c_done, CH["wq"] + u + 1)
                act.copy(pqT[:, 2 * u:2 * u + 2, :],
                         ub[:, (UN["wq"] + u) % 2, :].rearrange("p (a b) -> p a b", a=2)).then_inc(u_free, 1)
            for n in range(4):
                tt, k = n // 2, n % 2
                act.wait_ge(sk_ps, n + 1)
                for s in range(2):
                    last = act.copy(sc12[:, tt, 4 * k:4 * k + 4, s, :],
                                    acc[:, 2 * k + s, :].rearrange("p (a b) -> p a b", a=4))
                last.then_inc(sk_sb, 1)
            for tt in range(TT):
                act.wait_ge(tk_x, tt + 1)
                act.activation(gate_t[:, :, :], gate_t[:, :, :], ACT.Exp).then_inc(tk_e, 1)
                act.wait_ge(ix_ps, tt + 1)
                for k, dst in enumerate((i1T, i2T)):
                    act.copy(dst[:, tt * P:tt * P + P], mb[:, tt, k * P:k * P + P])
                act.copy(gTh[:, tt * P:tt * P + P].bitcast(F32R), mb[:, tt, 2 * P:3 * P]).then_inc(ix_sb, 1)

            def spread(n, b, tok, qb):
                act.wait_ge(g_ps, n + 1)
                act.copy(G[:, qb, :, tok], mb[:, b, 0:GT * QW].rearrange("p (t i) -> p i t", i=QW)
                         ).then_inc(g_sb, 1)

            with act.Fori(0, GROUPS // 2) as i:
                for j in range(2):
                    spread(i * 2 + j, j, bass.ds(i * (2 * GT) + j * GT, GT), 0)

            C5 = CH["peer"]

            def iteration(q, i, first=False):
                m = i + 8 * q
                c = m * 4 + (C5 - 1)

                def gelu(k):
                    act.wait_ge(c_done, C5 + 1 if first and k == 0 else m * 4 + (C5 + 2 * k))
                    if not first:
                        act.wait_ge(a_l, m * 2 + (k - 1))
                    act.activation(hid[:, k, :, :].rearrange("p a b -> p (a b)"), ub[:, k, :], ACT.Gelu
                                   ).then_inc(hd_g, 1)

                def high(k):
                    act.wait_ge(hd_m, m * 2 + (k + 1))
                    act.copy(ah[:, k, :, :], hid[:, k, :, :]).then_inc(a_h, 1)

                def groups(a):
                    if q + 1 < QG:
                        for j in (a, a + 1):
                            spread(i * 4 + ((q + 1) * GROUPS + j), j % 2,
                                   bass.ds(i * (4 * GT) + j * GT, GT), (q + 1) % 2)

                if first:
                    ahead(C5)
                    gelu(0)
                    high(0)
                    groups(0)
                    ahead(C5 + 1)
                    gelu(1)
                    ahead(C5 + 2)
                    high(1)
                    groups(2)
                    return
                ahead_at(c, C5 - 1)
                gelu(0)
                ahead_at(c + 1, C5)
                high(0)
                groups(0)
                ahead_at(c + 2, C5 + 1)
                gelu(1)
                ahead_at(c + 3, C5 + 2)
                high(1)
                groups(2)

            for q in range(QG):
                if q == 0:
                    iteration(0, 0, first=True)
                with act.Fori(1 if q == 0 else 0, 8) as i:
                    iteration(q, i)
            ahead(C5 + 127)
            read_acc(y_again, "peer")

            def ffn(gu, dn, nf):
                transposed(xh, xl, KD)
                C, U = CH[gu], UN[gu]

                def hidden(c, cmod, u, umod, n, b):
                    ahead_at(c, cmod)
                    act.wait_ge(c_done, c + 1)
                    if not isinstance(n, int) or n >= 2:
                        act.wait_ge(f_f, n - 1)
                    act.activation(fs[:, b, :], ub[:, umod % 2, 0:T], ACT.Silu).then_inc(f_s, 1)

                for j in range(2):
                    hidden(C + j, C + j, U + j, U + j, nf + j, j % 2)
                with act.Fori(0, 5) as i:
                    for j in range(2, 6):
                        hidden(i * 4 + (C + j), C + j, i * 4 + (U + j), U + j, i * 4 + (nf + j), j % 2)
                for c in range(CH[dn], CH[dn] + 11):
                    ahead(c)
                read_acc(y_again, dn)

            ffn("gu1", "dn1", 0)
            transposed(xh, xl, KD)
            act.wait_ge(x2_sb, 3)
            for u in range(7):
                ahead(CH["in2"] + u)
                act.wait_ge(c_done, CH["in2"] + u + 1)
                b = (UN["in2"] + u) % 2
                src = ub[:, b, :].rearrange("p (a b) -> p a b", a=2)
                if u < 2:
                    act.copy(xin[:, 2 * u:2 * u + 2, CONV - 1:], src).then_inc(u_free, 1)
                elif u < 4:
                    act.activation(gl[:, 2 * u - 4:2 * u - 2, :], src, ACT.Gelu_apprx_tanh).then_inc(u_free, 1)
                elif u < 6:
                    act.copy(q2T[:, 2 * u - 8:2 * u - 6, :], src).then_inc(u_free, 1)
                else:
                    act.copy(q2T[:, 4, :], src[:, 0, :]).then_inc(u_free, 1)
            act.copy(v2[:, :, :], mb[:, :, 0:P]).then_inc(v2_sb, 1)
            act.wait_ge(ls_z, 1)
            act.activation(lsg[:, 1, :], lsg[:, 0, :], ACT.Exp).then_inc(ls_e, 1)
            act.wait_ge(ls_z, 2)
            act.activation(lsg[:, 3, :], lsg[:, 2, :], ACT.Ln).then_inc(ls_e, 1)
            for t in range(LT):
                act.wait_ge(rg_ps, t + 1)
                act.activation(gr[:, t, :], acc[:, t, 0:T], ACT.Sigmoid, bias=cols[:, 5, t:t + 1])
                act.activation(gi[:, t, :], acc[:, t, T:2 * T], ACT.Sigmoid, bias=cols[:, 6, t:t + 1]
                               ).then_inc(rg_sb, 1)
            act.wait_ge(la_ok, 1)
            act.activation(th[:, :, :], la[:, :, :], ACT.Tanh).then_inc(la_e, 1)
            act.activation(la[:, :, :], la[:, :, :], ACT.Exp).then_inc(la_e, 1)
            attention(8, 24, s2_sb, p2_sb, p2T, smx2, rs2, lambda n: 1.0, lambda n: 2 * (1 + n % 2),
                      lambda n: P * (1 + n % 2), sink=True)
            act.wait_ge(m2_ok, 1)
            act.activation(th[:, :, :], th[:, :, :], ACT.Sqrt, scale=-1.0).then_inc(mu_ok, 1)
            transposed(xh, xl, 4, to=4)
            for c in range(CH["wo"], CH["wo"] + 4):
                ahead(c)
            read_acc(y_again, "wo")
            ffn("gu2", "dn2", 22)

        @block.vector
        def _(v):
            steps = [0]

            def link(ins):
                steps[0] += 1
                ins.then_inc(dve, 1)
                v.wait_ge(dve, steps[0])

            def low(c, slot):
                v.wait_ge(w_high, c + 1)
                v.tensor_tensor(wl[:, slot, :], raw[:, slot % RAW, :], wh[:, slot, :].bitcast(F32),
                                ALU.subtract).then_inc(w_low, 1)

            def ahead(c):
                if c + AHEAD < NCH:
                    low(c + AHEAD, (c + AHEAD) % RING)

            def ahead_at(c, cmod):
                low(c + AHEAD, (cmod + AHEAD) % RING)

            def rsqrt(dst, src, ti, ta, tb):
                link(v.tensor_scalar(ti, src.bitcast(I32), 1, None, ALU.logical_shift_right))
                link(v.tensor_scalar(dst.bitcast(I32), ti, -1.0, float(0x5F3759DF), ALU.mult, ALU.add))
                for _ in range(4):
                    link(v.tensor_tensor(ta, dst, dst, ALU.mult))
                    link(v.scalar_tensor_tensor(tb, ta, -0.5, src, ALU.mult, ALU.mult))
                    link(v.scalar_tensor_tensor(dst, tb, 1.5, dst, ALU.add, ALU.mult))

            nwb = [0]

            def rms(src, dst, scratch, factor=1.0, width=D):
                for tt in range(TT):
                    ins = v.tensor_tensor_reduce(scratch, src[:, tt, :], src[:, tt, :], 1.0, 0.0,
                                                 ALU.mult, ALU.add, ssq[:, tt:tt + 1])
                    link(ins)
                link(v.tensor_scalar(var[:, :], ssq[:, :], 1.0 / width, EPS, ALU.mult, ALU.add))
                rsqrt(rstd[:, :], var[:, :], nw_i[:, :], nw_a[:, :], nw_b[:, :])
                if factor != 1.0:
                    link(v.tensor_scalar(rstd[:, :], rstd[:, :], factor, None, ALU.mult))
                n = nwb[0]
                nwb[0] += 1
                v.wait_ge(wb_in[n % 2], 16 * (n // 2 + 1))
                for tt in range(TT):
                    last = v.scalar_tensor_tensor(dst[:, tt, :], src[:, tt, :], rstd[:, tt:tt + 1],
                                                  wb[:, n % 2, 0:width], ALU.mult, ALU.mult)
                    if tt == 0:
                        link(last)
                last.then_inc(wb_used, 1)
                v.wait_ge(wb_used, n + 1)

            nt = [0]

            def go_transpose():
                v.engine_nop().then_inc(t_in, 1)

            def transposed(dh, dl, tiles, to=0):
                for g in range(tiles // 2):
                    v.wait_ge(t_high, nt[0] + 1)
                    v.tensor_tensor(dl[:, to + 2 * g:to + 2 * g + 2, :],
                                    acc[:, g, :].rearrange("p (a b) -> p a b", a=2),
                                    dh[:, to + 2 * g:to + 2 * g + 2, :].bitcast(F32),
                                    ALU.subtract).then_inc(t_low, 1)
                    nt[0] += 1

            for c in range(AHEAD):
                low(c, c)
            v.wait_ge(x_in, 16)
            rms(resid, y, junk[:, :])
            go_transpose()
            v.wait_ge(consts, 3)
            link(v.scalar_tensor_tensor(nd[:, :], ndi[:, :], -1.0, ndi[:, :], ALU.mult, ALU.min))
            link(v.memset(nd[0:SUB, T - SUB:T], MASKED))
            v.wait_ge(par1, 48)
            for k in range(2):
                link(v.tensor_tensor_reduce(lqj[:, :], lq[:, 2 * k, :], lq[:, 2 * k + 1, :], 1.0, 0.0,
                                            ALU.mult, ALU.add, lams[:, k:k + 1]))
            v.engine_nop().then_inc(lam_s, 2)
            transposed(xh, xl, KD)
            with v.Fori(0, 3) as i:
                for j in range(4):
                    ahead_at(i * 4 + j, j)
            for c in range(CH["vd"], CH["gate"]):
                ahead(c)
            with v.Fori(0, 2) as i:
                for j in range(4):
                    ahead_at(i * 4 + (CH["gate"] + j), CH["gate"] + j)
            v.wait_ge(lam_e, 1)
            link(v.tensor_tensor(lams[:, 4:5], lams[:, 3:4], lams[:, 2:3], ALU.subtract))
            link(v.tensor_scalar(lams[:, 5:6], lams[:, 4:5], -LAM_INIT, None, ALU.add))
            v.wait_ge(rb_ok, 1)

            def first_bias(n):
                b, nk = n % 2, P * (1 + n % 2)
                v.wait_ge(at_sc, n + 1)
                pair = 2 * b
                src = acc[:, pair:pair + 2, 0:nk]
                cut = slice(T - nk, T)
                if n < 16:
                    slope = 2.0 ** (-(n // 2 + 1))
                    v.scalar_tensor_tensor(s_sb[:, b, :, 0:nk],
                                           nd[:, None, cut].to_broadcast([P, 2, nk]), 8.0 * slope, src,
                                           ALU.mult, ALU.add).then_inc(at_b, 1)
                else:
                    j = (n - 16) // 2
                    v.scalar_tensor_tensor(s_sb[:, b, :, 0:nk], src, 0.125,
                                           rb[:, 2 * j:2 * j + 2, cut], ALU.mult, ALU.add).then_inc(at_b, 1)
                v.wait_ge(at_b, n + 1)
                link(v.tensor_reduce(smx[:, b, :], s_sb[:, b, :, 0:nk], AX.X, ALU.max))
                v.tensor_scalar(smx[:, b, :], smx[:, b, :], -0.125 if n < 16 else -1.0, None, ALU.mult
                                ).then_inc(at_sm, 1)

            def first_weights(n):
                b, nk = n % 2, P * (1 + n % 2)
                v.wait_ge(at_ex, 2 * n + 2)
                if n >= 2:
                    v.wait_ge(at_d, n - 1)
                if n < 16:
                    link(v.reciprocal(rr[:, b, :], rs[:, b, :]))
                    link(v.tensor_scalar(p_sb[:, b, 0, 0:nk], p_sb[:, b, 0, 0:nk], rr[:, b, 0:1], None, ALU.mult))
                    link(v.tensor_tensor(rc[:, b:b + 1], rr[:, b, 1:2], lams[:, 5:6], ALU.mult))
                    v.scalar_tensor_tensor(p_sb[:, b, 0, 0:nk], p_sb[:, b, 1, 0:nk], rc[:, b:b + 1],
                                           p_sb[:, b, 0, 0:nk], ALU.mult, ALU.add).then_inc(at_a, 1)
                else:
                    v.reciprocal(rr[:, b, :], rs[:, b, :]).then_inc(at_a, 1)

            def first_output(n):
                b, j = n % 2, (n % 16) // 2
                v.wait_ge(at_o, n + 1)
                if n < 16:
                    v.tensor_copy(y[:, b, j * P:j * P + P], mb[:, b, 0:P]).then_inc(at_d, 1)
                else:
                    v.wait_ge(at_a, n + 1)
                    link(v.tensor_scalar(oc[:, b, j, 0:SUB], mb[:, b, 0:SUB], rr[:, b, 0:1], None, ALU.mult))
                    v.tensor_scalar(oc[:, b, j, SUB:P], mb[:, b, SUB:P], rr[:, b, 1:2], None, ALU.mult
                                    ).then_inc(at_d, 1)

            first_bias(0)
            for n in range(24):
                if n + 1 < 24:
                    first_bias(n + 1)
                first_weights(n)
                if n >= 1:
                    first_output(n - 1)
            first_output(23)
            v.wait_ge(at_d, 24)
            for tt in range(TT):
                for h in range(HEADS):
                    o = y[:, tt, h * P:h * P + P]
                    link(v.tensor_tensor_reduce(junk[:, 0:P], o, o, 1.0, 0.0, ALU.mult, ALU.add,
                                                sso[:, tt * 8 + h:tt * 8 + h + 1]))
            link(v.tensor_scalar(so[1][:, :], sso[:, :], 1.0 / P, EPS, ALU.mult, ALU.add))
            rsqrt(so[2][:, :], so[1][:, :], so[0][:, :], so[3][:, :], so[4][:, :])
            link(v.tensor_scalar(so[2][:, :], so[2][:, :], 1.0 - LAM_INIT, None, ALU.mult))
            for tt in range(TT):
                for h in range(HEADS):
                    o = y[:, tt, h * P:h * P + P]
                    link(v.scalar_tensor_tensor(o, o, so[2][:, tt * 8 + h:tt * 8 + h + 1], subw[:, :],
                                                ALU.mult, ALU.mult))
            go_transpose()
            go_transpose()
            transposed(odh, odl, KD)
            transposed(och, ocl, 4)
            mg = y[:, :, :].rearrange("p a (b c) -> p (a b) c", c=T)
            v.wait_ge(t_low, 4 + 4 + 2)
            for u in range(4):
                ahead(CH["bd"] + u)
                n = UN["bd"] + u
                v.wait_ge(c_done, CH["bd"] + u + 1)
                v.tensor_tensor(mg[:, 2 * u:2 * u + 2, :], ub[:, n % 2, :].rearrange("p (a b) -> p a b", a=2),
                                gate[:, 2 * u:2 * u + 2, :], ALU.mult).then_inc(u_free, 1)
            for u in range(4):
                if u % 2 == 0:
                    ahead(CH["bc"] + u // 2)
                n = UN["bc"] + u
                v.wait_ge(c_done, CH["bc"] + u // 2 + 1)
                gslice = gate[:, 8 + 2 * u:10 + 2 * u, :]
                v.tensor_tensor(gslice, ub[:, n % 2, :].rearrange("p (a b) -> p a b", a=2),
                                gslice, ALU.mult).then_inc(u_free, 1)
                v.wait_ge(u_free, 2 + n + 1)
                m = mg[:, 2 * u:2 * u + 2, :]
                link(v.tensor_tensor(m, m, gslice, ALU.add))
                link(v.tensor_copy(xh[:, 2 * u:2 * u + 2, :], m))
                v.tensor_tensor(xl[:, 2 * u:2 * u + 2, :], m, xh[:, 2 * u:2 * u + 2, :].bitcast(F32),
                                ALU.subtract).then_inc(bt_done, 1)
            v.wait_ge(bt_done, 4)
            v.engine_nop().then_inc(keys_go, 1)
            for c in range(CH["out"], CH["out"] + 4):
                ahead(c)

            ncd = [2]

            def add_acc(src):
                ncd[0] += 1
                v.wait_ge(c_read, ncd[0])
                for tt in range(TT):
                    link(v.tensor_tensor(resid[:, tt, :], resid[:, tt, :], src[:, tt, :], ALU.add))

            add_acc(y)
            rms(resid, y, junk[:, :])
            go_transpose()
            transposed(xh, xl, KD)
            for u in range(4):
                ahead(CH["wq"] + u)

            lowest = -3.0e38
            for tt in range(TT):
                v.wait_ge(sk_sb, 2 * tt + 2)
                units = [(h, s) for h in range(PEER_H) for s in range(2)]

                def each(items, ops):
                    for k, it in enumerate(items):
                        ins = ops(*it)
                        if k == len(items) - 1:
                            link(ins)

                each(units, lambda h, s: v.max(v16[:, h, s, 0:8], sc12[:, tt, h, s, :]))
                each(units, lambda h, s: v.max_index(i16[:, h, s, 0:8], v16[:, h, s, 0:8], sc12[:, tt, h, s, :]))
                each(units, lambda h, s: v.match_replace(sc_w[:, h, s, :], v16[:, h, s, 0:8],
                                                         sc12[:, tt, h, s, :], lowest))
                each(units, lambda h, s: v.max(v16[:, h, s, 8:16], sc_w[:, h, s, :]))
                each(units, lambda h, s: v.max_index(i16[:, h, s, 8:16], v16[:, h, s, 8:16], sc_w[:, h, s, :]))
                sq = [P, PEER_H, TOPK, TOPK]
                link(v.tensor_tensor(cand[:, :, :].rearrange("p h (a b) -> p h a b", a=TOPK),
                                     v16[:, :, 0, :, None].to_broadcast(sq),
                                     v16[:, :, 1, None, :].to_broadcast(sq), ALU.add))
                heads = [(h,) for h in range(PEER_H)]
                each(heads, lambda h: v.max(cv[:, h, 0:8], cand[:, h, :]))
                each(heads, lambda h: v.max_index(ci[:, h, 0:8], cv[:, h, 0:8], cand[:, h, :]))
                each(heads, lambda h: v.match_replace(cand_w[:, h, :], cv[:, h, 0:8], cand[:, h, :], lowest))
                each(heads, lambda h: v.max(cv[:, h, 8:16], cand_w[:, h, :]))
                each(heads, lambda h: v.max_index(ci[:, h, 8:16], cv[:, h, 8:16], cand_w[:, h, :]))
                if tt >= 1:
                    v.wait_ge(ix_ps, tt)
                v.tensor_tensor(gate_t[:, :, :], cv[:, :, :],
                                cv[:, :, 0:1].to_broadcast([P, PEER_H, TOPK]), ALU.subtract).then_inc(tk_x, 1)
                v.tensor_scalar(cab[:, 0, :, :], ci[:, :, :], 4, None, ALU.logical_shift_right)
                link(v.tensor_scalar(cab[:, 1, :, :], ci[:, :, :], TOPK - 1, None, ALU.bitwise_and))
                v.tensor_copy(cabf[:, :, :, :], cab[:, :, :, :])
                link(v.tensor_copy(i16f[:, :, :, :], i16[:, :, :, :]))
                for s in range(2):
                    work = (cand, cand_w)[s][:, :, :].rearrange("p h (a b) -> p h a b", a=TOPK)
                    link(v.tensor_tensor(work, cabf[:, s, :, :, None].to_broadcast(sq),
                                         iota[:, None, None, 0:TOPK].to_broadcast(sq), ALU.is_equal))
                    link(v.tensor_tensor(work, work, i16f[:, :, s, None, :].to_broadcast(sq), ALU.mult))
                    link(v.tensor_reduce(esel[:, s, :].rearrange("p (h k) -> p h k", h=PEER_H), work,
                                         AX.X, ALU.add))
                v.wait_ge(tk_e, tt + 1)
                link(v.tensor_reduce(gsum[:, :], gate_t[:, :, :], AX.X, ALU.add))
                link(v.reciprocal(grec[:, :], gsum[:, :]))
                v.tensor_tensor(gate_t[:, :, :], gate_t[:, :, :],
                                grec[:, :, None].to_broadcast([P, PEER_H, TOPK]), ALU.mult).then_inc(ix_in, 1)
                v.wait_ge(ix_sb, tt + 1)
                v.tensor_tensor(gTl[:, tt * P:tt * P + P].bitcast(F32R), mb[:, tt, 2 * P:3 * P],
                                gTh[:, tt * P:tt * P + P], ALU.subtract).then_inc(ix_l, 1)

            v.wait_ge(ix_l, 2)

            def second(n, b, tok, q):
                if not isinstance(n, int) or n >= 2:
                    v.wait_ge(g_ps, n - 1)
                shape = [P, GT, QW]
                if not isinstance(n, int) or n >= 1:
                    v.wait_ge(g_two, n)
                v.tensor_tensor(one2[:, :, :], i2T[:, tok][:, :, None].to_broadcast(shape),
                                iota[:, None, q * QW:q * QW + QW].to_broadcast(shape), ALU.is_equal
                                ).then_inc(g_eq, 1)
                v.wait_ge(g_eq, n + 1)
                v.tensor_tensor(g2h[:, b, :, :], one2[:, :, :], gTh[:, tok][:, :, None].to_broadcast(shape),
                                ALU.mult)
                v.tensor_tensor(g2l[:, b, :, :], one2[:, :, :], gTl[:, tok][:, :, None].to_broadcast(shape),
                                ALU.mult).then_inc(g_two, 1)

            def first_rows(n, b, tok):
                shape = [P, GT, NKEY]
                v.tensor_tensor(one1[:, b, :, :], i1T[:, tok][:, :, None].to_broadcast(shape),
                                iota[:, None, :].to_broadcast(shape), ALU.is_equal).then_inc(g_one1, 1)

            for j in range(2):
                second(j, j, slice(j * GT, j * GT + GT), 0)
                first_rows(j, j, slice(j * GT, j * GT + GT))
            with v.Fori(1, GROUPS // 2) as i:
                for j in range(2):
                    tok = bass.ds(i * (2 * GT) + j * GT, GT)
                    second(i * 2 + j, j, tok, 0)
                    first_rows(i * 2 + j, j, tok)

            C5 = CH["peer"]

            def iteration(q, i, first=False):
                m = i + 8 * q
                c = m * 4 + (C5 - 1)

                def masks(a):
                    if q + 1 < QG:
                        for j in (a, a + 1):
                            second(i * 4 + ((q + 1) * GROUPS + j), j % 2,
                                   bass.ds(i * (4 * GT) + j * GT, GT), q + 1)

                def gated(k):
                    v.wait_ge(hd_g, m * 2 + (k + 1))
                    v.wait_ge(g_sb, GROUPS * (q + 1))
                    v.tensor_tensor(hid[:, k, :, :], hid[:, k, :, :],
                                    G[:, q % 2, bass.ds(i * 4 + 2 * k, 2), :], ALU.mult).then_inc(hd_m, 1)

                def lowpart(k):
                    v.wait_ge(a_h, m * 2 + (k + 1))
                    v.tensor_tensor(al[:, k, :, :], hid[:, k, :, :], ah[:, k, :, :].bitcast(F32),
                                    ALU.subtract).then_inc(a_l, 1)

                if first:
                    masks(0)
                    ahead(C5)
                    gated(0)
                    lowpart(0)
                    masks(2)
                    ahead(C5 + 1)
                    gated(1)
                    ahead(C5 + 2)
                    lowpart(1)
                    return
                masks(0)
                ahead_at(c, C5 - 1)
                gated(0)
                ahead_at(c + 1, C5)
                lowpart(0)
                masks(2)
                ahead_at(c + 2, C5 + 1)
                gated(1)
                ahead_at(c + 3, C5 + 2)
                lowpart(1)

            for q in range(QG):
                if q == 0:
                    iteration(0, 0, first=True)
                with v.Fori(1 if q == 0 else 0, 8) as i:
                    iteration(q, i)
            ahead(C5 + 127)
            add_acc(y_again)
            rms(resid, resid, junk_again[:, :])

            def ffn(gu, dn, nf):
                rms(resid, y_again, junk_again[:, :])
                go_transpose()
                transposed(xh, xl, KD)
                C, U = CH[gu], UN[gu]

                def hidden(c, cmod, umod, n, b, dst):
                    ahead_at(c, cmod)
                    v.wait_ge(f_s, n + 1)
                    if not isinstance(n, int) or n >= 2:
                        v.wait_ge(f_l, n - 1)
                    v.tensor_tensor(ff[:, b, :], fs[:, b, :], ub[:, umod % 2, T:2 * T], ALU.mult
                                    ).then_inc(f_f, 1)
                    v.wait_ge(f_f, n + 1)
                    v.tensor_copy(fh[:, dst, :], ff[:, b:b + 1, :]).then_inc(u_free, 1)
                    v.wait_ge(u_free, 2 + U - nf + n + 1)
                    v.tensor_tensor(fl[:, dst, :], ff[:, b:b + 1, :], fh[:, dst, :].bitcast(F32),
                                    ALU.subtract).then_inc(f_l, 1)

                for j in range(2):
                    hidden(C + j, C + j, U + j, nf + j, j % 2, slice(j, j + 1))
                with v.Fori(0, 5) as i:
                    for j in range(2, 6):
                        hidden(i * 4 + (C + j), C + j, U + j, i * 4 + (nf + j), j % 2,
                               bass.ds(i * 4 + j, 1))
                for c in range(CH[dn], CH[dn] + 11):
                    ahead(c)
                ncd[0] += 1
                v.wait_ge(c_read, ncd[0])
                rms(y_again, y_again, junk_again[:, :], factor=0.5)
                for tt in range(TT):
                    link(v.tensor_tensor(resid[:, tt, :], resid[:, tt, :], y_again[:, tt, :], ALU.add))

            ffn("gu1", "dn1", 0)
            v.engine_nop().then_inc(par2_go, 1)
            rms(resid, y_again, junk_again[:, :])
            go_transpose()
            transposed(xh, xl, KD)
            for u in range(7):
                ahead(CH["in2"] + u)
            v.wait_ge(par2, 96)
            lamc = cols[:, 7, :]
            link(v.tensor_scalar(lsg[:, 4, :], lamc, -1.0, None, ALU.mult))
            v.tensor_tensor(lsg[:, 0, :], lsg[:, 4, :], lamc, ALU.min).then_inc(ls_z, 1)
            v.wait_ge(ls_e, 1)
            v.tensor_scalar(lsg[:, 2, :], lsg[:, 1, :], 1.0, None, ALU.add).then_inc(ls_z, 1)
            v.wait_ge(ls_e, 2)
            v.wait_ge(ls_z, 2)
            link(v.tensor_scalar(lsg[:, 2, :], lsg[:, 2, :], -1.0, None, ALU.add))
            link(v.tensor_scalar(lsg[:, 5, :], lsg[:, 2, :], 0.0, None, ALU.is_equal))
            link(v.tensor_tensor(lsg[:, 2, :], lsg[:, 2, :], lsg[:, 5, :], ALU.add))
            link(v.tensor_tensor(lsg[:, 3, :], lsg[:, 3, :], lsg[:, 5, :], ALU.add))
            link(v.reciprocal(lsg[:, 2, :], lsg[:, 2, :]))
            link(v.tensor_tensor(lsg[:, 3, :], lsg[:, 3, :], lsg[:, 2, :], ALU.mult))
            link(v.tensor_tensor(lsg[:, 3, :], lsg[:, 3, :], lsg[:, 1, :], ALU.mult))
            link(v.tensor_scalar(lsg[:, 4, :], lsg[:, 4, :], 0.0, None, ALU.max))
            link(v.tensor_tensor(lsg[:, 3, :], lsg[:, 3, :], lsg[:, 4, :], ALU.add))
            link(v.tensor_scalar(lsg[:, 3, :], lsg[:, 3, :], -8.0, None, ALU.mult))
            v.wait_ge(u_free, 2 + UN["in2"] + 2)
            for t in range(LT):
                link(v.tensor_scalar(xc[:, t, :], xin[:, t, 0:T], cols[:, 0, t:t + 1], cols[:, 4, t:t + 1],
                                     ALU.mult, ALU.add))
                for w in range(1, CONV):
                    ins = v.scalar_tensor_tensor(xc[:, t, :], xin[:, t, w:w + T], cols[:, w, t:t + 1],
                                                 xc[:, t, :], ALU.mult, ALU.add)
                    if w < CONV - 1:
                        link(ins)
                ins.then_inc(xc_ok, 1)
            for t in range(LT):
                v.wait_ge(rg_sb, t + 1)
                ins = v.tensor_scalar(la[:, t, :], gr[:, t, :], lsg[:, 3, t:t + 1], None, ALU.mult)
            ins.then_inc(la_ok, 1)
            v.wait_ge(xc_ok, LT)
            link(v.tensor_tensor(gi[:, :, :], gi[:, :, :], xc[:, :, :], ALU.mult))
            v.wait_ge(la_e, 2)
            link(v.tensor_tensor(gr[:, :, :], la[:, :, :], la[:, :, :], ALU.mult))
            v.scalar_tensor_tensor(th[:, :, :], gr[:, :, :], 1.0, th[:, :, :], ALU.add, ALU.mult
                                   ).then_inc(m2_ok, 1)

            def win_bias(n):
                b, nk, j = n % 2, P * (1 + n % 2), n // 2
                v.wait_ge(at_sc, 24 + n + 1)
                v.scalar_tensor_tensor(s2_sb[:, b, :, 0:nk], acc[:, 2 * b:2 * b + 2, 0:nk], 0.125,
                                       m2[:, None, T - nk:T].to_broadcast([P, 2, nk]),
                                       ALU.mult, ALU.add).then_inc(at_b, 1)
                v.wait_ge(at_b, 24 + n + 1)
                link(v.tensor_reduce(mx2[:, b, :], s2_sb[:, b, :, 0:nk], AX.X, ALU.max))
                link(v.tensor_tensor(mx2[:, b, :], mx2[:, b, :], sinkb[:, j, :], ALU.max))
                link(v.tensor_scalar(smx2[:, b, :], mx2[:, b, :], -1.0, None, ALU.mult))
                v.tensor_tensor(sd2[:, b, :], smx2[:, b, :], sinkb[:, j, :], ALU.add).then_inc(at_sm, 1)

            def win_weights(n):
                b = n % 2
                v.wait_ge(la_e, 2 + n + 1)
                v.wait_ge(at_ex, 2 * (24 + n) + 2)
                if n >= 2:
                    v.wait_ge(at_d, 24 + n - 1)
                link(v.tensor_tensor(rs2[:, b, :], rs2[:, b, :], es2[:, b, :], ALU.add))
                v.reciprocal(rr2[:, b, :], rs2[:, b, :]).then_inc(at_a, 1)

            def win_output(n):
                b, j = n % 2, n // 2
                v.wait_ge(at_o, 24 + n + 1)
                v.wait_ge(at_a, 24 + n + 1)
                link(v.tensor_scalar(o2[:, b, j, 0:SUB], mb[:, b, 0:SUB], rr2[:, b, 0:1], None, ALU.mult))
                v.tensor_scalar(o2[:, b, j, SUB:P], mb[:, b, SUB:P], rr2[:, b, 1:2], None, ALU.mult
                                ).then_inc(at_d, 1)

            v.wait_ge(x2_sb, 3)
            win_bias(0)
            for n in range(8):
                if n + 1 < 8:
                    win_bias(n + 1)
                win_weights(n)
                if n >= 1:
                    win_output(n - 1)
            win_output(7)
            v.wait_ge(at_d, 32)
            o2f = o2[:, :, :, :].rearrange("p a b c -> p a (b c)")
            rms(o2f, o2f, junk_again[:, 0:512], width=512)
            go_transpose()
            v.wait_ge(mu_ok, 1)
            link(v.tensor_tensor(gi[:, :, :], gi[:, :, :], th[:, :, :], ALU.mult))
            for t in range(LT):
                ins = v.tensor_tensor_scan(hs[:, t, :], la[:, t, :], gi[:, t, :], 0.0, ALU.mult, ALU.add)
            link(ins)
            v.wait_ge(u_free, 2 + UN["in2"] + 4)
            link(v.tensor_tensor(hs[:, :, :], hs[:, :, :], gl[:, :, :], ALU.mult))
            v.tensor_tensor(gr[:, :, :], hs[:, :, :], hs[:, :, :], ALU.mult).then_inc(yq_ok, 1)
            v.wait_ge(ss_ps, 1)
            link(v.tensor_scalar(wv[:, :], ub[:, 0, 0:T], 1.0 / 512, EPS, ALU.mult, ALU.add))
            rsqrt(wr_[:, :], wv[:, :], wi_[:, :], wa_[:, :], wb_[:, :])
            for t in range(LT):
                ins = v.scalar_tensor_tensor(hs[:, t, :], hs[:, t, :], cols[:, 8, t:t + 1], wr_[:, :],
                                             ALU.mult, ALU.mult)
            link(ins)
            link(v.tensor_copy(xh[:, 0:LT, :], hs[:, :, :]))
            v.tensor_tensor(xl[:, 0:LT, :], hs[:, :, :], xh[:, 0:LT, :].bitcast(F32), ALU.subtract
                            ).then_inc(yl_ok, 1)
            transposed(xh, xl, 4, to=4)
            for c in range(CH["wo"], CH["wo"] + 4):
                ahead(c)
            ncd[0] += 1
            v.wait_ge(c_read, ncd[0])
            rms(y_again, y_again, junk_again[:, :])
            for tt in range(TT):
                link(v.tensor_tensor(resid[:, tt, :], resid[:, tt, :], y_again[:, tt, :], ALU.add))
            ffn("gu2", "dn2", 22)
            v.engine_nop().then_inc(done, 1)

        @block.tensor
        def _(pe):
            pe.sem_inc(u_free, 2)
            pe.wait_ge(consts, 3)

            nt = [0]
            nin = [0]

            def transpose(src, tiles):
                nin[0] += 1
                pe.wait_ge(t_in, nin[0])
                if nt[0]:
                    pe.wait_ge(t_low, nt[0])
                for g in range(tiles // 2):
                    for k in range(2):
                        for tt in range(TT):
                            col = (2 * g + k) * P
                            last = pe.transpose(acc[:, g, k * T + tt * P:k * T + tt * P + P],
                                                src[:, tt, col:col + P], ident[:, :])
                    last.then_inc(t_ps, 1)
                    nt[0] += 1

            def three(dst, stand, move, first, last):
                (sh, sl), (mh, ml) = stand, move
                pe.matmul(dst, sh, mh, start=first, stop=False)
                pe.matmul(dst, sh, ml, start=False, stop=False)
                return pe.matmul(dst, sl, mh, start=False, stop=last)

            def unit(slot, u, ubank, kt=KD, at=0, sh=xh, sl=xl, tiles=2):
                if u is not None:
                    pe.wait_ge(u_free, u + 1)
                for t in range(tiles):
                    for k in range(kt):
                        o = at + (t * kt + k) * P
                        last = three(ub[:, ubank, t * T:t * T + T],
                                     (wh[:, slot, o:o + P], wl[:, slot, o:o + P]),
                                     (sh[:, k, :], sl[:, k, :]), k == 0, k == kt - 1)
                return last

            def unit_chunk(c, cmod, u, umod, tiles=2):
                pe.wait_ge(w_low, c + 1)
                unit(cmod % RING, u, umod % 2, tiles=tiles).then_inc(c_done, 1)

            def acc_chunk(c, cmod, sh, sl, k0, first, last, width=2):
                pe.wait_ge(w_low, c + 1)
                slot = cmod % RING
                for k in range(4 // width):
                    for tt in range(TT):
                        for nb in range(width):
                            o = (k * width + nb) * 512
                            tok = slice(tt * P, tt * P + P)
                            ins = three(acc[:, tt * width + nb, :],
                                        (sh[:, k0 + k, tok], sl[:, k0 + k, tok]),
                                        (wh[:, slot, o:o + 512], wl[:, slot, o:o + 512]),
                                        first and k == 0, last and k == 4 // width - 1)
                ins.then_inc(c_done, 1)

            transpose(y, KD)
            pe.wait_ge(t_low, nt[0])
            with pe.Fori(0, 3) as i:
                for j in range(4):
                    unit_chunk(i * 4 + j, j, i * 4 + j, j)
            for k in range(4):
                acc_chunk(CH["vd"] + k, CH["vd"] + k, xh, xl, 2 * k, k == 0, k == 3)
            pe.wait_ge(c_read, 1)
            for k in range(2):
                acc_chunk(CH["vc"] + k, CH["vc"] + k, xh, xl, 4 * k, k == 0, k == 1, width=1)
            with pe.Fori(0, 2) as i:
                for j in range(4):
                    unit_chunk(i * 4 + (CH["gate"] + j), CH["gate"] + j,
                               i * 4 + (UN["gate"] + j), UN["gate"] + j)

            def attention(count, n0, q_of, k_of, pb_, pt_, v_of, single_of):
                def scores(n):
                    b = n % 2
                    nk = P * (1 + b)
                    if n >= 2:
                        pe.wait_ge(at_b, n0 + n - 1)
                    for r in range(2):
                        rows = slice(SUB * r, SUB * r + SUB)
                        last = pe.matmul(acc[:, 2 * b + r, 0:nk], q_of(n)[rows, b * P:b * P + P],
                                         k_of(n)[rows, 0:nk], start=True, stop=True)
                    last.then_inc(at_sc, 1)

                def turn(n):
                    b = n % 2
                    pe.wait_ge(at_a, n0 + n + 1)
                    at = 0
                    for r in range(1 if single_of(n) else 2):
                        for kb in range(1 + b):
                            last = pe.transpose(ub[:, b, at:at + P], pb_[:, b, r, kb * P:kb * P + P],
                                                ident[:, :])
                            at += P
                    last.then_inc(at_t, 1)

                def output(n):
                    b = n % 2
                    pe.wait_ge(at_v, n0 + n + 1)
                    if n >= 2:
                        pe.wait_ge(at_d, n0 + n - 1)
                    parts = 1 if single_of(n) else 2
                    w = P // parts
                    for r in range(parts):
                        for kb in range(1 + b):
                            last = pe.matmul(mb[:, b, r * w:r * w + w], pt_[:, b, r * (1 + b) + kb, :],
                                             v_of(n, kb, r, w), start=kb == 0, stop=kb == b)
                    last.then_inc(at_o, 1)

                scores(0)
                for n in range(count):
                    if n + 1 < count:
                        scores(n + 1)
                    turn(n)
                    if n >= 1:
                        output(n - 1)
                output(count - 1)

            pe.wait_ge(c_read, 2)
            pe.wait_ge(u_free, 2 + UN["bd"])

            def v1(n, kb, r, w):
                j = (n % 16) // 2
                return (vd if n < 16 else vc)[:, kb, j * P + r * w:j * P + r * w + w]

            attention(24, 0, lambda n: qkT[:, n // 2 if n < 16 else 16 + (n - 16) // 2, :],
                      lambda n: qkT[:, 8 + n // 2 if n < 16 else 20 + (n - 16) // 2, :],
                      p_sb, pT, v1, lambda n: n < 16)
            transpose(y, KD)
            transpose(oc[:, :, :, :].rearrange("p a b c -> p a (b c)"), 4)
            pe.wait_ge(t_low, nt[0])
            for u in range(4):
                pe.wait_ge(w_low, CH["bd"] + u + 1)
                n = UN["bd"] + u
                unit((CH["bd"] + u) % RING, n, n % 2, sh=odh, sl=odl).then_inc(c_done, 1)
            for c in range(CH["bc"], CH["bc"] + 2):
                pe.wait_ge(w_low, c + 1)
                for k in range(2):
                    n = UN["bc"] + 2 * (c - CH["bc"]) + k
                    last = unit(c % RING, n, n % 2, kt=4, at=k * 2 * 4 * P, sh=och, sl=ocl)
                last.then_inc(c_done, 1)
            pe.wait_ge(bt_done, 4)
            for k in range(4):
                acc_chunk(CH["out"] + k, CH["out"] + k, xh, xl, 2 * k, k == 0, k == 3)
            transpose(y, KD)
            pe.wait_ge(t_low, nt[0])
            for u in range(4):
                unit_chunk(CH["wq"] + u, CH["wq"] + u, UN["wq"] + u, UN["wq"] + u)
            pe.wait_ge(u_free, 2 + UN["wq"] + 4)
            pe.wait_ge(keys_in, 16)
            for n in range(4):
                tt, k = n // 2, n % 2
                if n >= 2:
                    pe.wait_ge(sk_sb, n - 1)
                for s in range(2):
                    rows = slice(SUB * s, SUB * s + SUB)
                    for h in range(4):
                        last = pe.matmul(acc[:, 2 * k + s, h * NKEY:(h + 1) * NKEY],
                                         pqT[rows, 4 * k + h, tt * P:tt * P + P],
                                         keysT[rows, 4 * k + h, :], start=True, stop=True)
                last.then_inc(sk_ps, 1)
            for tt in range(TT):
                pe.wait_ge(ix_in, tt + 1)
                srcs = (esel[:, 0, :], esel[:, 1, :], gate_t[:, :, :].rearrange("p h k -> p (h k)"))
                for k, src in enumerate(srcs):
                    last = pe.transpose(mb[:, tt, k * P:k * P + P], src, ident[:, :])
                last.then_inc(ix_ps, 1)

            def spread(n, b):
                pe.wait_ge(g_two, n + 1)
                pe.wait_ge(g_one1, n + 1)
                if not isinstance(n, int) or n >= 2:
                    pe.wait_ge(g_sb, n - 1)
                for k in range(GT):
                    dst = mb[:, b, k * QW:k * QW + QW]
                    pe.matmul(dst, one1[:, b, k, :], g2h[:, b, k, :], start=True, stop=False)
                    last = pe.matmul(dst, one1[:, b, k, :], g2l[:, b, k, :], start=False, stop=True)
                last.then_inc(g_ps, 1)

            pe.wait_ge(ix_l, 2)
            for j in range(2):
                spread(j, j)
            with pe.Fori(1, GROUPS // 2) as i:
                for j in range(2):
                    spread(i * 2 + j, j)

            C5 = CH["peer"]

            def iteration(q, i, first=False):
                m = i + 8 * q

                def groups(a):
                    if q + 1 < QG:
                        for j in (a, a + 1):
                            spread(i * 4 + ((q + 1) * GROUPS + j), j % 2)

                def values(c, cmod, k, start=False):
                    pe.wait_ge(a_l, m * 2 if k == 1 else m * 2 + 1)
                    acc_chunk(c, cmod, ah[:, k, :, :], al[:, k, :, :], 0, start, False)

                def hidden(c, cmod, k):
                    if not (first and k == 0):
                        pe.wait_ge(hd_g, m * 2 + (k - 1))
                    unit_chunk(c, cmod, None, k)

                if first:
                    hidden(C5, C5, 0)
                    groups(0)
                    hidden(C5 + 1, C5 + 1, 1)
                    groups(2)
                    values(C5 + 2, C5 + 2, 0, start=True)
                    return
                c = m * 4 + (C5 - 1)
                hidden(c, C5 - 1, 0)
                groups(0)
                values(c + 1, C5, 1)
                hidden(c + 2, C5 + 1, 1)
                groups(2)
                values(c + 3, C5 + 2, 0)

            for q in range(QG):
                if q == 0:
                    iteration(0, 0, first=True)
                with pe.Fori(1 if q == 0 else 0, 8) as i:
                    iteration(q, i)
            pe.wait_ge(a_l, 64)
            acc_chunk(C5 + 127, C5 + 127, ah[:, 1, :, :], al[:, 1, :, :], 0, False, True)

            def ffn(gu, dn, nf):
                transpose(y_again, KD)
                pe.wait_ge(t_low, nt[0])
                C, U = CH[gu], UN[gu]
                for j in range(2):
                    unit_chunk(C + j, C + j, U + j, U + j)
                with pe.Fori(0, 5) as i:
                    for j in range(2, 6):
                        unit_chunk(i * 4 + (C + j), C + j, i * 4 + (U + j), U + j)
                pe.wait_ge(f_l, nf + FT)
                for k in range(11):
                    acc_chunk(CH[dn] + k, CH[dn] + k, fh, fl, 2 * k, k == 0, k == 10)

            ffn("gu1", "dn1", 0)
            transpose(y_again, KD)
            pe.wait_ge(t_low, nt[0])
            for u in range(6):
                unit_chunk(CH["in2"] + u, CH["in2"] + u, UN["in2"] + u, UN["in2"] + u)
            c = CH["in2"] + 6
            pe.wait_ge(w_low, c + 1)
            unit(c % RING, UN["in2"] + 6, (UN["in2"] + 6) % 2, tiles=1)
            for tt in range(TT):
                for k in range(KD):
                    o = (KD + k) * P
                    tok = slice(tt * P, tt * P + P)
                    last = three(mb[:, tt, 0:P], (xh[:, k, tok], xl[:, k, tok]),
                                 (wh[:, c % RING, o:o + P], wl[:, c % RING, o:o + P]), k == 0, k == KD - 1)
            last.then_inc(c_done, 1)
            pe.wait_ge(par2, 96)
            for t in range(LT):
                pe.wait_ge(xc_ok, t + 1)
                pe.matmul(acc[:, t, 0:T], bd[:, 0, t, :], xc[:, t, :], start=True, stop=True)
                pe.matmul(acc[:, t, T:2 * T], bd[:, 1, t, :], xc[:, t, :], start=True, stop=True
                          ).then_inc(rg_ps, 1)
            pe.wait_ge(u_free, 2 + UN["in2"] + 7)
            pe.wait_ge(v2_sb, 1)
            pe.wait_ge(rg_sb, LT)
            attention(8, 24, lambda n: q2T[:, n // 2, :], lambda n: q2T[:, 4, :], p2_sb, p2T,
                      lambda n, kb, r, w: v2[:, kb, r * SUB:r * SUB + SUB], lambda n: False)
            transpose(o2[:, :, :, :].rearrange("p a b c -> p a (b c)"), 4)
            pe.wait_ge(yq_ok, 1)
            for t in range(LT):
                last = pe.matmul(ub[:, 0, 0:T], ones[:, :], gr[:, t, :], start=t == 0, stop=t == LT - 1)
            last.then_inc(ss_ps, 1)
            pe.wait_ge(yl_ok, 1)
            pe.wait_ge(t_low, nt[0])
            for k in range(4):
                acc_chunk(CH["wo"] + k, CH["wo"] + k, xh, xl, 2 * k, k == 0, k == 3)
            ffn("gu2", "dn2", FT)


def layout(inputs):
    n = {k: np.asarray(a) for k, a in inputs.items()}

    def tiles(w):
        k, m = w.shape
        return w.reshape(k // P, P, m // P, P).transpose(2, 1, 0, 3)

    def chunks(t):
        per = CW // (t.shape[2] * P)
        return t.reshape(t.shape[0] // per, per, P, -1).transpose(0, 2, 1, 3).reshape(-1, P, CW)

    def wide(w):
        k, m = w.shape
        per = CW // m
        return w.reshape(k // P // per, per, P, m).transpose(0, 2, 1, 3).reshape(-1, P, CW)

    w_in = n["w_in"][0]
    s = np.split(w_in, [1024, 2048, 3072, 3584, 4096, 4608], axis=1)
    qd, kd, vd, qc, kc, vc, gates = s
    parts = {
        "qk": chunks(tiles(np.concatenate([qd, kd, qc, kc], axis=1))),
        "vd": wide(vd), "vc": wide(vc), "gate": chunks(tiles(gates)),
        "bd": chunks(tiles(n["w_branch_diff"][0])), "bc": chunks(tiles(n["w_branch_chunk"][0])),
        "out": wide(n["w_out"][0]), "wq": chunks(tiles(n["peer_wq"][0])),
    }
    u = n["peer_u"][0].reshape(NKEY, NKEY, KD, P).transpose(1, 3, 2, 0)
    u = u.reshape(NKEY // 2, 2, P, D).transpose(0, 2, 1, 3).reshape(NKEY // 2, P, CW)
    w = n["peer_v"][0].reshape(NKEY, NKEY // 2, 2 * D).transpose(1, 0, 2)
    parts["peer"] = [u[0]] + [a for k in range(1, NKEY // 2) for a in (u[k], w[k - 1])] + [w[-1]]
    for name, b in (("1", "ffn1"), ("2", "ffn2")):
        gu = tiles(n[f"{b}_w_gu_2"][0]).reshape(2, FT, P, D).transpose(1, 2, 0, 3).reshape(FT, P, CW)
        parts["gu" + name] = gu
        parts["dn" + name] = wide(n[f"{b}_w_down_2"][0])
    w2 = n["w_in_2"][0]

    def by_pair(a, axis):
        shape = a.shape[:axis] + (2, 4, SUB) + a.shape[axis + 1:]
        return a.reshape(shape).swapaxes(axis, axis + 1).reshape(a.shape)

    w2 = np.concatenate([w2[:, :1024], by_pair(w2[:, 1024:1536], 1), w2[:, 1536:]], axis=1)
    parts["in2"] = chunks(tiles(w2))
    wo = n["w_o_2"][0]
    parts["wo"] = wide(np.concatenate([wo[:512], by_pair(wo[512:], 0)], axis=0))
    stream = np.concatenate([np.asarray(parts[name]) for name, _ in _sizes], axis=0)

    def columns(a):
        return np.ascontiguousarray(a.reshape(-1, P).T)

    rev = np.pad(n["chunk_rel_bias"][0][:, ::-1], ((0, 0), (P - 1, P - 1)), mode="edge")
    rel = np.stack([rev[:, P - 1 - q:P - 1 - q + T] for q in range(P)])
    A = {
        "wstream": stream, "x": n["x"][0],
        "lq": np.concatenate([n["diff_lq1"], n["diff_lk1"], n["diff_lq2"], n["diff_lk2"]], axis=1),
        "subln": n["diff_subln_w"], "b_gate": columns(n["b_gate"][0]), "rel": rel,
        "keys": n["peer_keys"][0].transpose(1, 3, 0, 2).reshape(P, PEER_H, NKEY),
        "sinks": n["sinks_2"].reshape(1, 2, 4).transpose(0, 2, 1).reshape(1, 8),
        "cols": np.stack([columns(n["conv_w_2"][0][k]) for k in range(CONV)]
                         + [columns(n[k][0]) for k in ("conv_b_2", "b_rg_2", "b_ig_2", "lru_lambda_2",
                                                       "g_lru_out_2")], axis=1),
        "w_rg": n["w_rg_2"][0].reshape(LT, 2, SUB, SUB).transpose(1, 2, 0, 3),
        "w_ig": n["w_ig_2"][0].reshape(LT, 2, SUB, SUB).transpose(1, 2, 0, 3),
        "g_attn": by_pair(n["g_attn_out_2"], 1),
    }
    for name in NORMS:
        if name not in A:
            A[name] = n[name].reshape(1, D)
    return {k: np.ascontiguousarray(a) for k, a in A.items()}


def kernel(**inputs):
    import concourse.bacc as _bacc
    from concourse.bass_utils import run_bass_kernel_spmd as _run

    arrays = layout(inputs)
    nc = _bacc.Bacc("TRN2", target_bir_lowering=False, num_devices=1)
    A = {k: nc.dram_tensor(f"in_{k}", a.shape, mybir.dt.from_np(a.dtype), kind="ExternalInput").ap()
         for k, a in arrays.items()}
    out = nc.dram_tensor("out_x", (T, D), F32, kind="ExternalOutput").ap()
    build_program(nc, A, out)
    r = _run(nc, [{f"in_{k}": a for k, a in arrays.items()}], core_ids=[0])
    return r.results[0]["out_x"].reshape(1, T, D)
```

```python
import numpy as np

import concourse.bass as bass
import concourse.mybir as mybir
from contextlib import ExitStack

F32 = mybir.dt.float32
F32R = mybir.dt.float32r
BF16 = mybir.dt.bfloat16
I32 = mybir.dt.int32
U32 = mybir.dt.uint32
ALU = mybir.AluOpType
ACT = mybir.ActivationFunctionType
AX = mybir.AxisListType

P = 128
T = 256
TT = T // P
D = 1024
KD = D // P
EPS = 1e-6
HEADS = 8
SUB = 64
PEER_H, NKEY, TOPK = 8, 128, 16
D_FF = 2816
FT = D_FF // P
LT = 4
CONV = 4
MASKED = -1e30
LAM_INIT = 0.8 - 0.6

CW = 2048
RAW = 2
RING = 4
AHEAD = RING - 1
_sizes = [("qk", 12), ("vd", 4), ("vc", 2), ("gate", 8), ("bd", 4), ("bc", 2), ("out", 4),
          ("wq", 4), ("pu", 64), ("pv", 64), ("gu1", 22), ("dn1", 11), ("in2", 7), ("wo", 4),
          ("gu2", 22), ("dn2", 11)]
CH = {}
NCH = 0
for _name, _n in _sizes:
    CH[_name] = NCH
    NCH += _n

TOPK_U = 32

_usizes = [("qk", 12), ("gate", 8), ("bd", 4), ("bc", 4), ("wq", 4), ("gu1", 22),
           ("in2", 7), ("gu2", 22)]
UN = {}
_n0 = 0
for _name, _n in _usizes:
    UN[_name] = _n0
    _n0 += _n

QG = 4
QW = NKEY // QG
GT = 8
GROUPS = T // GT

NORMS = ["norm1_w", "norm2_w", "final_norm_w", "ffn1_pre_g_2", "ffn1_post_g_2", "mix_pre_g_2",
         "g_attn", "mix_post_g_2", "ffn2_pre_g_2", "ffn2_post_g_2"]


def build_program(nc, A, out):
    ctx = ExitStack()
    with ctx:
        def sem(name):
            return ctx.enter_context(nc.semaphore(name))

        def sb(name, shape, dt=F32, at=ctx):
            return at.enter_context(nc.sbuf_tensor(name, shape, dt))

        raw = sb("raw", [P, RAW, CW])
        wh = sb("wh", [P, RING, CW], F32R)
        wl = sb("wl", [P, RING, CW], F32R)
        resid = sb("resid", [P, TT, D])
        xh = sb("xh", [P, KD, T], F32R)
        xl = sb("xl", [P, KD, T], F32R)
        wb = sb("wb", [P, 2, D])
        ident = sb("ident", [P, P])
        iota = sb("iota", [P, NKEY])
        st = ExitStack()
        nd = sb("nd", [P, T], at=st)
        ndi = sb("ndi", [P, T], at=st)
        lq = sb("lq", [P, 4, SUB], at=st)
        st.close()
        i1T = sb("i1T", [P, T], BF16)
        i2T = sb("i2T", [P, T], BF16)
        iota8 = sb("iota8", [P, NKEY, GT], BF16)
        gT = sb("gT", [P, 3, T], BF16)
        ssq = sb("ssq", [P, TT])
        var = sb("var", [P, TT])
        nw_i = sb("nw_i", [P, TT], I32)
        nw_a = sb("nw_a", [P, TT])
        nw_b = sb("nw_b", [P, TT])
        rstd = sb("rstd", [P, TT])

        st = ExitStack()
        y = sb("y", [P, TT, D], at=st)
        junk = sb("junk", [P, D], at=st)
        st1 = ExitStack()
        gate = sb("gate", [P, 16, T], at=st1)
        oc = sb("oc", [P, TT, 4, P], at=st1)
        ndh = oc[:, 0, :, :].rearrange("p (a b) c -> p a (b c)", a=2)
        lqj = sb("lqj", [P, SUB], at=st1)
        lams = sb("lams", [P, 8], at=st1)
        subw = sb("subw", [P, P], at=st1)
        bgate = sb("bgate", [P, 16], at=st1)
        sso = sb("sso", [P, 16], at=st1)
        so = [sb(f"so{k}", [P, 16], I32 if k == 0 else F32, at=st1) for k in range(5)]
        s_sb = sb("s_sb", [P, 2, 2, T], at=st1)
        p_sb = sb("p_sb", [P, 2, 2, T], at=st1)
        pT = sb("pT", [P, 2, 4, P], at=st1)
        smx = sb("smx", [P, 2, 2], at=st1)
        rs = sb("rs", [P, 2, 2], at=st1)
        rr = sb("rr", [P, 4, 2], at=st1)
        rc = sb("rc", [P, 2], at=st1)
        st2 = ExitStack()
        qkT = sb("qkT", [P, 24, T], at=st2)
        vd = sb("vd", [P, TT, D], at=st2)
        vc = sb("vc", [P, TT, 512], at=st2)
        rb = sb("rb", [P, HEADS, T], at=st2)
        st2.close()
        st2 = ExitStack()
        odh = sb("odh", [P, KD, T], F32R, at=st2)
        odl = sb("odl", [P, KD, T], F32R, at=st2)
        och = sb("och", [P, 4, T], F32R, at=st2)
        ocl = sb("ocl", [P, 4, T], F32R, at=st2)
        st2.close()
        st1.close()

        st1 = ExitStack()
        pqT = sb("pqT", [P, PEER_H, T], at=st1)
        keysT = sb("keysT", [P, PEER_H, NKEY], at=st1)
        sc12 = sb("sc12", [P, TT, PEER_H, 2, NKEY], at=st1)
        sc_w = sb("sc_w", [P, PEER_H, 2, NKEY], at=st1)
        v16 = sb("v16", [P, PEER_H, 2, TOPK], at=st1)
        i16 = sb("i16", [P, PEER_H, 2, TOPK], U32, at=st1)
        i16f = sb("i16f", [P, PEER_H, 2, TOPK], at=st1)
        cand = sb("cand", [P, PEER_H, TOPK * TOPK], at=st1)
        cand_w = sb("cand_w", [P, PEER_H, TOPK * TOPK], at=st1)
        cv = sb("cv", [P, PEER_H, TOPK], at=st1)
        ci = sb("ci", [P, PEER_H, TOPK], U32, at=st1)
        cab = sb("cab", [P, 2, PEER_H, TOPK], U32, at=st1)
        cabf = sb("cabf", [P, 2, PEER_H, TOPK], at=st1)
        esel = sb("esel", [P, 2, PEER_H * TOPK], at=st1)
        gate_t = sb("gate_t", [P, PEER_H, TOPK], at=st1)
        gsum = sb("gsum", [P, PEER_H], at=st1)
        grec = sb("grec", [P, PEER_H], at=st1)
        gTr = sb("gTr", [P, T], at=st1)
        st1.close()
        st.close()

        st = ExitStack()
        G = sb("G", [P, 2 * QW, T], at=st)
        one1 = sb("one1", [P, 2, NKEY, GT], BF16, at=st)
        one2 = sb("one2", [P, QW, GT], BF16, at=st)
        g2 = sb("g2", [P, 2, 3, QW, GT], BF16, at=st)
        ah = sb("ah", [P, 2, 2, T], F32R, at=st)
        al = sb("al", [P, 2, 2, T], F32R, at=st)
        hid = sb("hid", [P, 4, 2, T], at=st)
        st.close()

        st = ExitStack()
        y_again = sb("y_again", [P, TT, D], at=st)
        junk_again = sb("junk_again", [P, D], at=st)
        st1 = ExitStack()
        fh = sb("fh", [P, FT, T], F32R, at=st1)
        fl = sb("fl", [P, FT, T], F32R, at=st1)
        fs = sb("fs", [P, 2, T], at=st1)
        ff = sb("ff", [P, 2, T], at=st1)
        st1.close()
        st1 = ExitStack()
        xin = sb("xin", [P, LT, CONV - 1 + T], at=st1)
        gl = sb("gl", [P, LT, T], at=st1)
        q2T = sb("q2T", [P, 5, T], at=st1)
        v2 = sb("v2", [P, TT, P], at=st1)
        xc = sb("xc", [P, LT, T], at=st1)
        gr = sb("gr", [P, LT, T], at=st1)
        gi = sb("gi", [P, LT, T], at=st1)
        la = sb("la", [P, LT, T], at=st1)
        th = sb("th", [P, LT, T], at=st1)
        hs = sb("hs", [P, LT, T], at=st1)
        bd = sb("bd", [P, 2, LT, P], at=st1)
        cols = sb("cols", [P, 9, LT], at=st1)
        lsg = sb("lsg", [P, 6, LT], at=st1)
        ones = sb("ones", [P, P], at=st1)
        m2 = sb("m2", [P, T], at=st1)
        sinkb = sb("sinkb", [P, 4, 2], at=st1)
        o2 = sb("o2", [P, TT, 4, P], at=st1)
        wv = sb("wv", [P, T], at=st1)
        wi_ = sb("wi_", [P, T], I32, at=st1)
        wa_ = sb("wa_", [P, T], at=st1)
        wb_ = sb("wb_", [P, T], at=st1)
        wr_ = sb("wr_", [P, T], at=st1)
        s2_sb = sb("s2_sb", [P, 2, 2, T], at=st1)
        p2_sb = sb("p2_sb", [P, 2, 2, T], at=st1)
        p2T = sb("p2T", [P, 2, 4, P], at=st1)
        smx2 = sb("smx2", [P, 2, 2], at=st1)
        es2 = sb("es2", [P, 2, 2], at=st1)
        rs2 = sb("rs2", [P, 2, 2], at=st1)
        rr2 = sb("rr2", [P, 4, 2], at=st1)
        nsink = sb("nsink", [P, 4, 2], at=st1)
        st1.close()
        st.close()

        hidden = nc.dram_tensor("hidden", (NKEY // 2, P, 2 * T), F32, kind="Internal").ap()

        acc = ctx.enter_context(nc.psum_tensor("acc", [P, 4, 512], F32))
        ub = ctx.enter_context(nc.psum_tensor("ub", [P, 2, 512], F32))
        mb = ctx.enter_context(nc.psum_tensor("mb", [P, 2, 512], F32))

        raw_in = [sem(f"raw_in{k}") for k in range(RAW)]
        w_high = sem("w_high")
        w_low = sem("w_low")
        c_done = sem("c_done")
        u_free = sem("u_free")
        c_read = sem("c_read")
        t_in = sem("t_in")
        t_ps = sem("t_ps")
        t_high = sem("t_high")
        t_low = sem("t_low")
        wb_in = [sem(f"wb_in{k}") for k in range(2)]
        wb_used = sem("wb_used")
        x_in = sem("x_in")
        x_out = sem("x_out")
        consts = sem("consts")
        par1 = sem("par1")
        rb_in = sem("rb_in")
        rb_ok = sem("rb_ok")
        keys_in = sem("keys_in")
        keys_go = sem("keys_go")
        par2 = sem("par2")
        par2_go = sem("par2_go")
        dve = sem("dve")
        at_sc = sem("at_sc")
        at_b = sem("at_b")
        nd_ok = sem("nd_ok")
        nh_ok = sem("nh_ok")
        at_ex = sem("at_ex")
        at_a = sem("at_a")
        at_t = sem("at_t")
        at_v = sem("at_v")
        at_o = sem("at_o")
        at_d = sem("at_d")
        lam_s = sem("lam_s")
        lam_e = sem("lam_e")
        bt_done = sem("bt_done")
        sk_ps = sem("sk_ps")
        sk_sb = sem("sk_sb")
        tk_x = sem("tk_x")
        tk_e = sem("tk_e")
        ix_in = sem("ix_in")
        ix_ps = sem("ix_ps")
        ix_sb = sem("ix_sb")
        ix_l = sem("ix_l")
        iota_ok = sem("iota_ok")
        spill = [sem(f"spill{k}") for k in range(4)]
        fetch = [sem(f"fetch{k}") for k in range(4)]
        pool_go = sem("pool_go")
        g_eq = sem("g_eq")
        g_two = sem("g_two")
        g_ps = sem("g_ps")
        g_sb = sem("g_sb")
        pool_c = sem("pool_c")
        hd_g = sem("hd_g")
        hd_m = sem("hd_m")
        a_h = sem("a_h")
        a_l = sem("a_l")
        f_s = sem("f_s")
        f_f = sem("f_f")
        f_h = sem("f_h")
        f_l = sem("f_l")
        v2_sb = sem("v2_sb")
        x2_sb = sem("x2_sb")
        ls_z = sem("ls_z")
        ls_e = sem("ls_e")
        xc_ok = sem("xc_ok")
        rg_ps = sem("rg_ps")
        rg_sb = sem("rg_sb")
        la_ok = sem("la_ok")
        la_e = sem("la_e")
        m2_ok = sem("m2_ok")
        mu_ok = sem("mu_ok")
        yq_ok = sem("yq_ok")
        ss_ps = sem("ss_ps")
        yl_ok = sem("yl_ok")
        done = sem("done")

        def groups_at(i, j):
            if isinstance(i, int):
                return range(4 * j, 4 * j + 4) if j < 2 else ()
            return range(2 * j, 2 * j + 2)

        block = ctx.enter_context(nc.Block())

        @block.sync
        def _(sp):
            stream = A["wstream"]
            for c in range(RAW):
                sp.dma_start(raw[:, c, :], stream[c]).then_inc(raw_in[c % RAW], 16)

            def load(c, slot):
                sp.wait_ge(w_low, c - RAW + 1)
                sp.dma_start(raw[:, slot, :],
                             stream[bass.ds(c, 1)].rearrange("a p n -> p (a n)")).then_inc(raw_in[slot], 16)

            pairs = (NCH - RAW) // 2
            with sp.Fori(0, pairs) as i:
                for j in range(2):
                    load(i * 2 + (RAW + j), j)
            for c in range(RAW + 2 * pairs, NCH):
                load(c, c % RAW)
            sp.wait_ge(done, 1)
            sp.dma_start(out.rearrange("(a p) d -> p a d", p=P), resid[:, :, :]).then_inc(x_out, 16)
            sp.wait_ge(x_out, 16)

        @block.gpsimd
        def _(pool):
            pool.dma_start(resid[:, :, :], A["x"].rearrange("(a p) d -> p a d", p=P)).then_inc(x_in, 16)

            def load_wb(n):
                if n >= 2:
                    pool.wait_ge(wb_used, n - 1)
                a = A[NORMS[n]]
                w = a.shape[1]
                pool.dma_start(wb[:, n % 2, 0:w], a.to_broadcast([P, w])).then_inc(wb_in[n % 2], 16)

            load_wb(0)
            load_wb(1)
            pool.memset(ident[:, :], 0.0).then_inc(pool_c, 1)
            pool.iota(iota[:, :], [[1, NKEY]], base=0, channel_multiplier=0,
                      allow_small_or_imprecise_dtypes=True).then_inc(consts, 1)
            pool.iota(ndi[:, :], [[1, T]], base=-P, channel_multiplier=-1,
                      allow_small_or_imprecise_dtypes=True).then_inc(consts, 1)
            pool.wait_ge(pool_c, 1)
            pool.affine_select(out=ident[:, :], in_=ident[:, :], compare_op=ALU.not_equal, fill=1.0,
                               base=0, pattern=[[-1, P]], channel_multiplier=1).then_inc(consts, 1)
            pool.dma_start(lq[:, :, :], A["lq"].to_broadcast([P, 4 * SUB])
                           .rearrange("p (a b) -> p a b", a=4)).then_inc(par1, 16)
            pool.dma_start(subw[:, :], A["subln"].to_broadcast([P, P])).then_inc(par1, 16)
            pool.dma_start(bgate[:, :], A["b_gate"]).then_inc(par1, 16)
            pool.dma_start(rb[:, :, :], A["rel"]).then_inc(rb_in, 16)
            pool.wait_ge(rb_in, 16)
            pool.tensor_scalar(rb[:, :, :], rb[:, :, :], 8.0, None, ALU.mult).then_inc(pool_c, 1)
            pool.wait_ge(pool_c, 2)
            pool.memset(rb[0:SUB, :, T - SUB:T], MASKED).then_inc(rb_ok, 1)
            load_wb(2)
            pool.wait_ge(nd_ok, 1)
            for h in range(HEADS):
                if h >= 2:
                    pool.wait_ge(at_b, 2 * h - 2)
                pool.tensor_scalar(ndh[:, h % 2, :], nd[:, :], 2.0 ** -(h + 1), None, ALU.mult
                                   ).then_inc(nh_ok, 1)
            pool.wait_ge(keys_go, 1)
            pool.dma_start(keysT[:, :, :], A["keys"]).then_inc(keys_in, 16)

            pool.tensor_copy(iota8[:, :, :], iota[:, :, None].to_broadcast([P, NKEY, GT])
                             ).then_inc(iota_ok, 1)

            def store(n, k):
                pool.wait_ge(hd_g, n + 1)
                pool.sem_inc(pool_go, 1)
                pool.dma_start(hidden[bass.ds(n, 1)].rearrange("a p n -> p (a n)"),
                               hid[:, k, :, :].rearrange("p a b -> p (a b)")).then_inc(spill[k], 16)

            def load(n, k, first=False):
                if first:
                    pool.wait_ge(spill[k], 16 * 16)
                else:
                    pool.wait_ge(a_l, n - 3)
                    pool.sem_inc(pool_go, 1)
                pool.dma_start(hid[:, k, :, :].rearrange("p a b -> p (a b)"),
                               hidden[bass.ds(n, 1)].rearrange("a p n -> p (a n)")).then_inc(fetch[k], 16)

            with pool.Fori(0, 16) as i:
                for k in range(4):
                    store(i * 4 + k, k)
            for k in range(4):
                load(k, k, first=True)

            def gated(n, k, mp):
                pool.wait_ge(fetch[k], (n - k) * 4 + 16)
                pool.sem_inc(pool_go, 1)
                pool.tensor_tensor(hid[:, k, :, :], hid[:, k, :, :], G[:, mp, :], ALU.mult
                                   ).then_inc(hd_m, 1)

            pool.wait_ge(g_sb, GROUPS)
            gated(0, 0, slice(0, 2))
            gated(1, 1, slice(2, 4))

            def value_step(q, i, j):
                n = i * 4 + (16 * q + j)
                if not (isinstance(n, int) and n + 4 >= 64):
                    load(n + 4, j)
                if isinstance(n, int):
                    if n + 2 < 64:
                        if (n + 2) % 16 == 0:
                            pool.wait_ge(g_sb, GROUPS * ((n + 2) // 16 + 1))
                        mp = (n + 2) % 32
                        gated(n + 2, (j + 2) % 4, slice(2 * mp, 2 * mp + 2))
                else:
                    gated(n + 2, (j + 2) % 4, bass.ds(i * 8 + (2 * (16 * (q % 2) + j + 2)), 2))

            for q in range(QG):
                with pool.Fori(0, 3) as i:
                    for j in range(4):
                        value_step(q, i, j)
                for j in range(4):
                    value_step(q, 3, j)

            for n in range(3, 6):
                load_wb(n)
            pool.wait_ge(par2_go, 1)
            pool.memset(xin[:, :, 0:CONV - 1], 0.0).then_inc(x2_sb, 1)
            pool.memset(ones[:, :], 1.0).then_inc(x2_sb, 1)
            pool.memset(bd[:, :, :, :], 0.0).then_inc(pool_c, 1)
            pool.memset(m2[:, :], 0.0).then_inc(pool_c, 1)
            pool.dma_start(cols[:, :, :], A["cols"]).then_inc(par2, 16)
            pool.dma_start(sinkb[:, :, :], A["sinks"].to_broadcast([P, 8])
                           .rearrange("p (a b) -> p a b", a=4)).then_inc(par2, 16)
            pool.wait_ge(pool_c, 2 + 2)
            for g, name in enumerate(("w_rg", "w_ig")):
                for r in range(2):
                    pool.dma_start(bd[SUB * r:SUB * r + SUB, g, :, SUB * r:SUB * r + SUB],
                                   A[name][r]).then_inc(par2, 16)
            pool.affine_select(out=m2[:, :], in_=m2[:, :], compare_op=ALU.is_ge, fill=MASKED,
                               base=P, pattern=[[-1, T]], channel_multiplier=1).then_inc(pool_c, 1)
            pool.wait_ge(pool_c, 2 + 3)
            pool.affine_select(out=m2[:, :], in_=m2[:, :], compare_op=ALU.is_gt, fill=MASKED,
                               base=0, pattern=[[1, T]], channel_multiplier=-1).then_inc(x2_sb, 1)
            for n in range(6, len(NORMS)):
                load_wb(n)

        @block.scalar
        def _(act):
            def split(c, slot):
                act.wait_ge(raw_in[slot % RAW], arrived(c, slot))
                if not isinstance(c, int) or c >= RING:
                    act.wait_ge(c_done, c - RING + 1)
                act.copy(wh[:, slot, :], raw[:, slot % RAW, :]).then_inc(w_high, 1)

            def arrived(c, slot):
                return ((c - slot % RAW) // RAW) * 16 + 16 if isinstance(c, int) else \
                    (c - slot % RAW) * (16 // RAW) + 16

            def ahead(c):
                if isinstance(c, int) and c + AHEAD < NCH:
                    split(c + AHEAD, (c + AHEAD) % RING)

            def ahead_at(c, cmod):
                split(c + AHEAD, (cmod + AHEAD) % RING)

            nt = [0]

            def transposed(dh, dl, tiles, to=0):
                for g in range(tiles // 2):
                    act.wait_ge(t_ps, nt[0] + 1)
                    act.copy(dh[:, to + 2 * g:to + 2 * g + 2, :],
                             acc[:, g, :].rearrange("p (a b) -> p a b", a=2)).then_inc(t_high, 1)
                    nt[0] += 1

            def read_acc(dst, stage, banks=4):
                act.wait_ge(c_done, CH[stage] + dict(_sizes)[stage])
                for b in range(banks):
                    tt, nb = (b // 2, b % 2) if banks == 4 else (b, 0)
                    last = act.copy(dst[:, tt, nb * 512:nb * 512 + 512], acc[:, b, :])
                last.then_inc(c_read, 1)

            for c in range(AHEAD):
                split(c, c)
            transposed(xh, xl, KD)
            for j in range(4):
                ahead(j)
                act.wait_ge(c_done, j + 1)
                act.copy(qkT[:, 2 * j:2 * j + 2, :],
                         ub[:, j % 2, :].rearrange("p (a b) -> p a b", a=2)).then_inc(u_free, 1)
            with act.Fori(1, 3) as i:
                for j in range(4):
                    ahead_at(i * 4 + j, j)
                    act.wait_ge(c_done, i * 4 + (j + 1))
                    act.copy(qkT[:, bass.ds(i * 8 + 2 * j, 2), :],
                             ub[:, j % 2, :].rearrange("p (a b) -> p a b", a=2)).then_inc(u_free, 1)
            for c in range(CH["vd"], CH["vd"] + 4):
                ahead(c)
            read_acc(vd, "vd")
            for c in range(CH["vc"], CH["vc"] + 2):
                ahead(c)
            read_acc(vc, "vc", banks=2)
            act.wait_ge(par1, 48)
            with act.Fori(0, 2) as i:
                for j in range(4):
                    ahead_at(i * 4 + (CH["gate"] + j), CH["gate"] + j)
                    act.wait_ge(c_done, i * 4 + (CH["gate"] + j + 1))
                    for k in range(2):
                        last = act.activation(gate[:, bass.ds(i * 8 + (2 * j + k), 1), :],
                                              ub[:, j % 2, k * T:k * T + T].rearrange("p (a b) -> p a b", a=1),
                                              ACT.Sigmoid, bias=bgate[:, bass.ds(i * 8 + (2 * j + k), 1)])
                    last.then_inc(u_free, 1)
            act.wait_ge(lam_s, 2)
            act.activation(lams[:, 2:4], lams[:, 0:2], ACT.Exp).then_inc(lam_e, 1)

            def attention(count, n0, sb_, pb_, pt_, mx_, r_, rr_, blocks_of, out_of, sink=False):
                def exps(n):
                    b = n % 2
                    nk = P * (1 + b)
                    act.wait_ge(at_b, n0 + n + 1)
                    for r in range(2):
                        act.activation(pb_[:, b, r, 0:nk], sb_[:, b, r, 0:nk], ACT.Exp,
                                       bias=mx_[:, b, r:r + 1], scale=-1.0,
                                       accum_out=r_[:, b, r:r + 1]).then_inc(at_ex, 1)
                    if sink:
                        for r in range(2):
                            act.activation(es2[:, b, r:r + 1], sinkb[:, n // 2, r:r + 1], ACT.Exp,
                                           bias=mx_[:, b, r:r + 1]).then_inc(la_e, 1)

                def turn(n):
                    b = n % 2
                    act.wait_ge(at_t, n0 + n + 1)
                    if n >= 2:
                        act.wait_ge(at_o, n0 + n - 1)
                    w = blocks_of(n)
                    act.copy(pt_[:, b, 0:w, :], ub[:, b, 0:w * P].rearrange("p (a b) -> p a b", a=w)
                             ).then_inc(at_v, 1)

                def output(n):
                    act.wait_ge(at_o, n0 + n + 1)
                    parts, dst = out_of(n)
                    w = P // parts
                    for r in range(parts):
                        last = act.activation(dst[:, r * w:r * w + w], mb[:, n % 2, r * w:r * w + w],
                                              ACT.Copy, scale=rr_[:, n % 4, r:r + 1])
                    last.then_inc(at_d, 1)

                for n in range(count):
                    exps(n)
                    if n >= 2:
                        output(n - 2)
                    if n >= 1:
                        turn(n - 1)
                output(count - 2)
                turn(count - 1)
                output(count - 1)

            attention(24, 0, s_sb, p_sb, pT, smx, rs, rr, lambda n: (1 if n < 16 else 2) * (1 + n % 2),
                      lambda n: (1, y[:, n % 2, n // 2 * P:n // 2 * P + P]) if n < 16 else
                      (2, oc[:, n % 2, (n - 16) // 2, :]))
            transposed(odh, odl, KD)
            transposed(och, ocl, 4)
            for c in range(CH["bd"], CH["bd"] + 6 + 4):
                ahead(c)
            read_acc(y, "out")
            transposed(xh, xl, KD)
            for u in range(4):
                ahead(CH["wq"] + u)
                act.wait_ge(c_done, CH["wq"] + u + 1)
                act.copy(pqT[:, 2 * u:2 * u + 2, :],
                         ub[:, (UN["wq"] + u) % 2, :].rearrange("p (a b) -> p a b", a=2)).then_inc(u_free, 1)
            for n in range(4):
                tt, k = n // 2, n % 2
                act.wait_ge(sk_ps, n + 1)
                for s in range(2):
                    last = act.copy(sc12[:, tt, 4 * k:4 * k + 4, s, :],
                                    acc[:, 2 * k + s, :].rearrange("p (a b) -> p a b", a=4))
                last.then_inc(sk_sb, 1)

            CU, CV = CH["pu"], CH["pv"]

            def hidden_step(n, nmod):
                ahead_at(n + CU, CU + nmod)
                act.wait_ge(c_done, n + (CU + 1))
                if not isinstance(n, int) or n >= 4:
                    act.wait_ge(spill[nmod % 4], (n - nmod % 4) * 4)
                act.activation(hid[:, nmod % 4, :, :].rearrange("p a b -> p (a b)"), ub[:, nmod % 2, :],
                               ACT.Gelu).then_inc(hd_g, 1)

            for n in range(TOPK_U):
                hidden_step(n, n)
                for tt in range(TT):
                    if n == 16 * tt + 12:
                        act.wait_ge(tk_x, tt + 1)
                        act.activation(gate_t[:, :, :], gate_t[:, :, :], ACT.Exp).then_inc(tk_e, 1)
                    if n == min(16 * tt + 17, TOPK_U - 1):
                        act.wait_ge(ix_ps, tt + 1)
                        for k, dst in enumerate((i1T, i2T)):
                            act.copy(dst[:, tt * P:tt * P + P], mb[:, tt, k * P:k * P + P])
                        act.copy(gT[:, 0, tt * P:tt * P + P], mb[:, tt, 2 * P:3 * P]).then_inc(ix_sb, 1)

            def spread(n, b, tok, qb):
                act.wait_ge(g_ps, n + 1)
                act.copy(G[:, qb * QW:qb * QW + QW, tok],
                         mb[:, b, 0:GT * QW].rearrange("p (t i) -> p i t", i=QW)).then_inc(g_sb, 1)

            for q in range(2):
                with act.Fori(0, 4) as i:
                    for j in range(4):
                        hidden_step(i * 4 + (TOPK_U + 16 * q + j), j)
                        for g in range(2):
                            spread(i * 8 + (GROUPS * q + 2 * j + g), g,
                                   bass.ds(i * (8 * GT) + (2 * j + g) * GT, GT), q)

            def high_step(n, nmod):
                act.wait_ge(hd_m, n + 1)
                if not isinstance(n, int) or n >= 2:
                    act.wait_ge(c_done, n + (CV - 1))
                act.copy(ah[:, nmod % 2, :, :], hid[:, nmod % 4, :, :]).then_inc(a_h, 1)

            high_step(0, 0)

            def value_step(q, i, j):
                n = i * 4 + (16 * q + j)
                if not (isinstance(n, int) and n == 63):
                    high_step(n + 1, j + 1)
                ahead_at(n + CV, CV + j)
                if q in (1, 2):
                    for g in groups_at(i, j):
                        spread(i * 8 + (GROUPS * (q + 1) + g), g % 2,
                               bass.ds(i * (8 * GT) + g * GT, GT), (q + 1) % 2)

            for q in range(QG):
                if q in (1, 2):
                    act.wait_ge(hd_m, 16 * q)
                with act.Fori(0, 3) as i:
                    for j in range(4):
                        value_step(q, i, j)
                for j in range(4):
                    value_step(q, 3, j)
            read_acc(y_again, "pv")

            def ffn(gu, dn, nf):
                transposed(xh, xl, KD)
                C, U = CH[gu], UN[gu]

                def hidden(c, cmod, u, umod, n, b):
                    ahead_at(c, cmod)
                    act.wait_ge(c_done, c + 1)
                    if not isinstance(n, int) or n >= 2:
                        act.wait_ge(f_f, n - 1)
                    act.activation(fs[:, b, :], ub[:, umod % 2, 0:T], ACT.Silu).then_inc(f_s, 1)

                for j in range(2):
                    hidden(C + j, C + j, U + j, U + j, nf + j, j % 2)
                with act.Fori(0, 5) as i:
                    for j in range(2, 6):
                        hidden(i * 4 + (C + j), C + j, i * 4 + (U + j), U + j, i * 4 + (nf + j), j % 2)
                for c in range(CH[dn], CH[dn] + 11):
                    ahead(c)
                read_acc(y_again, dn)

            ffn("gu1", "dn1", 0)
            transposed(xh, xl, KD)
            act.wait_ge(x2_sb, 3)
            for u in range(7):
                ahead(CH["in2"] + u)
                act.wait_ge(c_done, CH["in2"] + u + 1)
                b = (UN["in2"] + u) % 2
                src = ub[:, b, :].rearrange("p (a b) -> p a b", a=2)
                if u < 2:
                    act.copy(xin[:, 2 * u:2 * u + 2, CONV - 1:], src).then_inc(u_free, 1)
                elif u < 4:
                    act.activation(gl[:, 2 * u - 4:2 * u - 2, :], src, ACT.Gelu_apprx_tanh).then_inc(u_free, 1)
                elif u < 6:
                    act.copy(q2T[:, 2 * u - 8:2 * u - 6, :], src).then_inc(u_free, 1)
                else:
                    act.copy(q2T[:, 4, :], src[:, 0, :]).then_inc(u_free, 1)
            act.copy(v2[:, :, :], mb[:, :, 0:P]).then_inc(v2_sb, 1)
            act.wait_ge(ls_z, 1)
            act.activation(lsg[:, 1, :], lsg[:, 0, :], ACT.Exp).then_inc(ls_e, 1)
            act.wait_ge(ls_z, 2)
            act.activation(lsg[:, 3, :], lsg[:, 2, :], ACT.Ln).then_inc(ls_e, 1)
            for t in range(LT):
                act.wait_ge(rg_ps, t + 1)
                act.activation(gr[:, t, :], acc[:, t, 0:T], ACT.Sigmoid, bias=cols[:, 5, t:t + 1])
                act.activation(gi[:, t, :], acc[:, t, T:2 * T], ACT.Sigmoid, bias=cols[:, 6, t:t + 1]
                               ).then_inc(rg_sb, 1)
            act.wait_ge(la_ok, 1)
            act.activation(th[:, :, :], la[:, :, :], ACT.Tanh).then_inc(la_e, 1)
            act.activation(la[:, :, :], la[:, :, :], ACT.Exp).then_inc(la_e, 1)
            act.wait_ge(par2, 96)
            attention(8, 24, s2_sb, p2_sb, p2T, smx2, rs2, rr2, lambda n: 2 * (1 + n % 2),
                      lambda n: (2, o2[:, n % 2, n // 2, :]), sink=True)
            act.wait_ge(m2_ok, 1)
            act.activation(th[:, :, :], th[:, :, :], ACT.Sqrt, scale=-1.0).then_inc(mu_ok, 1)
            transposed(xh, xl, 4, to=4)
            for c in range(CH["wo"], CH["wo"] + 4):
                ahead(c)
            read_acc(y_again, "wo")
            ffn("gu2", "dn2", 22)

        @block.vector
        def _(v):
            steps = [0]

            def link(ins):
                steps[0] += 1
                ins.then_inc(dve, 1)
                v.wait_ge(dve, steps[0])

            def low(c, slot):
                v.wait_ge(w_high, c + 1)
                v.tensor_tensor(wl[:, slot, :], raw[:, slot % RAW, :], wh[:, slot, :].bitcast(F32),
                                ALU.subtract).then_inc(w_low, 1)

            def ahead(c):
                if c + AHEAD < NCH:
                    low(c + AHEAD, (c + AHEAD) % RING)

            def ahead_at(c, cmod):
                low(c + AHEAD, (cmod + AHEAD) % RING)

            def rsqrt(dst, src, ti, ta, tb):
                link(v.tensor_scalar(ti, src.bitcast(I32), 1, None, ALU.logical_shift_right))
                link(v.tensor_scalar(dst.bitcast(I32), ti, -1.0, float(0x5F3759DF), ALU.mult, ALU.add))
                for _ in range(3):
                    link(v.tensor_tensor(ta, dst, dst, ALU.mult))
                    link(v.scalar_tensor_tensor(tb, ta, -0.5, src, ALU.mult, ALU.mult))
                    link(v.scalar_tensor_tensor(dst, tb, 1.5, dst, ALU.add, ALU.mult))

            nwb = [0]

            def rms(src, dst, scratch, factor=1.0, width=D):
                for tt in range(TT):
                    ins = v.tensor_tensor_reduce(scratch, src[:, tt, :], src[:, tt, :], 1.0, 0.0,
                                                 ALU.mult, ALU.add, ssq[:, tt:tt + 1])
                    link(ins)
                link(v.tensor_scalar(var[:, :], ssq[:, :], 1.0 / width, EPS, ALU.mult, ALU.add))
                rsqrt(rstd[:, :], var[:, :], nw_i[:, :], nw_a[:, :], nw_b[:, :])
                if factor != 1.0:
                    link(v.tensor_scalar(rstd[:, :], rstd[:, :], factor, None, ALU.mult))
                n = nwb[0]
                nwb[0] += 1
                v.wait_ge(wb_in[n % 2], 16 * (n // 2 + 1))
                for tt in range(TT):
                    last = v.scalar_tensor_tensor(dst[:, tt, :], src[:, tt, :], rstd[:, tt:tt + 1],
                                                  wb[:, n % 2, 0:width], ALU.mult, ALU.mult)
                    if tt == 0:
                        link(last)
                last.then_inc(wb_used, 1)
                v.wait_ge(wb_used, n + 1)

            nt = [0]

            def go_transpose():
                v.engine_nop().then_inc(t_in, 1)

            def transposed(dh, dl, tiles, to=0):
                for g in range(tiles // 2):
                    v.wait_ge(t_high, nt[0] + 1)
                    v.tensor_tensor(dl[:, to + 2 * g:to + 2 * g + 2, :],
                                    acc[:, g, :].rearrange("p (a b) -> p a b", a=2),
                                    dh[:, to + 2 * g:to + 2 * g + 2, :].bitcast(F32),
                                    ALU.subtract).then_inc(t_low, 1)
                    nt[0] += 1

            for c in range(AHEAD):
                low(c, c)
            v.wait_ge(x_in, 16)
            rms(resid, y, junk[:, :])
            go_transpose()
            v.wait_ge(consts, 3)
            link(v.scalar_tensor_tensor(nd[:, :], ndi[:, :], -1.0, ndi[:, :], ALU.mult, ALU.min))
            link(v.tensor_scalar(nd[:, :], nd[:, :], 8.0, None, ALU.mult))
            v.memset(nd[0:SUB, T - SUB:T], MASKED).then_inc(nd_ok, 1)
            v.wait_ge(par1, 48)
            for k in range(2):
                link(v.tensor_tensor_reduce(lqj[:, :], lq[:, 2 * k, :], lq[:, 2 * k + 1, :], 1.0, 0.0,
                                            ALU.mult, ALU.add, lams[:, k:k + 1]))
            v.engine_nop().then_inc(lam_s, 2)
            transposed(xh, xl, KD)
            with v.Fori(0, 3) as i:
                for j in range(4):
                    ahead_at(i * 4 + j, j)
            for c in range(CH["vd"], CH["gate"]):
                ahead(c)
            with v.Fori(0, 2) as i:
                for j in range(4):
                    ahead_at(i * 4 + (CH["gate"] + j), CH["gate"] + j)
            v.wait_ge(lam_e, 1)
            link(v.tensor_tensor(lams[:, 4:5], lams[:, 3:4], lams[:, 2:3], ALU.subtract))
            link(v.tensor_scalar(lams[:, 5:6], lams[:, 4:5], -LAM_INIT, None, ALU.add))
            v.wait_ge(rb_ok, 1)

            def biased(n, n0, dst, bias_of, mx_, start_of):
                b, nk = n % 2, P * (1 + n % 2)
                v.wait_ge(at_sc, n0 + n + 1)
                for r in range(2):
                    last = v.tensor_tensor_reduce(dst[:, b, r, 0:nk], acc[:, 2 * b + r, 0:nk],
                                                  bias_of(n, r)[:, T - nk:T], -0.125, start_of(n, r),
                                                  ALU.add, ALU.min, mx_[:, b, r:r + 1])
                last.then_inc(at_b, 1)

            def first_bias(n):
                if n < 16:
                    v.wait_ge(nh_ok, n // 2 + 1)
                biased(n, 0, s_sb, lambda n, r: ndh[:, n // 2 % 2, :] if n < 16 else rb[:, 2 * (n // 2 - 8) + r, :],
                       smx, lambda n, r: 3.0e38)

            def first_weights(n):
                b, nk = n % 2, P * (1 + n % 2)
                v.wait_ge(at_ex, 2 * n + 2)
                if n >= 4:
                    v.wait_ge(at_d, n - 3)
                if n < 16:
                    link(v.reciprocal(rr[:, n % 4, :], rs[:, b, :]))
                    link(v.scalar_tensor_tensor(rc[:, b:b + 1], rr[:, n % 4, 1:2], rs[:, b, 0:1],
                                                lams[:, 5:6], ALU.mult, ALU.mult))
                    v.scalar_tensor_tensor(p_sb[:, b, 0, 0:nk], p_sb[:, b, 1, 0:nk], rc[:, b:b + 1],
                                           p_sb[:, b, 0, 0:nk], ALU.mult, ALU.add).then_inc(at_a, 1)
                else:
                    v.reciprocal(rr[:, n % 4, :], rs[:, b, :]).then_inc(at_a, 1)

            first_bias(0)
            for n in range(24):
                if n + 1 < 24:
                    first_bias(n + 1)
                first_weights(n)
            v.wait_ge(at_d, 24)
            for tt in range(TT):
                for h in range(HEADS):
                    o = y[:, tt, h * P:h * P + P]
                    link(v.tensor_tensor_reduce(junk[:, 0:P], o, o, 1.0, 0.0, ALU.mult, ALU.add,
                                                sso[:, tt * 8 + h:tt * 8 + h + 1]))
            link(v.tensor_scalar(so[1][:, :], sso[:, :], 1.0 / P, EPS, ALU.mult, ALU.add))
            rsqrt(so[2][:, :], so[1][:, :], so[0][:, :], so[3][:, :], so[4][:, :])
            link(v.tensor_scalar(so[2][:, :], so[2][:, :], 1.0 - LAM_INIT, None, ALU.mult))
            for tt in range(TT):
                for h in range(HEADS):
                    o = y[:, tt, h * P:h * P + P]
                    link(v.scalar_tensor_tensor(o, o, so[2][:, tt * 8 + h:tt * 8 + h + 1], subw[:, :],
                                                ALU.mult, ALU.mult))
            go_transpose()
            go_transpose()
            transposed(odh, odl, KD)
            transposed(och, ocl, 4)
            mg = y[:, :, :].rearrange("p a (b c) -> p (a b) c", c=T)
            v.wait_ge(t_low, 4 + 4 + 2)
            for u in range(4):
                ahead(CH["bd"] + u)
                n = UN["bd"] + u
                v.wait_ge(c_done, CH["bd"] + u + 1)
                v.tensor_tensor(mg[:, 2 * u:2 * u + 2, :], ub[:, n % 2, :].rearrange("p (a b) -> p a b", a=2),
                                gate[:, 2 * u:2 * u + 2, :], ALU.mult).then_inc(u_free, 1)
            for u in range(4):
                if u % 2 == 0:
                    ahead(CH["bc"] + u // 2)
                n = UN["bc"] + u
                v.wait_ge(c_done, CH["bc"] + u // 2 + 1)
                gslice = gate[:, 8 + 2 * u:10 + 2 * u, :]
                v.tensor_tensor(gslice, ub[:, n % 2, :].rearrange("p (a b) -> p a b", a=2),
                                gslice, ALU.mult).then_inc(u_free, 1)
                v.wait_ge(u_free, 2 + n + 1)
                m = mg[:, 2 * u:2 * u + 2, :]
                link(v.tensor_tensor(m, m, gslice, ALU.add))
                link(v.tensor_copy(xh[:, 2 * u:2 * u + 2, :], m))
                v.tensor_tensor(xl[:, 2 * u:2 * u + 2, :], m, xh[:, 2 * u:2 * u + 2, :].bitcast(F32),
                                ALU.subtract).then_inc(bt_done, 1)
            v.wait_ge(bt_done, 4)
            v.engine_nop().then_inc(keys_go, 1)
            for c in range(CH["out"], CH["out"] + 4):
                ahead(c)

            ncd = [2]

            def add_acc(src):
                ncd[0] += 1
                v.wait_ge(c_read, ncd[0])
                for tt in range(TT):
                    link(v.tensor_tensor(resid[:, tt, :], resid[:, tt, :], src[:, tt, :], ALU.add))

            add_acc(y)
            rms(resid, y, junk[:, :])
            go_transpose()
            transposed(xh, xl, KD)
            for u in range(4):
                ahead(CH["wq"] + u)

            lowest = -3.0e38
            CU, CV = CH["pu"], CH["pv"]
            nu = [0]

            def beside():
                if nu[0] < TOPK_U:
                    ahead(CU + nu[0])
                    nu[0] += 1

            def rest_of_gate(tt):
                v.wait_ge(ix_sb, tt + 1)
                rest, tok = gTr[:, tt * P:tt * P + P], slice(tt * P, tt * P + P)
                link(v.tensor_tensor(rest, mb[:, tt, 2 * P:3 * P], gT[:, 0, tok], ALU.subtract))
                link(v.tensor_copy(gT[:, 1, tok], rest))
                link(v.tensor_tensor(rest, rest, gT[:, 1, tok], ALU.subtract))
                v.tensor_copy(gT[:, 2, tok], rest).then_inc(ix_l, 1)

            for tt in range(TT):
                v.wait_ge(sk_sb, 2 * tt + 2)
                units = [(h, s) for h in range(PEER_H) for s in range(2)]

                def each(items, ops):
                    for k, it in enumerate(items):
                        ins = ops(*it)
                        if k == len(items) - 1:
                            link(ins)
                    beside()

                each(units, lambda h, s: v.max(v16[:, h, s, 0:8], sc12[:, tt, h, s, :]))
                each(units, lambda h, s: v.max_index(i16[:, h, s, 0:8], v16[:, h, s, 0:8], sc12[:, tt, h, s, :]))
                each(units, lambda h, s: v.match_replace(sc_w[:, h, s, :], v16[:, h, s, 0:8],
                                                         sc12[:, tt, h, s, :], lowest))
                each(units, lambda h, s: v.max(v16[:, h, s, 8:16], sc_w[:, h, s, :]))
                each(units, lambda h, s: v.max_index(i16[:, h, s, 8:16], v16[:, h, s, 8:16], sc_w[:, h, s, :]))
                sq = [P, PEER_H, TOPK, TOPK]
                link(v.tensor_tensor(cand[:, :, :].rearrange("p h (a b) -> p h a b", a=TOPK),
                                     v16[:, :, 0, :, None].to_broadcast(sq),
                                     v16[:, :, 1, None, :].to_broadcast(sq), ALU.add))
                beside()
                heads = [(h,) for h in range(PEER_H)]
                each(heads, lambda h: v.max(cv[:, h, 0:8], cand[:, h, :]))
                each(heads, lambda h: v.max_index(ci[:, h, 0:8], cv[:, h, 0:8], cand[:, h, :]))
                each(heads, lambda h: v.match_replace(cand_w[:, h, :], cv[:, h, 0:8], cand[:, h, :], lowest))
                each(heads, lambda h: v.max(cv[:, h, 8:16], cand_w[:, h, :]))
                each(heads, lambda h: v.max_index(ci[:, h, 8:16], cv[:, h, 8:16], cand_w[:, h, :]))
                if tt >= 1:
                    v.wait_ge(ix_ps, tt)
                v.tensor_tensor(gate_t[:, :, :], cv[:, :, :],
                                cv[:, :, 0:1].to_broadcast([P, PEER_H, TOPK]), ALU.subtract).then_inc(tk_x, 1)
                v.tensor_scalar(cab[:, 0, :, :], ci[:, :, :], 4, None, ALU.logical_shift_right)
                link(v.tensor_scalar(cab[:, 1, :, :], ci[:, :, :], TOPK - 1, None, ALU.bitwise_and))
                v.tensor_copy(cabf[:, :, :, :], cab[:, :, :, :])
                link(v.tensor_copy(i16f[:, :, :, :], i16[:, :, :, :]))
                for s in range(2):
                    work = (cand, cand_w)[s][:, :, :].rearrange("p h (a b) -> p h a b", a=TOPK)
                    link(v.tensor_tensor(work, cabf[:, s, :, :, None].to_broadcast(sq),
                                         iota[:, None, None, 0:TOPK].to_broadcast(sq), ALU.is_equal))
                    beside()
                    link(v.tensor_tensor(work, work, i16f[:, :, s, None, :].to_broadcast(sq), ALU.mult))
                    link(v.tensor_reduce(esel[:, s, :].rearrange("p (h k) -> p h k", h=PEER_H), work,
                                         AX.X, ALU.add))
                    beside()
                v.wait_ge(tk_e, tt + 1)
                link(v.tensor_reduce(gsum[:, :], gate_t[:, :, :], AX.X, ALU.add))
                link(v.reciprocal(grec[:, :], gsum[:, :]))
                v.tensor_tensor(gate_t[:, :, :], gate_t[:, :, :],
                                grec[:, :, None].to_broadcast([P, PEER_H, TOPK]), ALU.mult).then_inc(ix_in, 1)
                while nu[0] < 16 * (tt + 1):
                    beside()
            for tt in range(TT):
                rest_of_gate(tt)
            v.wait_ge(ix_l, 2)
            v.wait_ge(iota_ok, 1)

            def onehots(n, b, tok, q):
                if not isinstance(n, int) or n >= 2:
                    v.wait_ge(g_ps, n - 1)
                v.tensor_tensor(one1[:, b, :, :], iota8[:, :, :],
                                i1T[:, tok][:, None, :].to_broadcast([P, NKEY, GT]), ALU.is_equal)
                if not isinstance(n, int) or n >= 1:
                    v.wait_ge(g_two, n)
                v.tensor_tensor(one2[:, :, :], iota8[:, q * QW:q * QW + QW, :],
                                i2T[:, tok][:, None, :].to_broadcast([P, QW, GT]), ALU.is_equal
                                ).then_inc(g_eq, 1)
                v.wait_ge(g_eq, n + 1)
                shape = [P, 3, QW, GT]
                v.tensor_tensor(g2[:, b, :, :, :], one2[:, None, :, :].to_broadcast(shape),
                                gT[:, :, tok][:, :, None, :].to_broadcast(shape), ALU.mult
                                ).then_inc(g_two, 1)

            def gates_step(q, i, j):
                for g in range(2):
                    onehots(i * 8 + (GROUPS * q + 2 * j + g), g,
                            bass.ds(i * (8 * GT) + (2 * j + g) * GT, GT), q)
                ahead_at(i * 4 + (CU + TOPK_U + 16 * q + j), CU + j)

            for j in range(4):
                gates_step(0, 0, j)
            for q in range(2):
                with v.Fori(1 - q, 4) as i:
                    for j in range(4):
                        gates_step(q, i, j)

            def lowpart(n, k):
                v.wait_ge(a_h, n + 1)
                v.tensor_tensor(al[:, k % 2, :, :], hid[:, k % 4, :, :], ah[:, k % 2, :, :].bitcast(F32),
                                ALU.subtract).then_inc(a_l, 1)

            lowpart(0, 0)

            def value_step(q, i, j):
                n = i * 4 + (16 * q + j)
                if not (isinstance(n, int) and n == 63):
                    lowpart(n + 1, j + 1)
                if q in (1, 2):
                    for g in groups_at(i, j):
                        onehots(i * 8 + (GROUPS * (q + 1) + g), g % 2,
                                bass.ds(i * (8 * GT) + g * GT, GT), q + 1)
                ahead_at(n + CV, CV + j)

            for q in range(QG):
                with v.Fori(0, 3) as i:
                    for j in range(4):
                        value_step(q, i, j)
                for j in range(4):
                    value_step(q, 3, j)
            add_acc(y_again)
            rms(resid, resid, junk_again[:, :])

            def ffn(gu, dn, nf):
                rms(resid, y_again, junk_again[:, :])
                go_transpose()
                transposed(xh, xl, KD)
                C, U = CH[gu], UN[gu]

                def hidden(c, cmod, umod, n, b, dst):
                    ahead_at(c, cmod)
                    v.wait_ge(f_s, n + 1)
                    if not isinstance(n, int) or n >= 2:
                        v.wait_ge(f_l, n - 1)
                    v.tensor_tensor(ff[:, b, :], fs[:, b, :], ub[:, umod % 2, T:2 * T], ALU.mult
                                    ).then_inc(f_f, 1)
                    v.wait_ge(f_f, n + 1)
                    v.tensor_copy(fh[:, dst, :], ff[:, b:b + 1, :]).then_inc(u_free, 1)
                    v.wait_ge(u_free, 2 + U - nf + n + 1)
                    v.tensor_tensor(fl[:, dst, :], ff[:, b:b + 1, :], fh[:, dst, :].bitcast(F32),
                                    ALU.subtract).then_inc(f_l, 1)

                for j in range(2):
                    hidden(C + j, C + j, U + j, nf + j, j % 2, slice(j, j + 1))
                with v.Fori(0, 5) as i:
                    for j in range(2, 6):
                        hidden(i * 4 + (C + j), C + j, U + j, i * 4 + (nf + j), j % 2,
                               bass.ds(i * 4 + j, 1))
                for c in range(CH[dn], CH[dn] + 11):
                    ahead(c)
                ncd[0] += 1
                v.wait_ge(c_read, ncd[0])
                rms(y_again, y_again, junk_again[:, :], factor=0.5)
                for tt in range(TT):
                    link(v.tensor_tensor(resid[:, tt, :], resid[:, tt, :], y_again[:, tt, :], ALU.add))

            ffn("gu1", "dn1", 0)
            v.engine_nop().then_inc(par2_go, 1)
            rms(resid, y_again, junk_again[:, :])
            go_transpose()
            transposed(xh, xl, KD)
            for u in range(7):
                ahead(CH["in2"] + u)
            v.wait_ge(par2, 96)
            lamc = cols[:, 7, :]
            link(v.tensor_scalar(lsg[:, 4, :], lamc, -1.0, None, ALU.mult))
            v.tensor_tensor(lsg[:, 0, :], lsg[:, 4, :], lamc, ALU.min).then_inc(ls_z, 1)
            v.wait_ge(ls_e, 1)
            v.tensor_scalar(lsg[:, 2, :], lsg[:, 1, :], 1.0, None, ALU.add).then_inc(ls_z, 1)
            v.wait_ge(ls_e, 2)
            v.wait_ge(ls_z, 2)
            link(v.tensor_scalar(lsg[:, 2, :], lsg[:, 2, :], -1.0, None, ALU.add))
            link(v.tensor_scalar(lsg[:, 5, :], lsg[:, 2, :], 0.0, None, ALU.is_equal))
            link(v.tensor_tensor(lsg[:, 2, :], lsg[:, 2, :], lsg[:, 5, :], ALU.add))
            link(v.tensor_tensor(lsg[:, 3, :], lsg[:, 3, :], lsg[:, 5, :], ALU.add))
            link(v.reciprocal(lsg[:, 2, :], lsg[:, 2, :]))
            link(v.tensor_tensor(lsg[:, 3, :], lsg[:, 3, :], lsg[:, 2, :], ALU.mult))
            link(v.tensor_tensor(lsg[:, 3, :], lsg[:, 3, :], lsg[:, 1, :], ALU.mult))
            link(v.tensor_scalar(lsg[:, 4, :], lsg[:, 4, :], 0.0, None, ALU.max))
            link(v.tensor_tensor(lsg[:, 3, :], lsg[:, 3, :], lsg[:, 4, :], ALU.add))
            link(v.tensor_scalar(lsg[:, 3, :], lsg[:, 3, :], -8.0, None, ALU.mult))
            v.wait_ge(u_free, 2 + UN["in2"] + 2)
            for t in range(LT):
                link(v.tensor_scalar(xc[:, t, :], xin[:, t, 0:T], cols[:, 0, t:t + 1], cols[:, 4, t:t + 1],
                                     ALU.mult, ALU.add))
                for w in range(1, CONV):
                    ins = v.scalar_tensor_tensor(xc[:, t, :], xin[:, t, w:w + T], cols[:, w, t:t + 1],
                                                 xc[:, t, :], ALU.mult, ALU.add)
                    if w < CONV - 1:
                        link(ins)
                ins.then_inc(xc_ok, 1)
            for t in range(LT):
                v.wait_ge(rg_sb, t + 1)
                ins = v.tensor_scalar(la[:, t, :], gr[:, t, :], lsg[:, 3, t:t + 1], None, ALU.mult)
            ins.then_inc(la_ok, 1)
            v.wait_ge(xc_ok, LT)
            link(v.tensor_tensor(gi[:, :, :], gi[:, :, :], xc[:, :, :], ALU.mult))
            v.wait_ge(la_e, 2)
            link(v.tensor_tensor(gr[:, :, :], la[:, :, :], la[:, :, :], ALU.mult))
            v.scalar_tensor_tensor(th[:, :, :], gr[:, :, :], 1.0, th[:, :, :], ALU.add, ALU.mult
                                   ).then_inc(m2_ok, 1)

            def win_bias(n):
                biased(n, 24, s2_sb, lambda n, r: m2[:, :], smx2,
                       lambda n, r: nsink[:, n // 2, r:r + 1])

            def win_weights(n):
                b = n % 2
                v.wait_ge(la_e, 2 + 2 * n + 2)
                v.wait_ge(at_ex, 2 * (24 + n) + 2)
                if n >= 4:
                    v.wait_ge(at_d, 24 + n - 3)
                link(v.tensor_tensor(rs2[:, b, :], rs2[:, b, :], es2[:, b, :], ALU.add))
                v.reciprocal(rr2[:, n % 4, :], rs2[:, b, :]).then_inc(at_a, 1)

            v.wait_ge(x2_sb, 3)
            link(v.tensor_scalar(nsink[:, :, :], sinkb[:, :, :], -1.0, None, ALU.mult))
            win_bias(0)
            for n in range(8):
                if n + 1 < 8:
                    win_bias(n + 1)
                win_weights(n)
            v.wait_ge(at_d, 32)
            o2f = o2[:, :, :, :].rearrange("p a b c -> p a (b c)")
            rms(o2f, o2f, junk_again[:, 0:512], width=512)
            go_transpose()
            v.wait_ge(mu_ok, 1)
            link(v.tensor_tensor(gi[:, :, :], gi[:, :, :], th[:, :, :], ALU.mult))
            for t in range(LT):
                ins = v.tensor_tensor_scan(hs[:, t, :], la[:, t, :], gi[:, t, :], 0.0, ALU.mult, ALU.add)
            link(ins)
            v.wait_ge(u_free, 2 + UN["in2"] + 4)
            link(v.tensor_tensor(hs[:, :, :], hs[:, :, :], gl[:, :, :], ALU.mult))
            v.tensor_tensor(gr[:, :, :], hs[:, :, :], hs[:, :, :], ALU.mult).then_inc(yq_ok, 1)
            v.wait_ge(ss_ps, 1)
            link(v.tensor_scalar(wv[:, :], ub[:, 0, 0:T], 1.0 / 512, EPS, ALU.mult, ALU.add))
            rsqrt(wr_[:, :], wv[:, :], wi_[:, :], wa_[:, :], wb_[:, :])
            for t in range(LT):
                ins = v.scalar_tensor_tensor(hs[:, t, :], hs[:, t, :], cols[:, 8, t:t + 1], wr_[:, :],
                                             ALU.mult, ALU.mult)
            link(ins)
            link(v.tensor_copy(xh[:, 0:LT, :], hs[:, :, :]))
            v.tensor_tensor(xl[:, 0:LT, :], hs[:, :, :], xh[:, 0:LT, :].bitcast(F32), ALU.subtract
                            ).then_inc(yl_ok, 1)
            transposed(xh, xl, 4, to=4)
            for c in range(CH["wo"], CH["wo"] + 4):
                ahead(c)
            ncd[0] += 1
            v.wait_ge(c_read, ncd[0])
            rms(y_again, y_again, junk_again[:, :])
            for tt in range(TT):
                link(v.tensor_tensor(resid[:, tt, :], resid[:, tt, :], y_again[:, tt, :], ALU.add))
            ffn("gu2", "dn2", 22)
            v.engine_nop().then_inc(done, 1)

        @block.tensor
        def _(pe):
            pe.sem_inc(u_free, 2)
            pe.wait_ge(consts, 3)

            nt = [0]
            nin = [0]

            def transpose(src, tiles):
                nin[0] += 1
                pe.wait_ge(t_in, nin[0])
                if nt[0]:
                    pe.wait_ge(t_low, nt[0])
                for g in range(tiles // 2):
                    for k in range(2):
                        for tt in range(TT):
                            col = (2 * g + k) * P
                            last = pe.transpose(acc[:, g, k * T + tt * P:k * T + tt * P + P],
                                                src[:, tt, col:col + P], ident[:, :])
                    last.then_inc(t_ps, 1)
                    nt[0] += 1

            def three(dst, stand, move, first, last):
                (sh, sl), (mh, ml) = stand, move
                pe.matmul(dst, sh, mh, start=first, stop=False)
                pe.matmul(dst, sh, ml, start=False, stop=False)
                return pe.matmul(dst, sl, mh, start=False, stop=last)

            def unit(slot, u, ubank, kt=KD, at=0, sh=xh, sl=xl, tiles=2):
                if u is not None:
                    pe.wait_ge(u_free, u + 1)
                for t in range(tiles):
                    for k in range(kt):
                        o = at + (t * kt + k) * P
                        last = three(ub[:, ubank, t * T:t * T + T],
                                     (wh[:, slot, o:o + P], wl[:, slot, o:o + P]),
                                     (sh[:, k, :], sl[:, k, :]), k == 0, k == kt - 1)
                return last

            def unit_chunk(c, cmod, u, umod, tiles=2):
                pe.wait_ge(w_low, c + 1)
                unit(cmod % RING, u, umod % 2, tiles=tiles).then_inc(c_done, 1)

            def acc_chunk(c, cmod, sh, sl, k0, first, last, width=2):
                pe.wait_ge(w_low, c + 1)
                slot = cmod % RING
                for k in range(4 // width):
                    for tt in range(TT):
                        for nb in range(width):
                            o = (k * width + nb) * 512
                            tok = slice(tt * P, tt * P + P)
                            ins = three(acc[:, tt * width + nb, :],
                                        (sh[:, k0 + k, tok], sl[:, k0 + k, tok]),
                                        (wh[:, slot, o:o + 512], wl[:, slot, o:o + 512]),
                                        first and k == 0, last and k == 4 // width - 1)
                ins.then_inc(c_done, 1)

            transpose(y, KD)
            pe.wait_ge(t_low, nt[0])
            with pe.Fori(0, 3) as i:
                for j in range(4):
                    unit_chunk(i * 4 + j, j, i * 4 + j, j)
            for k in range(4):
                acc_chunk(CH["vd"] + k, CH["vd"] + k, xh, xl, 2 * k, k == 0, k == 3)
            pe.wait_ge(c_read, 1)
            for k in range(2):
                acc_chunk(CH["vc"] + k, CH["vc"] + k, xh, xl, 4 * k, k == 0, k == 1, width=1)
            with pe.Fori(0, 2) as i:
                for j in range(4):
                    unit_chunk(i * 4 + (CH["gate"] + j), CH["gate"] + j,
                               i * 4 + (UN["gate"] + j), UN["gate"] + j)

            def attention(count, n0, q_of, k_of, pb_, pt_, v_of, single_of):
                def scores(n):
                    b = n % 2
                    nk = P * (1 + b)
                    if n >= 2:
                        pe.wait_ge(at_b, n0 + n - 1)
                    for r in range(2):
                        rows = slice(SUB * r, SUB * r + SUB)
                        last = pe.matmul(acc[:, 2 * b + r, 0:nk], q_of(n)[rows, b * P:b * P + P],
                                         k_of(n)[rows, 0:nk], start=True, stop=True)
                    last.then_inc(at_sc, 1)

                def turn(n):
                    b = n % 2
                    pe.wait_ge(at_a, n0 + n + 1)
                    at = 0
                    for r in range(1 if single_of(n) else 2):
                        for kb in range(1 + b):
                            last = pe.transpose(ub[:, b, at:at + P], pb_[:, b, r, kb * P:kb * P + P],
                                                ident[:, :])
                            at += P
                    last.then_inc(at_t, 1)

                def output(n):
                    b = n % 2
                    pe.wait_ge(at_v, n0 + n + 1)
                    if n >= 2:
                        pe.wait_ge(at_d, n0 + n - 1)
                    parts = 1 if single_of(n) else 2
                    w = P // parts
                    for r in range(parts):
                        for kb in range(1 + b):
                            last = pe.matmul(mb[:, b, r * w:r * w + w], pt_[:, b, r * (1 + b) + kb, :],
                                             v_of(n, kb, r, w), start=kb == 0, stop=kb == b)
                    last.then_inc(at_o, 1)

                scores(0)
                for n in range(count):
                    if n + 1 < count:
                        scores(n + 1)
                    if n >= 1:
                        output(n - 1)
                    turn(n)
                output(count - 1)

            pe.wait_ge(c_read, 2)
            pe.wait_ge(u_free, 2 + UN["bd"])

            def v1(n, kb, r, w):
                j = (n % 16) // 2
                return (vd if n < 16 else vc)[:, kb, j * P + r * w:j * P + r * w + w]

            attention(24, 0, lambda n: qkT[:, n // 2 if n < 16 else 16 + (n - 16) // 2, :],
                      lambda n: qkT[:, 8 + n // 2 if n < 16 else 20 + (n - 16) // 2, :],
                      p_sb, pT, v1, lambda n: n < 16)
            transpose(y, KD)
            transpose(oc[:, :, :, :].rearrange("p a b c -> p a (b c)"), 4)
            pe.wait_ge(t_low, nt[0])
            for u in range(4):
                pe.wait_ge(w_low, CH["bd"] + u + 1)
                n = UN["bd"] + u
                unit((CH["bd"] + u) % RING, n, n % 2, sh=odh, sl=odl).then_inc(c_done, 1)
            for c in range(CH["bc"], CH["bc"] + 2):
                pe.wait_ge(w_low, c + 1)
                for k in range(2):
                    n = UN["bc"] + 2 * (c - CH["bc"]) + k
                    last = unit(c % RING, n, n % 2, kt=4, at=k * 2 * 4 * P, sh=och, sl=ocl)
                last.then_inc(c_done, 1)
            pe.wait_ge(bt_done, 4)
            for k in range(4):
                acc_chunk(CH["out"] + k, CH["out"] + k, xh, xl, 2 * k, k == 0, k == 3)
            transpose(y, KD)
            pe.wait_ge(t_low, nt[0])
            for u in range(4):
                unit_chunk(CH["wq"] + u, CH["wq"] + u, UN["wq"] + u, UN["wq"] + u)
            pe.wait_ge(u_free, 2 + UN["wq"] + 4)
            pe.wait_ge(keys_in, 16)
            for n in range(4):
                tt, k = n // 2, n % 2
                if n >= 2:
                    pe.wait_ge(sk_sb, n - 1)
                for s in range(2):
                    rows = slice(SUB * s, SUB * s + SUB)
                    for h in range(4):
                        last = pe.matmul(acc[:, 2 * k + s, h * NKEY:(h + 1) * NKEY],
                                         pqT[rows, 4 * k + h, tt * P:tt * P + P],
                                         keysT[rows, 4 * k + h, :], start=True, stop=True)
                last.then_inc(sk_ps, 1)
            CU, CV = CH["pu"], CH["pv"]

            def hidden_step(n, nmod):
                if not isinstance(n, int) or n >= 2:
                    pe.wait_ge(hd_g, n - 1)
                unit_chunk(n + CU, CU + nmod, None, nmod)

            def turn_indices(tt):
                pe.wait_ge(ix_in, tt + 1)
                srcs = (esel[:, 0, :], esel[:, 1, :], gate_t[:, :, :].rearrange("p h k -> p (h k)"))
                for k, src in enumerate(srcs):
                    last = pe.transpose(mb[:, tt, k * P:k * P + P], src, ident[:, :])
                last.then_inc(ix_ps, 1)

            def spread(n, b):
                pe.wait_ge(g_two, n + 1)
                if not isinstance(n, int) or n >= 2:
                    pe.wait_ge(g_sb, n - 1)
                for k in range(GT):
                    dst = mb[:, b, k * QW:k * QW + QW]
                    for part in range(3):
                        last = pe.matmul(dst, one1[:, b, :, k], g2[:, b, part, :, k],
                                         start=part == 0, stop=part == 2)
                last.then_inc(g_ps, 1)

            for n in range(16):
                hidden_step(n, n)
            hidden_step(16, 16)
            turn_indices(0)
            for n in range(17, TOPK_U):
                hidden_step(n, n)
            turn_indices(1)
            def gates_step(q, i, j):
                hidden_step(i * 4 + (TOPK_U + 16 * q + j), j)
                for g in range(2):
                    spread(i * 8 + (GROUPS * q + 2 * j + g), g)

            for j in range(4):
                gates_step(0, 0, j)
            for q in range(2):
                with pe.Fori(1 - q, 4) as i:
                    for j in range(4):
                        gates_step(q, i, j)

            def value_step(q, i, j, first=False, last=False):
                n = i * 4 + (16 * q + j)
                pe.wait_ge(a_l, n + 1)
                acc_chunk(n + CV, CV + j, ah[:, j % 2, :, :], al[:, j % 2, :, :], 0, first, last)
                if q in (1, 2):
                    for g in groups_at(i, j):
                        spread(i * 8 + (GROUPS * (q + 1) + g), g % 2)

            for q in range(QG):
                if q == 0:
                    for j in range(4):
                        value_step(0, 0, j, first=j == 0)
                with pe.Fori(1 if q == 0 else 0, 3) as i:
                    for j in range(4):
                        value_step(q, i, j)
                for j in range(4):
                    value_step(q, 3, j, last=q == QG - 1 and j == 3)

            def ffn(gu, dn, nf):
                transpose(y_again, KD)
                pe.wait_ge(t_low, nt[0])
                C, U = CH[gu], UN[gu]
                for j in range(2):
                    unit_chunk(C + j, C + j, U + j, U + j)
                with pe.Fori(0, 5) as i:
                    for j in range(2, 6):
                        unit_chunk(i * 4 + (C + j), C + j, i * 4 + (U + j), U + j)
                pe.wait_ge(f_l, nf + FT)
                for k in range(11):
                    acc_chunk(CH[dn] + k, CH[dn] + k, fh, fl, 2 * k, k == 0, k == 10)

            ffn("gu1", "dn1", 0)
            transpose(y_again, KD)
            pe.wait_ge(t_low, nt[0])
            for u in range(6):
                unit_chunk(CH["in2"] + u, CH["in2"] + u, UN["in2"] + u, UN["in2"] + u)
            c = CH["in2"] + 6
            pe.wait_ge(w_low, c + 1)
            unit(c % RING, UN["in2"] + 6, (UN["in2"] + 6) % 2, tiles=1)
            for tt in range(TT):
                for k in range(KD):
                    o = (KD + k) * P
                    tok = slice(tt * P, tt * P + P)
                    last = three(mb[:, tt, 0:P], (xh[:, k, tok], xl[:, k, tok]),
                                 (wh[:, c % RING, o:o + P], wl[:, c % RING, o:o + P]), k == 0, k == KD - 1)
            last.then_inc(c_done, 1)
            pe.wait_ge(par2, 96)
            for t in range(LT):
                pe.wait_ge(xc_ok, t + 1)
                pe.matmul(acc[:, t, 0:T], bd[:, 0, t, :], xc[:, t, :], start=True, stop=True)
                pe.matmul(acc[:, t, T:2 * T], bd[:, 1, t, :], xc[:, t, :], start=True, stop=True
                          ).then_inc(rg_ps, 1)
            pe.wait_ge(u_free, 2 + UN["in2"] + 7)
            pe.wait_ge(v2_sb, 1)
            pe.wait_ge(rg_sb, LT)
            attention(8, 24, lambda n: q2T[:, n // 2, :], lambda n: q2T[:, 4, :], p2_sb, p2T,
                      lambda n, kb, r, w: v2[:, kb, r * SUB:r * SUB + SUB], lambda n: False)
            transpose(o2[:, :, :, :].rearrange("p a b c -> p a (b c)"), 4)
            pe.wait_ge(yq_ok, 1)
            for t in range(LT):
                last = pe.matmul(ub[:, 0, 0:T], ones[:, :], gr[:, t, :], start=t == 0, stop=t == LT - 1)
            last.then_inc(ss_ps, 1)
            pe.wait_ge(yl_ok, 1)
            pe.wait_ge(t_low, nt[0])
            for k in range(4):
                acc_chunk(CH["wo"] + k, CH["wo"] + k, xh, xl, 2 * k, k == 0, k == 3)
            ffn("gu2", "dn2", FT)


def layout(inputs):
    n = {k: np.asarray(a) for k, a in inputs.items()}

    def tiles(w):
        k, m = w.shape
        return w.reshape(k // P, P, m // P, P).transpose(2, 1, 0, 3)

    def chunks(t):
        per = CW // (t.shape[2] * P)
        return t.reshape(t.shape[0] // per, per, P, -1).transpose(0, 2, 1, 3).reshape(-1, P, CW)

    def wide(w):
        k, m = w.shape
        per = CW // m
        return w.reshape(k // P // per, per, P, m).transpose(0, 2, 1, 3).reshape(-1, P, CW)

    w_in = n["w_in"][0]
    s = np.split(w_in, [1024, 2048, 3072, 3584, 4096, 4608], axis=1)
    qd, kd, vd, qc, kc, vc, gates = s
    parts = {
        "qk": chunks(tiles(np.concatenate([qd, kd, qc, kc], axis=1))),
        "vd": wide(vd), "vc": wide(vc), "gate": chunks(tiles(gates)),
        "bd": chunks(tiles(n["w_branch_diff"][0])), "bc": chunks(tiles(n["w_branch_chunk"][0])),
        "out": wide(n["w_out"][0]), "wq": chunks(tiles(n["peer_wq"][0])),
    }
    u = n["peer_u"][0].reshape(NKEY, NKEY, KD, P).transpose(1, 3, 2, 0)
    u = u.reshape(NKEY // 2, 2, P, D).transpose(0, 2, 1, 3).reshape(NKEY // 2, P, CW)
    w = n["peer_v"][0].reshape(NKEY, NKEY // 2, 2 * D).transpose(1, 0, 2)
    parts["pu"], parts["pv"] = u, w
    for name, b in (("1", "ffn1"), ("2", "ffn2")):
        gu = tiles(n[f"{b}_w_gu_2"][0]).reshape(2, FT, P, D).transpose(1, 2, 0, 3).reshape(FT, P, CW)
        parts["gu" + name] = gu
        parts["dn" + name] = wide(n[f"{b}_w_down_2"][0])
    w2 = n["w_in_2"][0]

    def by_pair(a, axis):
        shape = a.shape[:axis] + (2, 4, SUB) + a.shape[axis + 1:]
        return a.reshape(shape).swapaxes(axis, axis + 1).reshape(a.shape)

    w2 = np.concatenate([w2[:, :1024], by_pair(w2[:, 1024:1536], 1), w2[:, 1536:]], axis=1)
    parts["in2"] = chunks(tiles(w2))
    wo = n["w_o_2"][0]
    parts["wo"] = wide(np.concatenate([wo[:512], by_pair(wo[512:], 0)], axis=0))
    stream = np.concatenate([np.asarray(parts[name]) for name, _ in _sizes], axis=0)

    def columns(a):
        return np.ascontiguousarray(a.reshape(-1, P).T)

    rev = np.pad(n["chunk_rel_bias"][0][:, ::-1], ((0, 0), (P - 1, P - 1)), mode="edge")
    rel = np.stack([rev[:, P - 1 - q:P - 1 - q + T] for q in range(P)])
    A = {
        "wstream": stream, "x": n["x"][0],
        "lq": np.concatenate([n["diff_lq1"], n["diff_lk1"], n["diff_lq2"], n["diff_lk2"]], axis=1),
        "subln": n["diff_subln_w"], "b_gate": columns(n["b_gate"][0]), "rel": rel,
        "keys": n["peer_keys"][0].transpose(1, 3, 0, 2).reshape(P, PEER_H, NKEY),
        "sinks": n["sinks_2"].reshape(1, 2, 4).transpose(0, 2, 1).reshape(1, 8),
        "cols": np.stack([columns(n["conv_w_2"][0][k]) for k in range(CONV)]
                         + [columns(n[k][0]) for k in ("conv_b_2", "b_rg_2", "b_ig_2", "lru_lambda_2",
                                                       "g_lru_out_2")], axis=1),
        "w_rg": n["w_rg_2"][0].reshape(LT, 2, SUB, SUB).transpose(1, 2, 0, 3),
        "w_ig": n["w_ig_2"][0].reshape(LT, 2, SUB, SUB).transpose(1, 2, 0, 3),
        "g_attn": by_pair(n["g_attn_out_2"], 1),
    }
    for name in NORMS:
        if name not in A:
            A[name] = n[name].reshape(1, D)
    return {k: np.ascontiguousarray(a) for k, a in A.items()}


def kernel(**inputs):
    import concourse.bacc as _bacc
    from concourse.bass_utils import run_bass_kernel_spmd as _run

    arrays = layout(inputs)
    nc = _bacc.Bacc("TRN2", target_bir_lowering=False, num_devices=1)
    A = {k: nc.dram_tensor(f"in_{k}", a.shape, mybir.dt.from_np(a.dtype), kind="ExternalInput").ap()
         for k, a in arrays.items()}
    out = nc.dram_tensor("out_x", (T, D), F32, kind="ExternalOutput").ap()
    build_program(nc, A, out)
    r = _run(nc, [{f"in_{k}": a for k, a in arrays.items()}], core_ids=[0])
    return r.results[0]["out_x"].reshape(1, T, D)
```

```python
import numpy as np

import concourse.bass as bass
import concourse.mybir as mybir
from contextlib import ExitStack

F32 = mybir.dt.float32
F32R = mybir.dt.float32r
BF16 = mybir.dt.bfloat16
I32 = mybir.dt.int32
U32 = mybir.dt.uint32
ALU = mybir.AluOpType
ACT = mybir.ActivationFunctionType
AX = mybir.AxisListType

P = 128
T = 256
TT = T // P
D = 1024
KD = D // P
EPS = 1e-6
HEADS = 8
SUB = 64
PEER_H, NKEY, TOPK = 8, 128, 16
D_FF = 2816
FT = D_FF // P
LT = 4
CONV = 4
MASKED = -1e30
LAM_INIT = 0.8 - 0.6

CW = 2048
RAW = 2
RING = 4
AHEAD = RING - 1
_sizes = [("qk", 12), ("vd", 4), ("vc", 2), ("gate", 8), ("bd", 4), ("bc", 2), ("out", 4),
          ("wq", 4), ("pu", 64), ("pv", 64), ("gu1", 22), ("dn1", 11), ("in2", 7), ("wo", 4),
          ("gu2", 22), ("dn2", 11)]
CH = {}
NCH = 0
for _name, _n in _sizes:
    CH[_name] = NCH
    NCH += _n

TOPK_U = 32

_usizes = [("qk", 12), ("gate", 8), ("bd", 4), ("bc", 4), ("wq", 4), ("gu1", 22),
           ("in2", 7), ("gu2", 22)]
UN = {}
_n0 = 0
for _name, _n in _usizes:
    UN[_name] = _n0
    _n0 += _n

LAST_R = 2 * 5

QG = 4
QW = NKEY // QG
GT = 8
GROUPS = T // GT

NORMS = ["norm1_w", "norm2_w", "final_norm_w", "ffn1_pre_g_2", "ffn1_post_g_2", "mix_pre_g_2",
         "g_attn", "mix_post_g_2", "ffn2_pre_g_2", "ffn2_post_g_2"]


def build_program(nc, A, out):
    ctx = ExitStack()
    with ctx:
        def sem(name):
            return ctx.enter_context(nc.semaphore(name))

        def sb(name, shape, dt=F32, at=ctx):
            return at.enter_context(nc.sbuf_tensor(name, shape, dt))

        raw = sb("raw", [P, RAW, CW])
        wh = sb("wh", [P, RING, CW], F32R)
        wl = sb("wl", [P, RING, CW], F32R)
        resid = sb("resid", [P, TT, D])
        xh = sb("xh", [P, KD, T], F32R)
        xl = sb("xl", [P, KD, T], F32R)
        wb = sb("wb", [P, 2, D])
        ident = sb("ident", [P, P])
        iota = sb("iota", [P, NKEY])
        st = ExitStack()
        nd = sb("nd", [P, T], at=st)
        ndi = sb("ndi", [P, T], at=st)
        lq = sb("lq", [P, 4, SUB], at=st)
        st.close()
        i1T = sb("i1T", [P, T], BF16)
        i2T = sb("i2T", [P, T], BF16)
        iota8 = sb("iota8", [P, NKEY, GT], BF16)
        gT = sb("gT", [P, 3, T], BF16)
        ssq = sb("ssq", [P, TT])
        var = sb("var", [P, TT])
        nw_i = sb("nw_i", [P, TT], I32)
        nw_a = sb("nw_a", [P, TT])
        nw_b = sb("nw_b", [P, TT])
        rstd = sb("rstd", [P, TT])

        st = ExitStack()
        y = sb("y", [P, TT, D], at=st)
        junk = sb("junk", [P, D], at=st)
        st1 = ExitStack()
        gate = sb("gate", [P, 16, T], at=st1)
        oc = sb("oc", [P, TT, 4, P], at=st1)
        ndh = oc[:, 0, :, :].rearrange("p (a b) c -> p a (b c)", a=2)
        lqj = sb("lqj", [P, SUB], at=st1)
        lams = sb("lams", [P, 8], at=st1)
        subw = sb("subw", [P, P], at=st1)
        bgate = sb("bgate", [P, 16], at=st1)
        sso = sb("sso", [P, 16], at=st1)
        so = [sb(f"so{k}", [P, 16], I32 if k == 0 else F32, at=st1) for k in range(5)]
        s_sb = sb("s_sb", [P, 2, 2, T], at=st1)
        p_sb = sb("p_sb", [P, 2, 2, T], at=st1)
        pT = sb("pT", [P, 2, 4, P], at=st1)
        smx = sb("smx", [P, 2, 2], at=st1)
        rs = sb("rs", [P, 2, 2], at=st1)
        rr = sb("rr", [P, 4, 2], at=st1)
        rc = sb("rc", [P, 2], at=st1)
        st2 = ExitStack()
        qkT = sb("qkT", [P, 24, T], at=st2)
        vd = sb("vd", [P, TT, D], at=st2)
        vc = sb("vc", [P, TT, 512], at=st2)
        rb = sb("rb", [P, HEADS, T], at=st2)
        st2.close()
        st2 = ExitStack()
        odh = sb("odh", [P, KD, T], F32R, at=st2)
        odl = sb("odl", [P, KD, T], F32R, at=st2)
        och = sb("och", [P, 4, T], F32R, at=st2)
        ocl = sb("ocl", [P, 4, T], F32R, at=st2)
        st2.close()
        st1.close()

        st1 = ExitStack()
        pqT = sb("pqT", [P, PEER_H, T], at=st1)
        keysT = sb("keysT", [P, PEER_H, NKEY], at=st1)
        sc12 = sb("sc12", [P, TT, PEER_H, 2, NKEY], at=st1)
        sc_w = sb("sc_w", [P, PEER_H, 2, NKEY], at=st1)
        v16 = sb("v16", [P, PEER_H, 2, TOPK], at=st1)
        i16 = sb("i16", [P, PEER_H, 2, TOPK], U32, at=st1)
        i16f = sb("i16f", [P, PEER_H, 2, TOPK], at=st1)
        cand = sb("cand", [P, PEER_H, TOPK * TOPK], at=st1)
        cand_w = sb("cand_w", [P, PEER_H, TOPK * TOPK], at=st1)
        cv = sb("cv", [P, PEER_H, TOPK], at=st1)
        ci = sb("ci", [P, PEER_H, TOPK], U32, at=st1)
        cab = sb("cab", [P, 2, PEER_H, TOPK], U32, at=st1)
        cabf = sb("cabf", [P, 2, PEER_H, TOPK], at=st1)
        esel = sb("esel", [P, 2, PEER_H * TOPK], at=st1)
        gate_t = sb("gate_t", [P, PEER_H, TOPK], at=st1)
        gsum = sb("gsum", [P, PEER_H], at=st1)
        grec = sb("grec", [P, PEER_H], at=st1)
        gTr = sb("gTr", [P, T], at=st1)
        st1.close()
        st.close()

        st = ExitStack()
        G = sb("G", [P, 2 * QW, T], at=st)
        one1 = sb("one1", [P, 2, NKEY, GT], BF16, at=st)
        one2 = sb("one2", [P, QW, GT], BF16, at=st)
        g2 = sb("g2", [P, 2, 3, QW, GT], BF16, at=st)
        ah = sb("ah", [P, 2, 2, T], F32R, at=st)
        al = sb("al", [P, 2, 2, T], F32R, at=st)
        hid = sb("hid", [P, 4, 2, T], at=st)
        st.close()

        st = ExitStack()
        y_again = sb("y_again", [P, TT, D], at=st)
        junk_again = sb("junk_again", [P, D], at=st)
        st1 = ExitStack()
        fh = sb("fh", [P, FT, T], F32R, at=st1)
        fl = sb("fl", [P, FT, T], F32R, at=st1)
        fs = sb("fs", [P, 2, T], at=st1)
        ff = sb("ff", [P, 2, T], at=st1)
        st1.close()
        st1 = ExitStack()
        xin = sb("xin", [P, LT, CONV - 1 + T], at=st1)
        gl = sb("gl", [P, LT, T], at=st1)
        q2T = sb("q2T", [P, 5, T], at=st1)
        v2 = sb("v2", [P, TT, P], at=st1)
        xc = sb("xc", [P, LT, T], at=st1)
        gr = sb("gr", [P, LT, T], at=st1)
        gi = sb("gi", [P, LT, T], at=st1)
        la = sb("la", [P, LT, T], at=st1)
        th = sb("th", [P, LT, T], at=st1)
        hs = sb("hs", [P, LT, T], at=st1)
        bd = sb("bd", [P, 2, LT, P], at=st1)
        cols = sb("cols", [P, 9, LT], at=st1)
        lsg = sb("lsg", [P, 6, LT], at=st1)
        ones = sb("ones", [P, P], at=st1)
        m2 = sb("m2", [P, T], at=st1)
        sinkb = sb("sinkb", [P, 4, 2], at=st1)
        o2 = sb("o2", [P, TT, 4, P], at=st1)
        wv = sb("wv", [P, T], at=st1)
        wi_ = sb("wi_", [P, T], I32, at=st1)
        wa_ = sb("wa_", [P, T], at=st1)
        wb_ = sb("wb_", [P, T], at=st1)
        wr_ = sb("wr_", [P, T], at=st1)
        s2_sb = sb("s2_sb", [P, 2, 2, T], at=st1)
        p2_sb = sb("p2_sb", [P, 2, 2, T], at=st1)
        p2T = sb("p2T", [P, 2, 4, P], at=st1)
        smx2 = sb("smx2", [P, 2, 2], at=st1)
        es2 = sb("es2", [P, 2, 2], at=st1)
        rs2 = sb("rs2", [P, 2, 2], at=st1)
        rr2 = sb("rr2", [P, 4, 2], at=st1)
        nsink = sb("nsink", [P, 4, 2], at=st1)
        st1.close()
        st.close()

        hidden = nc.dram_tensor("hidden", (NKEY // 2, P, 2 * T), F32, kind="Internal").ap()

        acc = ctx.enter_context(nc.psum_tensor("acc", [P, 4, 512], F32))
        ub = ctx.enter_context(nc.psum_tensor("ub", [P, 2, 512], F32))
        mb = ctx.enter_context(nc.psum_tensor("mb", [P, 2, 512], F32))

        raw_in = [sem(f"raw_in{k}") for k in range(RAW)]
        w_high = sem("w_high")
        w_low = sem("w_low")
        c_done = sem("c_done")
        u_free = sem("u_free")
        c_read = sem("c_read")
        t_in = sem("t_in")
        t_ps = sem("t_ps")
        t_high = sem("t_high")
        t_low = sem("t_low")
        wb_in = [sem(f"wb_in{k}") for k in range(2)]
        wb_used = sem("wb_used")
        x_in = sem("x_in")
        x_out = sem("x_out")
        r_ok = sem("r_ok")
        sq_ok = sem("sq_ok")
        half_ok = sem("half_ok")
        rs_ok = sem("rs_ok")
        consts = sem("consts")
        par1 = sem("par1")
        rb_in = sem("rb_in")
        rb_ok = sem("rb_ok")
        keys_in = sem("keys_in")
        keys_go = sem("keys_go")
        par2 = sem("par2")
        par2_go = sem("par2_go")
        dve = sem("dve")
        at_sc = sem("at_sc")
        at_b = sem("at_b")
        at_sk = sem("at_sk")
        nd_ok = sem("nd_ok")
        nh_ok = sem("nh_ok")
        at_ex = sem("at_ex")
        at_a = sem("at_a")
        at_t = sem("at_t")
        at_v = sem("at_v")
        at_o = sem("at_o")
        at_d = sem("at_d")
        gate_ok = sem("gate_ok")
        lam_s = sem("lam_s")
        lam_e = sem("lam_e")
        bt_done = sem("bt_done")
        sk_ps = sem("sk_ps")
        sk_sb = sem("sk_sb")
        tk_x = sem("tk_x")
        tk_e = sem("tk_e")
        ix_in = sem("ix_in")
        ix_ps = sem("ix_ps")
        ix_sb = sem("ix_sb")
        ix_l = sem("ix_l")
        iota_ok = sem("iota_ok")
        spill = [sem(f"spill{k}") for k in range(4)]
        fetch = [sem(f"fetch{k}") for k in range(4)]
        pool_go = sem("pool_go")
        g_eq = sem("g_eq")
        g_two = sem("g_two")
        g_ps = sem("g_ps")
        g_sb = sem("g_sb")
        pool_c = sem("pool_c")
        hd_g = sem("hd_g")
        hd_m = sem("hd_m")
        a_h = sem("a_h")
        a_l = sem("a_l")
        f_s = sem("f_s")
        f_f = sem("f_f")
        f_l = sem("f_l")
        v2_sb = sem("v2_sb")
        x2_sb = sem("x2_sb")
        ls_z = sem("ls_z")
        ls_e = sem("ls_e")
        xc_ok = sem("xc_ok")
        rg_ps = sem("rg_ps")
        rg_sb = sem("rg_sb")
        la_ok = sem("la_ok")
        la_e = sem("la_e")
        m2_ok = sem("m2_ok")
        mu_ok = sem("mu_ok")
        yq_ok = sem("yq_ok")
        ss_ps = sem("ss_ps")
        yl_ok = sem("yl_ok")

        def groups_at(i, j):
            if isinstance(i, int):
                return range(4 * j, 4 * j + 4) if j < 2 else ()
            return range(2 * j, 2 * j + 2)

        block = ctx.enter_context(nc.Block())

        @block.sync
        def _(sp):
            stream = A["wstream"]
            sp.dma_start(resid[:, :, :], A["x"].rearrange("(a p) d -> p a d", p=P)).then_inc(x_in, 16)
            for c in range(RAW):
                sp.dma_start(raw[:, c, :], stream[c]).then_inc(raw_in[c % RAW], 16)

            def load(c, slot):
                sp.wait_ge(w_low, c - RAW + 1)
                sp.dma_start(raw[:, slot, :],
                             stream[bass.ds(c, 1)].rearrange("a p n -> p (a n)")).then_inc(raw_in[slot], 16)

            pairs = (NCH - RAW) // 2
            with sp.Fori(0, pairs) as i:
                for j in range(2):
                    load(i * 2 + (RAW + j), j)
            for c in range(RAW + 2 * pairs, NCH):
                load(c, c % RAW)
            for tt in range(TT):
                sp.wait_ge(r_ok, LAST_R + tt + 1)
                sp.dma_start(out[tt * P:tt * P + P, :], resid[:, tt, :]).then_inc(x_out, 16)
            sp.wait_ge(x_out, 32)

        @block.gpsimd
        def _(pool):
            def load_wb(n):
                if n >= 2:
                    pool.wait_ge(wb_used, n - 1)
                a = A[NORMS[n]]
                w = a.shape[1]
                pool.dma_start(wb[:, n % 2, 0:w], a.to_broadcast([P, w])).then_inc(wb_in[n % 2], 16)

            load_wb(0)
            load_wb(1)
            pool.memset(ident[:, :], 0.0).then_inc(pool_c, 1)
            pool.iota(iota[:, :], [[1, NKEY]], base=0, channel_multiplier=0,
                      allow_small_or_imprecise_dtypes=True).then_inc(consts, 1)
            pool.iota(ndi[:, :], [[1, T]], base=-P, channel_multiplier=-1,
                      allow_small_or_imprecise_dtypes=True).then_inc(consts, 1)
            pool.wait_ge(pool_c, 1)
            pool.affine_select(out=ident[:, :], in_=ident[:, :], compare_op=ALU.not_equal, fill=1.0,
                               base=0, pattern=[[-1, P]], channel_multiplier=1).then_inc(consts, 1)
            pool.dma_start(lq[:, :, :], A["lq"].to_broadcast([P, 4 * SUB])
                           .rearrange("p (a b) -> p a b", a=4)).then_inc(par1, 16)
            pool.dma_start(subw[:, :], A["subln"].to_broadcast([P, P])).then_inc(par1, 16)
            pool.dma_start(bgate[:, :], A["b_gate"]).then_inc(par1, 16)
            pool.dma_start(rb[:, :, :], A["rel"]).then_inc(rb_in, 16)
            pool.wait_ge(rb_in, 16)
            pool.tensor_scalar(rb[:, :, :], rb[:, :, :], 8.0, None, ALU.mult).then_inc(pool_c, 1)
            pool.wait_ge(pool_c, 2)
            pool.memset(rb[0:SUB, :, T - SUB:T], MASKED).then_inc(rb_ok, 1)
            load_wb(2)
            pool.wait_ge(nd_ok, 1)
            for h in range(HEADS):
                if h >= 2:
                    pool.wait_ge(at_b, 2 * h - 2)
                pool.tensor_scalar(ndh[:, h % 2, :], nd[:, :], 2.0 ** -(h + 1), None, ALU.mult
                                   ).then_inc(nh_ok, 1)
            pool.wait_ge(keys_go, 1)
            pool.dma_start(keysT[:, :, :], A["keys"]).then_inc(keys_in, 16)

            pool.tensor_copy(iota8[:, :, :], iota[:, :, None].to_broadcast([P, NKEY, GT])
                             ).then_inc(iota_ok, 1)

            def store(n, k):
                pool.wait_ge(hd_g, n + 1)
                pool.sem_inc(pool_go, 1)
                pool.dma_start(hidden[bass.ds(n + 4, 1)].rearrange("a p n -> p (a n)"),
                               hid[:, k, :, :].rearrange("p a b -> p (a b)")).then_inc(spill[k], 16)

            def load(n, k):
                pool.wait_ge(a_l, n - 3)
                pool.sem_inc(pool_go, 1)
                pool.dma_start(hid[:, k, :, :].rearrange("p a b -> p (a b)"),
                               hidden[bass.ds(n, 1)].rearrange("a p n -> p (a n)")).then_inc(fetch[k], 16)

            with pool.Fori(0, 15) as i:
                for k in range(4):
                    store(i * 4 + k, k)

            def gated(n, k, mp):
                if not isinstance(n, int) or n >= 4:
                    pool.wait_ge(fetch[k], (n - k) * 4)
                    pool.sem_inc(pool_go, 1)
                pool.tensor_tensor(hid[:, k, :, :], hid[:, k, :, :], G[:, mp, :], ALU.mult
                                   ).then_inc(hd_m, 1)

            for k in range(4):
                pool.wait_ge(spill[k], 15 * 16)
            pool.wait_ge(g_sb, GROUPS)
            pool.wait_ge(hd_g, 64)
            gated(0, 0, slice(0, 2))
            gated(1, 1, slice(2, 4))

            def value_step(q, i, j):
                n = i * 4 + (16 * q + j)
                if not (isinstance(n, int) and n + 4 >= 64):
                    load(n + 4, j)
                if isinstance(n, int):
                    if n + 2 < 64:
                        if (n + 2) % 16 == 0:
                            pool.wait_ge(g_sb, GROUPS * ((n + 2) // 16 + 1))
                        mp = (n + 2) % 32
                        gated(n + 2, (j + 2) % 4, slice(2 * mp, 2 * mp + 2))
                else:
                    gated(n + 2, (j + 2) % 4, bass.ds(i * 8 + (2 * (16 * (q % 2) + j + 2)), 2))

            for q in range(QG):
                if q == 0:
                    for j in range(4):
                        value_step(0, 0, j)
                with pool.Fori(1 if q == 0 else 0, 3) as i:
                    for j in range(4):
                        value_step(q, i, j)
                for j in range(4):
                    value_step(q, 3, j)

            for n in range(3, 6):
                load_wb(n)
            pool.wait_ge(par2_go, 1)
            pool.memset(xin[:, :, 0:CONV - 1], 0.0).then_inc(x2_sb, 1)
            pool.memset(ones[:, :], 1.0).then_inc(x2_sb, 1)
            pool.memset(bd[:, :, :, :], 0.0).then_inc(pool_c, 1)
            pool.memset(m2[:, :], 0.0).then_inc(pool_c, 1)
            pool.dma_start(cols[:, :, :], A["cols"]).then_inc(par2, 16)
            pool.dma_start(sinkb[:, :, :], A["sinks"].to_broadcast([P, 8])
                           .rearrange("p (a b) -> p a b", a=4)).then_inc(par2, 16)
            pool.wait_ge(pool_c, 2 + 2)
            for g, name in enumerate(("w_rg", "w_ig")):
                for r in range(2):
                    pool.dma_start(bd[SUB * r:SUB * r + SUB, g, :, SUB * r:SUB * r + SUB],
                                   A[name][r]).then_inc(par2, 16)
            pool.affine_select(out=m2[:, :], in_=m2[:, :], compare_op=ALU.is_ge, fill=MASKED,
                               base=P, pattern=[[-1, T]], channel_multiplier=1).then_inc(pool_c, 1)
            pool.wait_ge(pool_c, 2 + 3)
            pool.affine_select(out=m2[:, :], in_=m2[:, :], compare_op=ALU.is_gt, fill=MASKED,
                               base=0, pattern=[[1, T]], channel_multiplier=-1).then_inc(x2_sb, 1)
            for n in range(6, len(NORMS)):
                load_wb(n)

        @block.scalar
        def _(act):
            def split(c, slot):
                act.wait_ge(raw_in[slot % RAW], arrived(c, slot))
                if not isinstance(c, int) or c >= RING:
                    act.wait_ge(c_done, c - RING + 1)
                act.copy(wh[:, slot, :], raw[:, slot % RAW, :]).then_inc(w_high, 1)

            def arrived(c, slot):
                return ((c - slot % RAW) // RAW) * 16 + 16 if isinstance(c, int) else \
                    (c - slot % RAW) * (16 // RAW) + 16

            def ahead(c):
                if isinstance(c, int) and c + AHEAD < NCH:
                    split(c + AHEAD, (c + AHEAD) % RING)

            def ahead_at(c, cmod):
                split(c + AHEAD, (cmod + AHEAD) % RING)

            nt = [0]

            def transposed(dh, dl, tiles, to=0, bank=acc):
                for g in range(tiles // 2):
                    act.wait_ge(t_ps, nt[0] + 1)
                    act.copy(dh[:, to + 2 * g:to + 2 * g + 2, :],
                             bank[:, g, :].rearrange("p (a b) -> p a b", a=2)).then_inc(t_high, 1)
                    nt[0] += 1

            def read_acc(dst, stage, banks=4):
                act.wait_ge(c_done, CH[stage] + dict(_sizes)[stage])
                for b in range(banks):
                    tt, nb = (b // 2, b % 2) if banks == 4 else (b, 0)
                    last = act.copy(dst[:, tt, nb * 512:nb * 512 + 512], acc[:, b, :])
                last.then_inc(c_read, 1)

            nsq, nr, nrs = [0], [0], [0]

            halves = [0]

            def squares(src_of, scratch, ready=True, nh=None):
                for tt in range(TT):
                    if ready:
                        nr[0] += 1
                        act.wait_ge(r_ok, nr[0])
                    if not ready and tt == 1 and nh is not None:
                        nh[0] += 1
                        act.wait_ge(half_ok, nh[0])
                    if nsq[0]:
                        act.wait_ge(sq_ok, nsq[0])
                    act.activation(scratch[:, :], src_of(tt), ACT.Square, accum_out=ssq[:, tt:tt + 1]
                                   ).then_inc(sq_ok, 1)
                    nsq[0] += 1

            def resid_of(tt):
                return resid[:, tt, :]

            def acc_of(tt):
                return acc[:, 2 * tt:2 * tt + 2, :].rearrange("p a b -> p (a b)")

            def scaled(dst):
                nrs[0] += 1
                act.wait_ge(rs_ok, nrs[0])
                act.activation(dst[:, 1, :], dst[:, 1, :], ACT.Copy, scale=rstd[:, 1:2]).then_inc(t_in, 1)

            act.wait_ge(x_in, 16)
            squares(resid_of, junk, ready=False)
            for c in range(AHEAD - 1):
                split(c, c)
            scaled(y)
            transposed(xh, xl, KD)
            split(AHEAD - 1, AHEAD - 1)
            for j in range(4):
                ahead(j)
                act.wait_ge(c_done, j + 1)
                act.copy(qkT[:, 2 * j:2 * j + 2, :],
                         ub[:, j % 2, :].rearrange("p (a b) -> p a b", a=2)).then_inc(u_free, 1)
            with act.Fori(1, 3) as i:
                for j in range(4):
                    ahead_at(i * 4 + j, j)
                    act.wait_ge(c_done, i * 4 + (j + 1))
                    act.copy(qkT[:, bass.ds(i * 8 + 2 * j, 2), :],
                             ub[:, j % 2, :].rearrange("p (a b) -> p a b", a=2)).then_inc(u_free, 1)
            for c in range(CH["vd"], CH["vd"] + 4):
                ahead(c)
            read_acc(vd, "vd")
            for c in range(CH["vc"], CH["vc"] + 2):
                ahead(c)
            read_acc(vc, "vc", banks=2)
            act.wait_ge(par1, 48)
            act.wait_ge(lam_s, 2)
            act.activation(lams[:, 2:4], lams[:, 0:2], ACT.Exp).then_inc(lam_e, 1)

            def attention(count, n0, sb_, pb_, pt_, mx_, r_, rr_, blocks_of, out_of, sink=False, beside=None):
                def exps(n):
                    b = n % 2
                    nk = P * (1 + b)
                    act.wait_ge(at_b, n0 + n + 1)
                    for r in range(2):
                        act.activation(pb_[:, b, r, 0:nk], sb_[:, b, r, 0:nk], ACT.Exp,
                                       bias=mx_[:, b, r:r + 1], scale=-1.0,
                                       accum_out=r_[:, b, r:r + 1]).then_inc(at_ex, 1)
                    if sink:
                        for r in range(2):
                            act.activation(es2[:, b, r:r + 1], sinkb[:, n // 2, r:r + 1], ACT.Exp,
                                           bias=mx_[:, b, r:r + 1]).then_inc(at_sk, 1)

                def turn(n):
                    b = n % 2
                    act.wait_ge(at_t, n0 + n + 1)
                    if n >= 2:
                        act.wait_ge(at_o, n0 + n - 1)
                    w = blocks_of(n)
                    act.copy(pt_[:, b, 0:w, :], mb[:, 0, 0:w * P].rearrange("p (a b) -> p a b", a=w)
                             ).then_inc(at_v, 1)

                def output(n):
                    act.wait_ge(at_o, n0 + n + 1)
                    parts, dst = out_of(n)
                    w = P // parts
                    for r in range(parts):
                        last = act.activation(dst[:, r * w:r * w + w], (mb, ub)[n % 2][:, 1, r * w:r * w + w],
                                              ACT.Copy, scale=rr_[:, n % 4, r:r + 1])
                    last.then_inc(at_d, 1)

                for n in range(count):
                    exps(n)
                    if n >= 2:
                        output(n - 2)
                    if n >= 1:
                        turn(n - 1)
                    if beside is not None:
                        beside(n)
                output(count - 2)
                turn(count - 1)
                output(count - 1)

            def gates_beside(n):
                if n % 3 == 2:
                    g = n // 3
                    ahead(CH["gate"] + g)
                    act.wait_ge(c_done, CH["gate"] + g + 1)
                    for k in range(2):
                        last = act.activation(gate[:, 2 * g + k, :], ub[:, 0, k * T:k * T + T],
                                              ACT.Identity, bias=bgate[:, 2 * g + k:2 * g + k + 1])
                    last.then_inc(u_free, 1)

            attention(24, 0, s_sb, p_sb, pT, smx, rs, rr, lambda n: (1 if n < 16 else 2) * (1 + n % 2),
                      lambda n: (1, y[:, n % 2, n // 2 * P:n // 2 * P + P]) if n < 16 else
                      (2, oc[:, n % 2, (n - 16) // 2, :]), beside=gates_beside)
            act.wait_ge(u_free, 2 + UN["bd"])
            act.activation(gate[:, :, :], gate[:, :, :], ACT.Sigmoid).then_inc(gate_ok, 1)
            transposed(odh, odl, KD)
            transposed(och, ocl, 4)
            for c in range(CH["bd"], CH["bd"] + 6 + 4):
                ahead(c)
            squares(resid_of, junk)
            scaled(y)
            transposed(xh, xl, KD)
            for u in range(4):
                ahead(CH["wq"] + u)
                act.wait_ge(c_done, CH["wq"] + u + 1)
                act.copy(pqT[:, 2 * u:2 * u + 2, :],
                         ub[:, (UN["wq"] + u) % 2, :].rearrange("p (a b) -> p a b", a=2)).then_inc(u_free, 1)
            for n in range(4):
                tt, k = n // 2, n % 2
                act.wait_ge(sk_ps, n + 1)
                for s in range(2):
                    last = act.copy(sc12[:, tt, 4 * k:4 * k + 4, s, :],
                                    acc[:, 2 * k + s, :].rearrange("p (a b) -> p a b", a=4))
                last.then_inc(sk_sb, 1)

            CU, CV = CH["pu"], CH["pv"]

            def hidden_step(n, nmod):
                ahead_at(n + CU, CU + nmod)
                act.wait_ge(c_done, n + (CU + 1))
                if not isinstance(n, int) or n >= 4:
                    act.wait_ge(spill[nmod % 4], (n - nmod % 4) * 4)
                act.activation(hid[:, nmod % 4, :, :].rearrange("p a b -> p (a b)"), ub[:, nmod % 2, :],
                               ACT.Gelu).then_inc(hd_g, 1)

            for n in range(TOPK_U):
                hidden_step(n, n)
                for tt in range(TT):
                    if n == 16 * tt + 12:
                        act.wait_ge(tk_x, tt + 1)
                        act.activation(gate_t[:, :, :], gate_t[:, :, :], ACT.Exp).then_inc(tk_e, 1)
                    if n == min(16 * tt + 17, TOPK_U - 1):
                        act.wait_ge(ix_ps, tt + 1)
                        for k, dst in enumerate((i1T, i2T)):
                            act.copy(dst[:, tt * P:tt * P + P], mb[:, tt, k * P:k * P + P])
                        act.copy(gT[:, 0, tt * P:tt * P + P], mb[:, tt, 2 * P:3 * P]).then_inc(ix_sb, 1)

            def spread(n, b, tok, qb):
                act.wait_ge(g_ps, n + 1)
                act.copy(G[:, qb * QW:qb * QW + QW, tok],
                         mb[:, b, 0:GT * QW].rearrange("p (t i) -> p i t", i=QW)).then_inc(g_sb, 1)

            for q in range(2):
                with act.Fori(0, 4) as i:
                    for j in range(4):
                        hidden_step(i * 4 + (TOPK_U + 16 * q + j), j)
                        for g in range(2):
                            spread(i * 8 + (GROUPS * q + 2 * j + g), g,
                                   bass.ds(i * (8 * GT) + (2 * j + g) * GT, GT), q)

            def high_step(n, nmod):
                act.wait_ge(hd_m, n + 1)
                if not isinstance(n, int) or n >= 2:
                    act.wait_ge(c_done, n + (CV - 1))
                act.copy(ah[:, nmod % 2, :, :], hid[:, nmod % 4, :, :]).then_inc(a_h, 1)

            high_step(0, 0)

            def value_step(q, i, j):
                n = i * 4 + (16 * q + j)
                if not (isinstance(n, int) and n == 63):
                    high_step(n + 1, j + 1)
                ahead_at(n + CV, CV + j)
                if q in (1, 2):
                    for g in groups_at(i, j):
                        spread(i * 8 + (GROUPS * (q + 1) + g), g % 2,
                               bass.ds(i * (8 * GT) + g * GT, GT), (q + 1) % 2)

            for q in range(QG):
                if q in (1, 2):
                    act.wait_ge(hd_m, 16 * q)
                with act.Fori(0, 3) as i:
                    for j in range(4):
                        value_step(q, i, j)
                for j in range(4):
                    value_step(q, 3, j)
            squares(resid_of, junk_again)

            def ffn(gu, dn, nf):
                squares(resid_of, junk_again)
                scaled(y_again)
                transposed(xh, xl, KD)
                C, U = CH[gu], UN[gu]

                def hidden(c, cmod, u, umod, n, b):
                    ahead_at(c, cmod)
                    act.wait_ge(c_done, c + 1)
                    if not isinstance(n, int) or n >= 2:
                        act.wait_ge(f_f, n - 1)
                    act.activation(fs[:, b, :], ub[:, umod % 2, 0:T], ACT.Silu).then_inc(f_s, 1)

                for j in range(2):
                    hidden(C + j, C + j, U + j, U + j, nf + j, j % 2)
                with act.Fori(0, 5) as i:
                    for j in range(2, 6):
                        hidden(i * 4 + (C + j), C + j, i * 4 + (U + j), U + j, i * 4 + (nf + j), j % 2)
                for c in range(CH[dn], CH[dn] + 11):
                    ahead(c)
                act.wait_ge(c_done, CH[dn] + 11)
                squares(acc_of, junk_again, ready=False, nh=halves)

            ffn("gu1", "dn1", 0)
            squares(resid_of, junk_again)
            scaled(y_again)
            transposed(xh, xl, KD)
            act.wait_ge(x2_sb, 3)
            for u in range(7):
                ahead(CH["in2"] + u)
                act.wait_ge(c_done, CH["in2"] + u + 1)
                b = (UN["in2"] + u) % 2
                src = ub[:, b, :].rearrange("p (a b) -> p a b", a=2)
                if u < 2:
                    act.copy(xin[:, 2 * u:2 * u + 2, CONV - 1:], src).then_inc(u_free, 1)
                elif u < 4:
                    act.activation(gl[:, 2 * u - 4:2 * u - 2, :], src, ACT.Gelu_apprx_tanh).then_inc(u_free, 1)
                elif u < 6:
                    act.copy(q2T[:, 2 * u - 8:2 * u - 6, :], src).then_inc(u_free, 1)
                else:
                    act.copy(q2T[:, 4, :], src[:, 0, :]).then_inc(u_free, 1)
                if u == 2:
                    act.wait_ge(ls_z, 1)
                    act.activation(lsg[:, 1, :], lsg[:, 0, :], ACT.Exp).then_inc(ls_e, 1)
                if u == 4:
                    act.wait_ge(ls_z, 2)
                    act.activation(lsg[:, 3, :], lsg[:, 2, :], ACT.Ln).then_inc(ls_e, 1)
            act.copy(v2[:, :, :], mb[:, :, 0:P]).then_inc(v2_sb, 1)
            act.wait_ge(par2, 96)
            for t in range(LT):
                act.wait_ge(rg_ps, t + 1)
                src = (ub, mb)[t // 2][:, t % 2, :]
                act.activation(gr[:, t, :], src[:, 0:T], ACT.Sigmoid, bias=cols[:, 5, t:t + 1])
                act.activation(gi[:, t, :], src[:, T:2 * T], ACT.Sigmoid, bias=cols[:, 6, t:t + 1]
                               ).then_inc(rg_sb, 1)

            def lru_beside(n):
                if n == 0:
                    act.wait_ge(la_ok, 1)
                    act.activation(th[:, :, :], la[:, :, :], ACT.Tanh).then_inc(la_e, 1)
                    act.activation(la[:, :, :], la[:, :, :], ACT.Exp).then_inc(la_e, 1)
                if n == 3:
                    act.wait_ge(m2_ok, 1)
                    act.activation(th[:, :, :], th[:, :, :], ACT.Sqrt, scale=-1.0).then_inc(mu_ok, 1)

            attention(8, 24, s2_sb, p2_sb, p2T, smx2, rs2, rr2, lambda n: 2 * (1 + n % 2),
                      lambda n: (2, o2[:, n % 2, n // 2, :]), sink=True, beside=lru_beside)
            ahead(CH["wo"])
            transposed(xh, xl, 4, to=4, bank=ub)
            for c in range(CH["wo"] + 1, CH["wo"] + 4):
                ahead(c)
            act.wait_ge(c_done, CH["wo"] + 4)
            squares(acc_of, junk_again, ready=False, nh=halves)
            ffn("gu2", "dn2", 22)

        @block.vector
        def _(v):
            steps = [0]

            def link(ins):
                steps[0] += 1
                ins.then_inc(dve, 1)
                v.wait_ge(dve, steps[0])

            def low(c, slot):
                v.wait_ge(w_high, c + 1)
                v.tensor_tensor(wl[:, slot, :], raw[:, slot % RAW, :], wh[:, slot, :].bitcast(F32),
                                ALU.subtract).then_inc(w_low, 1)

            def ahead(c):
                if c + AHEAD < NCH:
                    low(c + AHEAD, (c + AHEAD) % RING)

            def ahead_at(c, cmod):
                low(c + AHEAD, (cmod + AHEAD) % RING)

            def rsqrt(dst, src, ti, ta, tb):
                link(v.tensor_scalar(ti, src.bitcast(I32), 1, None, ALU.logical_shift_right))
                link(v.tensor_scalar(dst.bitcast(I32), ti, -1.0, float(0x5F3759DF), ALU.mult, ALU.add))
                for _ in range(3):
                    link(v.tensor_tensor(ta, dst, dst, ALU.mult))
                    link(v.scalar_tensor_tensor(tb, ta, -0.5, src, ALU.mult, ALU.mult))
                    link(v.scalar_tensor_tensor(dst, tb, 1.5, dst, ALU.add, ALU.mult))

            nwb = [0]

            def rms(src, dst, scratch, factor=1.0, width=D):
                for tt in range(TT):
                    ins = v.tensor_tensor_reduce(scratch, src[:, tt, :], src[:, tt, :], 1.0, 0.0,
                                                 ALU.mult, ALU.add, ssq[:, tt:tt + 1])
                    link(ins)
                link(v.tensor_scalar(var[:, :], ssq[:, :], 1.0 / width, EPS, ALU.mult, ALU.add))
                rsqrt(rstd[:, :], var[:, :], nw_i[:, :], nw_a[:, :], nw_b[:, :])
                if factor != 1.0:
                    link(v.tensor_scalar(rstd[:, :], rstd[:, :], factor, None, ALU.mult))
                n = nwb[0]
                nwb[0] += 1
                v.wait_ge(wb_in[n % 2], 16 * (n // 2 + 1))
                for tt in range(TT):
                    last = v.scalar_tensor_tensor(dst[:, tt, :], src[:, tt, :], rstd[:, tt:tt + 1],
                                                  wb[:, n % 2, 0:width], ALU.mult, ALU.mult)
                    if tt == 0:
                        link(last)
                last.then_inc(wb_used, 1)
                v.wait_ge(wb_used, n + 1)

            nt = [0]

            def go_transpose():
                v.engine_nop().then_inc(t_in, 2)

            nsq = [0]

            def weighted(src_of, dst, banks=False):
                n = nwb[0]
                nwb[0] += 1
                v.wait_ge(wb_in[n % 2], 16 * (n // 2 + 1))
                if banks:
                    v.tensor_tensor(dst[:, 1, :], src_of(1), wb[:, n % 2, :], ALU.mult).then_inc(half_ok, 1)
                    v.wait_ge(sq_ok, nsq[0] + 1)
                    last = v.tensor_tensor(dst[:, 0, :], src_of(0), wb[:, n % 2, :], ALU.mult)
                else:
                    for tt in range(TT):
                        last = v.tensor_tensor(dst[:, tt, :], src_of(tt), wb[:, n % 2, :], ALU.mult)
                last.then_inc(wb_used, 1)
                nsq[0] += 2
                v.wait_ge(sq_ok, nsq[0])
                link(v.tensor_scalar(var[:, :], ssq[:, :], 1.0 / D, EPS, ALU.mult, ALU.add))
                rsqrt(rstd[:, :], var[:, :], nw_i[:, :], nw_a[:, :], nw_b[:, :])
                v.wait_ge(wb_used, n + 1)

            def resid_of(tt):
                return resid[:, tt, :]

            def acc_of(tt):
                return acc[:, 2 * tt:2 * tt + 2, :].rearrange("p a b -> p (a b)")

            def norm(dst):
                weighted(resid_of, dst)
                v.engine_nop().then_inc(rs_ok, 1)
                v.tensor_scalar(dst[:, 0, :], dst[:, 0, :], rstd[:, 0:1], None, ALU.mult).then_inc(t_in, 1)

            nr = [0]

            def next_resid(ins):
                nr[0] += 1
                ins.then_inc(r_ok, 1)

            def add_norm(stage, scratch, factor=1.0):
                v.wait_ge(c_done, CH[stage] + dict(_sizes)[stage])
                weighted(acc_of, scratch, banks=True)
                if factor != 1.0:
                    link(v.tensor_scalar(rstd[:, :], rstd[:, :], factor, None, ALU.mult))
                for tt in range(TT):
                    next_resid(v.scalar_tensor_tensor(resid[:, tt, :], scratch[:, tt, :], rstd[:, tt:tt + 1],
                                                      resid[:, tt, :], ALU.mult, ALU.add))
                v.wait_ge(r_ok, nr[0])

            def transposed(dh, dl, tiles, to=0, bank=acc):
                for g in range(tiles // 2):
                    v.wait_ge(t_high, nt[0] + 1)
                    v.tensor_tensor(dl[:, to + 2 * g:to + 2 * g + 2, :],
                                    bank[:, g, :].rearrange("p (a b) -> p a b", a=2),
                                    dh[:, to + 2 * g:to + 2 * g + 2, :].bitcast(F32),
                                    ALU.subtract).then_inc(t_low, 1)
                    nt[0] += 1

            v.wait_ge(x_in, 16)
            norm(y)
            for c in range(AHEAD - 1):
                low(c, c)
            v.wait_ge(consts, 3)
            link(v.scalar_tensor_tensor(nd[:, :], ndi[:, :], -1.0, ndi[:, :], ALU.mult, ALU.min))
            link(v.tensor_scalar(nd[:, :], nd[:, :], 8.0, None, ALU.mult))
            v.memset(nd[0:SUB, T - SUB:T], MASKED).then_inc(nd_ok, 1)
            v.wait_ge(par1, 48)
            for k in range(2):
                link(v.tensor_tensor_reduce(lqj[:, :], lq[:, 2 * k, :], lq[:, 2 * k + 1, :], 1.0, 0.0,
                                            ALU.mult, ALU.add, lams[:, k:k + 1]))
            v.engine_nop().then_inc(lam_s, 2)
            transposed(xh, xl, KD)
            low(AHEAD - 1, AHEAD - 1)
            with v.Fori(0, 3) as i:
                for j in range(4):
                    ahead_at(i * 4 + j, j)
            for c in range(CH["vd"], CH["gate"]):
                ahead(c)
            v.wait_ge(lam_e, 1)
            link(v.tensor_tensor(lams[:, 4:5], lams[:, 3:4], lams[:, 2:3], ALU.subtract))
            link(v.tensor_scalar(lams[:, 5:6], lams[:, 4:5], -LAM_INIT, None, ALU.add))
            v.wait_ge(rb_ok, 1)

            def biased(n, n0, dst, bias_of, mx_, start_of):
                b, nk = n % 2, P * (1 + n % 2)
                v.wait_ge(at_sc, n0 + n + 1)
                for r in range(2):
                    last = v.tensor_tensor_reduce(dst[:, b, r, 0:nk], acc[:, 2 * b + r, 0:nk],
                                                  bias_of(n, r)[:, T - nk:T], -0.125, start_of(n, r),
                                                  ALU.add, ALU.min, mx_[:, b, r:r + 1])
                last.then_inc(at_b, 1)

            def first_bias(n):
                if n < 16:
                    v.wait_ge(nh_ok, n // 2 + 1)
                biased(n, 0, s_sb, lambda n, r: ndh[:, n // 2 % 2, :] if n < 16 else rb[:, 2 * (n // 2 - 8) + r, :],
                       smx, lambda n, r: 3.0e38)

            def first_weights(n):
                b, nk = n % 2, P * (1 + n % 2)
                v.wait_ge(at_ex, 2 * n + 2)
                if n >= 4:
                    v.wait_ge(at_d, n - 3)
                if n < 16:
                    link(v.reciprocal(rr[:, n % 4, :], rs[:, b, :]))
                    link(v.scalar_tensor_tensor(rc[:, b:b + 1], rr[:, n % 4, 1:2], rs[:, b, 0:1],
                                                lams[:, 5:6], ALU.mult, ALU.mult))
                    v.scalar_tensor_tensor(p_sb[:, b, 0, 0:nk], p_sb[:, b, 1, 0:nk], rc[:, b:b + 1],
                                           p_sb[:, b, 0, 0:nk], ALU.mult, ALU.add).then_inc(at_a, 1)
                else:
                    v.reciprocal(rr[:, n % 4, :], rs[:, b, :]).then_inc(at_a, 1)

            def heads_norm(n):
                if n in (18, 19):
                    tt = n - 18
                    if tt == 0:
                        v.wait_ge(at_d, 16)
                    for h in range(HEADS):
                        o = y[:, tt, h * P:h * P + P]
                        ins = v.tensor_tensor_reduce(junk[:, h * P:h * P + P], o, o, 1.0, 0.0, ALU.mult, ALU.add,
                                                     sso[:, tt * 8 + h:tt * 8 + h + 1])
                    link(ins)
                elif n == 20:
                    link(v.tensor_scalar(so[1][:, :], sso[:, :], 1.0 / P, EPS, ALU.mult, ALU.add))
                    rsqrt(so[2][:, :], so[1][:, :], so[0][:, :], so[3][:, :], so[4][:, :])
                    link(v.tensor_scalar(so[2][:, :], so[2][:, :], 1.0 - LAM_INIT, None, ALU.mult))
                elif n in (21, 22):
                    tt = n - 21
                    for h in range(HEADS):
                        o = y[:, tt, h * P:h * P + P]
                        ins = v.scalar_tensor_tensor(o, o, so[2][:, tt * 8 + h:tt * 8 + h + 1], subw[:, :],
                                                     ALU.mult, ALU.mult)
                    ins.then_inc(t_in, 1)

            first_bias(0)
            for n in range(24):
                if n + 1 < 24:
                    first_bias(n + 1)
                first_weights(n)
                if n % 3 == 2:
                    ahead(CH["gate"] + n // 3)
                heads_norm(n)
            v.wait_ge(at_d, 24)
            go_transpose()
            transposed(odh, odl, KD)
            transposed(och, ocl, 4)
            mg = y[:, :, :].rearrange("p a (b c) -> p (a b) c", c=T)
            v.wait_ge(t_low, 4 + 4 + 2)
            v.wait_ge(gate_ok, 1)
            for u in range(4):
                ahead(CH["bd"] + u)
                n = UN["bd"] + u
                v.wait_ge(c_done, CH["bd"] + u + 1)
                v.tensor_tensor(mg[:, 2 * u:2 * u + 2, :], ub[:, n % 2, :].rearrange("p (a b) -> p a b", a=2),
                                gate[:, 2 * u:2 * u + 2, :], ALU.mult).then_inc(u_free, 1)
            for u in range(4):
                if u % 2 == 0:
                    ahead(CH["bc"] + u // 2)
                n = UN["bc"] + u
                v.wait_ge(c_done, CH["bc"] + u // 2 + 1)
                gslice = gate[:, 8 + 2 * u:10 + 2 * u, :]
                v.tensor_tensor(gslice, ub[:, n % 2, :].rearrange("p (a b) -> p a b", a=2),
                                gslice, ALU.mult).then_inc(u_free, 1)
                v.wait_ge(u_free, 2 + n + 1)
                m = mg[:, 2 * u:2 * u + 2, :]
                link(v.tensor_tensor(m, m, gslice, ALU.add))
                link(v.tensor_copy(xh[:, 2 * u:2 * u + 2, :], m))
                v.tensor_tensor(xl[:, 2 * u:2 * u + 2, :], m, xh[:, 2 * u:2 * u + 2, :].bitcast(F32),
                                ALU.subtract).then_inc(bt_done, 1)
            v.wait_ge(bt_done, 4)
            v.engine_nop().then_inc(keys_go, 1)
            for c in range(CH["out"], CH["out"] + 4):
                ahead(c)

            def add_acc(stage):
                v.wait_ge(c_done, CH[stage] + dict(_sizes)[stage])
                for tt in range(TT):
                    next_resid(v.tensor_tensor(resid[:, tt, :], resid[:, tt, :], acc_of(tt), ALU.add))
                v.wait_ge(r_ok, nr[0])

            add_acc("out")
            norm(y)
            transposed(xh, xl, KD)
            for u in range(4):
                ahead(CH["wq"] + u)

            lowest = -3.0e38
            CU, CV = CH["pu"], CH["pv"]
            nu = [0]

            def beside():
                if nu[0] < TOPK_U:
                    ahead(CU + nu[0])
                    nu[0] += 1

            def rest_of_gate(tt):
                v.wait_ge(ix_sb, tt + 1)
                rest, tok = gTr[:, tt * P:tt * P + P], slice(tt * P, tt * P + P)
                link(v.tensor_tensor(rest, mb[:, tt, 2 * P:3 * P], gT[:, 0, tok], ALU.subtract))
                link(v.tensor_copy(gT[:, 1, tok], rest))
                link(v.tensor_tensor(rest, rest, gT[:, 1, tok], ALU.subtract))
                v.tensor_copy(gT[:, 2, tok], rest).then_inc(ix_l, 1)

            for tt in range(TT):
                v.wait_ge(sk_sb, 2 * tt + 2)
                units = [(h, s) for h in range(PEER_H) for s in range(2)]

                def each(items, ops):
                    for k, it in enumerate(items):
                        ins = ops(*it)
                        if k == len(items) - 1:
                            link(ins)
                    beside()

                each(units, lambda h, s: v.max(v16[:, h, s, 0:8], sc12[:, tt, h, s, :]))
                each(units, lambda h, s: v.max_index(i16[:, h, s, 0:8], v16[:, h, s, 0:8], sc12[:, tt, h, s, :]))
                each(units, lambda h, s: v.match_replace(sc_w[:, h, s, :], v16[:, h, s, 0:8],
                                                         sc12[:, tt, h, s, :], lowest))
                each(units, lambda h, s: v.max(v16[:, h, s, 8:16], sc_w[:, h, s, :]))
                each(units, lambda h, s: v.max_index(i16[:, h, s, 8:16], v16[:, h, s, 8:16], sc_w[:, h, s, :]))
                sq = [P, PEER_H, TOPK, TOPK]
                link(v.tensor_tensor(cand[:, :, :].rearrange("p h (a b) -> p h a b", a=TOPK),
                                     v16[:, :, 0, :, None].to_broadcast(sq),
                                     v16[:, :, 1, None, :].to_broadcast(sq), ALU.add))
                beside()
                heads = [(h,) for h in range(PEER_H)]
                each(heads, lambda h: v.max(cv[:, h, 0:8], cand[:, h, :]))
                each(heads, lambda h: v.max_index(ci[:, h, 0:8], cv[:, h, 0:8], cand[:, h, :]))
                each(heads, lambda h: v.match_replace(cand_w[:, h, :], cv[:, h, 0:8], cand[:, h, :], lowest))
                each(heads, lambda h: v.max(cv[:, h, 8:16], cand_w[:, h, :]))
                each(heads, lambda h: v.max_index(ci[:, h, 8:16], cv[:, h, 8:16], cand_w[:, h, :]))
                if tt >= 1:
                    v.wait_ge(ix_ps, tt)
                v.tensor_tensor(gate_t[:, :, :], cv[:, :, :],
                                cv[:, :, 0:1].to_broadcast([P, PEER_H, TOPK]), ALU.subtract).then_inc(tk_x, 1)
                v.tensor_scalar(cab[:, 0, :, :], ci[:, :, :], 4, None, ALU.logical_shift_right)
                link(v.tensor_scalar(cab[:, 1, :, :], ci[:, :, :], TOPK - 1, None, ALU.bitwise_and))
                v.tensor_copy(cabf[:, :, :, :], cab[:, :, :, :])
                link(v.tensor_copy(i16f[:, :, :, :], i16[:, :, :, :]))
                for s in range(2):
                    work = (cand, cand_w)[s][:, :, :].rearrange("p h (a b) -> p h a b", a=TOPK)
                    link(v.tensor_tensor(work, cabf[:, s, :, :, None].to_broadcast(sq),
                                         iota[:, None, None, 0:TOPK].to_broadcast(sq), ALU.is_equal))
                    beside()
                    link(v.tensor_tensor(work, work, i16f[:, :, s, None, :].to_broadcast(sq), ALU.mult))
                    link(v.tensor_reduce(esel[:, s, :].rearrange("p (h k) -> p h k", h=PEER_H), work,
                                         AX.X, ALU.add))
                    beside()
                v.wait_ge(tk_e, tt + 1)
                link(v.tensor_reduce(gsum[:, :], gate_t[:, :, :], AX.X, ALU.add))
                link(v.reciprocal(grec[:, :], gsum[:, :]))
                v.tensor_tensor(gate_t[:, :, :], gate_t[:, :, :],
                                grec[:, :, None].to_broadcast([P, PEER_H, TOPK]), ALU.mult).then_inc(ix_in, 1)
                while nu[0] < 16 * (tt + 1):
                    beside()
            for tt in range(TT):
                rest_of_gate(tt)
            v.wait_ge(ix_l, 2)
            v.wait_ge(iota_ok, 1)

            def onehots(n, b, tok, q):
                if not isinstance(n, int) or n >= 2:
                    v.wait_ge(g_ps, n - 1)
                v.tensor_tensor(one1[:, b, :, :], iota8[:, :, :],
                                i1T[:, tok][:, None, :].to_broadcast([P, NKEY, GT]), ALU.is_equal)
                if not isinstance(n, int) or n >= 1:
                    v.wait_ge(g_two, n)
                v.tensor_tensor(one2[:, :, :], iota8[:, q * QW:q * QW + QW, :],
                                i2T[:, tok][:, None, :].to_broadcast([P, QW, GT]), ALU.is_equal
                                ).then_inc(g_eq, 1)
                v.wait_ge(g_eq, n + 1)
                shape = [P, 3, QW, GT]
                v.tensor_tensor(g2[:, b, :, :, :], one2[:, None, :, :].to_broadcast(shape),
                                gT[:, :, tok][:, :, None, :].to_broadcast(shape), ALU.mult
                                ).then_inc(g_two, 1)

            def gates_step(q, i, j):
                for g in range(2):
                    onehots(i * 8 + (GROUPS * q + 2 * j + g), g,
                            bass.ds(i * (8 * GT) + (2 * j + g) * GT, GT), q)
                ahead_at(i * 4 + (CU + TOPK_U + 16 * q + j), CU + j)

            for j in range(4):
                gates_step(0, 0, j)
            for q in range(2):
                with v.Fori(1 - q, 4) as i:
                    for j in range(4):
                        gates_step(q, i, j)

            def lowpart(n, k):
                v.wait_ge(a_h, n + 1)
                v.tensor_tensor(al[:, k % 2, :, :], hid[:, k % 4, :, :], ah[:, k % 2, :, :].bitcast(F32),
                                ALU.subtract).then_inc(a_l, 1)

            lowpart(0, 0)

            def value_step(q, i, j):
                n = i * 4 + (16 * q + j)
                if not (isinstance(n, int) and n == 63) and not (q in (1, 2) and groups_at(i, j)):
                    lowpart(n + 1, j + 1)
                if q in (1, 2):
                    for g in groups_at(i, j):
                        onehots(i * 8 + (GROUPS * (q + 1) + g), g % 2,
                                bass.ds(i * (8 * GT) + g * GT, GT), q + 1)
                        if g == groups_at(i, j)[0]:
                            lowpart(n + 1, j + 1)
                ahead_at(n + CV, CV + j)

            for q in range(QG):
                with v.Fori(0, 3) as i:
                    for j in range(4):
                        value_step(q, i, j)
                for j in range(4):
                    value_step(q, 3, j)
            add_acc("pv")
            weighted(resid_of, y_again)
            for tt in range(TT):
                next_resid(v.tensor_scalar(resid[:, tt, :], y_again[:, tt, :], rstd[:, tt:tt + 1], None,
                                           ALU.mult))
            v.wait_ge(r_ok, nr[0])

            def ffn(gu, dn, nf):
                norm(y_again)
                transposed(xh, xl, KD)
                C, U = CH[gu], UN[gu]

                def hidden(c, cmod, umod, n, b, dst):
                    ahead_at(c, cmod)
                    v.wait_ge(f_s, n + 1)
                    if not isinstance(n, int) or n >= 2:
                        v.wait_ge(f_l, n - 1)
                    v.tensor_tensor(ff[:, b, :], fs[:, b, :], ub[:, umod % 2, T:2 * T], ALU.mult
                                    ).then_inc(f_f, 1)
                    v.wait_ge(f_f, n + 1)
                    v.tensor_copy(fh[:, dst, :], ff[:, b:b + 1, :]).then_inc(u_free, 1)
                    v.wait_ge(u_free, 2 + U - nf + n + 1)
                    v.tensor_tensor(fl[:, dst, :], ff[:, b:b + 1, :], fh[:, dst, :].bitcast(F32),
                                    ALU.subtract).then_inc(f_l, 1)

                for j in range(2):
                    hidden(C + j, C + j, U + j, nf + j, j % 2, slice(j, j + 1))
                with v.Fori(0, 5) as i:
                    for j in range(2, 6):
                        hidden(i * 4 + (C + j), C + j, U + j, i * 4 + (nf + j), j % 2,
                               bass.ds(i * 4 + j, 1))
                for c in range(CH[dn], CH[dn] + 11):
                    ahead(c)
                add_norm(dn, y_again, factor=0.5)

            ffn("gu1", "dn1", 0)
            v.engine_nop().then_inc(par2_go, 1)
            norm(y_again)
            transposed(xh, xl, KD)

            def softplus(part):
                if part == 0:
                    v.wait_ge(par2, 96)
                    lamc = cols[:, 7, :]
                    link(v.tensor_scalar(lsg[:, 4, :], lamc, -1.0, None, ALU.mult))
                    v.tensor_tensor(lsg[:, 0, :], lsg[:, 4, :], lamc, ALU.min).then_inc(ls_z, 1)
                elif part == 1:
                    v.wait_ge(ls_e, 1)
                    v.tensor_scalar(lsg[:, 2, :], lsg[:, 1, :], 1.0, None, ALU.add).then_inc(ls_z, 1)
                else:
                    v.wait_ge(ls_e, 2)
                    v.wait_ge(ls_z, 2)
                    link(v.tensor_scalar(lsg[:, 2, :], lsg[:, 2, :], -1.0, None, ALU.add))
                    link(v.tensor_scalar(lsg[:, 5, :], lsg[:, 2, :], 0.0, None, ALU.is_equal))
                    link(v.tensor_tensor(lsg[:, 2, :], lsg[:, 2, :], lsg[:, 5, :], ALU.add))
                    link(v.tensor_tensor(lsg[:, 3, :], lsg[:, 3, :], lsg[:, 5, :], ALU.add))
                    link(v.reciprocal(lsg[:, 2, :], lsg[:, 2, :]))
                    link(v.tensor_tensor(lsg[:, 3, :], lsg[:, 3, :], lsg[:, 2, :], ALU.mult))
                    link(v.tensor_tensor(lsg[:, 3, :], lsg[:, 3, :], lsg[:, 1, :], ALU.mult))
                    link(v.tensor_scalar(lsg[:, 4, :], lsg[:, 4, :], 0.0, None, ALU.max))
                    link(v.tensor_tensor(lsg[:, 3, :], lsg[:, 3, :], lsg[:, 4, :], ALU.add))
                    link(v.tensor_scalar(lsg[:, 3, :], lsg[:, 3, :], -8.0, None, ALU.mult))

            def convolve(t):
                v.wait_ge(u_free, 2 + UN["in2"] + 2)
                link(v.tensor_scalar(xc[:, t, :], xin[:, t, 0:T], cols[:, 0, t:t + 1], cols[:, 4, t:t + 1],
                                     ALU.mult, ALU.add))
                for w in range(1, CONV):
                    ins = v.scalar_tensor_tensor(xc[:, t, :], xin[:, t, w:w + T], cols[:, w, t:t + 1],
                                                 xc[:, t, :], ALU.mult, ALU.add)
                    if w < CONV - 1:
                        link(ins)
                ins.then_inc(xc_ok, 1)

            for u in range(7):
                ahead(CH["in2"] + u)
                if u == 1:
                    softplus(0)
                if u >= 3:
                    convolve(u - 3)
                if u == 3:
                    softplus(1)
                if u == 5:
                    softplus(2)
            def win_bias(n):
                biased(n, 24, s2_sb, lambda n, r: m2[:, :], smx2,
                       lambda n, r: nsink[:, n // 2, r:r + 1])

            def win_weights(n):
                b = n % 2
                v.wait_ge(at_sk, 2 * n + 2)
                v.wait_ge(at_ex, 2 * (24 + n) + 2)
                if n >= 4:
                    v.wait_ge(at_d, 24 + n - 3)
                link(v.tensor_tensor(rs2[:, b, :], rs2[:, b, :], es2[:, b, :], ALU.add))
                v.reciprocal(rr2[:, n % 4, :], rs2[:, b, :]).then_inc(at_a, 1)

            v.wait_ge(x2_sb, 3)
            link(v.tensor_scalar(nsink[:, :, :], sinkb[:, :, :], -1.0, None, ALU.mult))
            win_bias(0)
            for t in range(LT):
                v.wait_ge(rg_sb, t + 1)
                ins = v.tensor_scalar(la[:, t, :], gr[:, t, :], lsg[:, 3, t:t + 1], None, ALU.mult)
            ins.then_inc(la_ok, 1)

            def lru_beside(n):
                if n == 0:
                    v.wait_ge(xc_ok, LT)
                    link(v.tensor_tensor(gi[:, :, :], gi[:, :, :], xc[:, :, :], ALU.mult))
                elif n == 1:
                    v.wait_ge(la_e, 2)
                    link(v.tensor_tensor(gr[:, :, :], la[:, :, :], la[:, :, :], ALU.mult))
                    v.scalar_tensor_tensor(th[:, :, :], gr[:, :, :], 1.0, th[:, :, :], ALU.add, ALU.mult
                                           ).then_inc(m2_ok, 1)
                elif n == 4:
                    v.wait_ge(mu_ok, 1)
                    link(v.tensor_tensor(gi[:, :, :], gi[:, :, :], th[:, :, :], ALU.mult))
                    for t in range(2):
                        ins = v.tensor_tensor_scan(hs[:, t, :], la[:, t, :], gi[:, t, :], 0.0, ALU.mult, ALU.add)
                elif n == 5:
                    for t in range(2, 4):
                        ins = v.tensor_tensor_scan(hs[:, t, :], la[:, t, :], gi[:, t, :], 0.0, ALU.mult, ALU.add)
                    link(ins)
                    v.wait_ge(u_free, 2 + UN["in2"] + 4)
                    link(v.tensor_tensor(hs[:, :, :], hs[:, :, :], gl[:, :, :], ALU.mult))
                elif n == 6:
                    v.tensor_tensor(gr[:, :, :], hs[:, :, :], hs[:, :, :], ALU.mult).then_inc(yq_ok, 1)

            for n in range(8):
                if n + 1 < 8:
                    win_bias(n + 1)
                win_weights(n)
                lru_beside(n)
            v.wait_ge(ss_ps, 1)
            link(v.tensor_scalar(wv[:, :], acc[:, 1, 0:T], 1.0 / 512, EPS, ALU.mult, ALU.add))
            rsqrt(wr_[:, :], wv[:, :], wi_[:, :], wa_[:, :], wb_[:, :])
            for t in range(LT):
                ins = v.scalar_tensor_tensor(hs[:, t, :], hs[:, t, :], cols[:, 8, t:t + 1], wr_[:, :],
                                             ALU.mult, ALU.mult)
            link(ins)
            link(v.tensor_copy(xh[:, 0:LT, :], hs[:, :, :]))
            v.tensor_tensor(xl[:, 0:LT, :], hs[:, :, :], xh[:, 0:LT, :].bitcast(F32), ALU.subtract
                            ).then_inc(yl_ok, 1)
            v.wait_ge(at_d, 32)
            o2f = o2[:, :, :, :].rearrange("p a b c -> p a (b c)")
            rms(o2f, o2f, y_again[:, 0, 0:512], width=512)
            go_transpose()
            ahead(CH["wo"])
            transposed(xh, xl, 4, to=4, bank=ub)
            for c in range(CH["wo"] + 1, CH["wo"] + 4):
                ahead(c)
            add_norm("wo", y_again)
            ffn("gu2", "dn2", 22)

        @block.tensor
        def _(pe):
            pe.sem_inc(u_free, 2)
            pe.wait_ge(consts, 3)

            nt = [0]
            nin = [0]

            def transpose(src, tiles, bank=acc):
                nin[0] += 2
                pe.wait_ge(t_in, nin[0])
                if nt[0]:
                    pe.wait_ge(t_low, nt[0])
                for g in range(tiles // 2):
                    for k in range(2):
                        for tt in range(TT):
                            col = (2 * g + k) * P
                            last = pe.transpose(bank[:, g, k * T + tt * P:k * T + tt * P + P],
                                                src[:, tt, col:col + P], ident[:, :])
                    last.then_inc(t_ps, 1)
                    nt[0] += 1

            def three(dst, stand, move, first, last):
                (sh, sl), (mh, ml) = stand, move
                pe.matmul(dst, sh, mh, start=first, stop=False)
                pe.matmul(dst, sh, ml, start=False, stop=False)
                return pe.matmul(dst, sl, mh, start=False, stop=last)

            def unit_tile(slot, ubank, t, kt=KD, at=0, sh=xh, sl=xl, fresh=False):
                for k in range(kt):
                    if fresh and t == 0 and k % 2 == 0:
                        pe.wait_ge(t_low, nt[0] - (kt - k) // 2 + 1)
                    o = at + (t * kt + k) * P
                    last = three(ub[:, ubank, t * T:t * T + T],
                                 (wh[:, slot, o:o + P], wl[:, slot, o:o + P]),
                                 (sh[:, k, :], sl[:, k, :]), k == 0, k == kt - 1)
                return last

            def unit(slot, u, ubank, kt=KD, at=0, sh=xh, sl=xl, tiles=2, fresh=False):
                if u is not None:
                    pe.wait_ge(u_free, u + 1)
                for t in range(tiles):
                    last = unit_tile(slot, ubank, t, kt, at, sh, sl, fresh)
                return last

            def unit_chunk(c, cmod, u, umod, tiles=2, fresh=False):
                pe.wait_ge(w_low, c + 1)
                unit(cmod % RING, u, umod % 2, tiles=tiles, fresh=fresh).then_inc(c_done, 1)

            def acc_chunk(c, cmod, sh, sl, k0, first, last, width=2):
                pe.wait_ge(w_low, c + 1)
                slot = cmod % RING
                for k in range(4 // width):
                    for tt in range(TT):
                        for nb in range(width):
                            o = (k * width + nb) * 512
                            tok = slice(tt * P, tt * P + P)
                            ins = three(acc[:, tt * width + nb, :],
                                        (sh[:, k0 + k, tok], sl[:, k0 + k, tok]),
                                        (wh[:, slot, o:o + 512], wl[:, slot, o:o + 512]),
                                        first and k == 0, last and k == 4 // width - 1)
                ins.then_inc(c_done, 1)

            transpose(y, KD)
            pe.wait_ge(t_low, nt[0])
            with pe.Fori(0, 3) as i:
                for j in range(4):
                    unit_chunk(i * 4 + j, j, i * 4 + j, j)
            for k in range(4):
                acc_chunk(CH["vd"] + k, CH["vd"] + k, xh, xl, 2 * k, k == 0, k == 3)
            pe.wait_ge(c_read, 1)
            for k in range(2):
                acc_chunk(CH["vc"] + k, CH["vc"] + k, xh, xl, 4 * k, k == 0, k == 1, width=1)

            def attention(count, n0, q_of, k_of, pb_, pt_, v_of, single_of, first=None, beside=None):
                def scores(n):
                    b = n % 2
                    nk = P * (1 + b)
                    if n >= 2:
                        pe.wait_ge(at_b, n0 + n - 1)
                    for r in range(2):
                        rows = slice(SUB * r, SUB * r + SUB)
                        last = pe.matmul(acc[:, 2 * b + r, 0:nk], q_of(n)[rows, b * P:b * P + P],
                                         k_of(n)[rows, 0:nk], start=True, stop=True)
                    last.then_inc(at_sc, 1)

                def turn(n):
                    b = n % 2
                    pe.wait_ge(at_a, n0 + n + 1)
                    at = 0
                    for r in range(1 if single_of(n) else 2):
                        for kb in range(1 + b):
                            last = pe.transpose(mb[:, 0, at:at + P], pb_[:, b, r, kb * P:kb * P + P],
                                                ident[:, :])
                            at += P
                    last.then_inc(at_t, 1)

                def output(n):
                    b = n % 2
                    pe.wait_ge(at_v, n0 + n + 1)
                    if n >= 2:
                        pe.wait_ge(at_d, n0 + n - 1)
                    parts = 1 if single_of(n) else 2
                    w = P // parts
                    for r in range(parts):
                        for kb in range(1 + b):
                            last = pe.matmul((mb, ub)[b][:, 1, r * w:r * w + w], pt_[:, b, r * (1 + b) + kb, :],
                                             v_of(n, kb, r, w), start=kb == 0, stop=kb == b)
                    last.then_inc(at_o, 1)

                scores(0)
                if first is not None:
                    first()
                for n in range(count):
                    if n + 1 < count:
                        scores(n + 1)
                    if n >= 1:
                        output(n - 1)
                    if beside is not None:
                        beside(n)
                    turn(n)
                output(count - 1)

            pe.wait_ge(c_read, 2)

            def v1(n, kb, r, w):
                j = (n % 16) // 2
                return (vd if n < 16 else vc)[:, kb, j * P + r * w:j * P + r * w + w]

            def gates_beside(n):
                g, t = n // 3, n % 3
                if t < 2:
                    c, u = CH["gate"] + g, UN["gate"] + g
                    if t == 0:
                        pe.wait_ge(w_low, c + 1)
                        pe.wait_ge(u_free, u + 2)
                    last = unit_tile(c % RING, 0, t)
                    if t == 1:
                        last.then_inc(c_done, 1)

            attention(24, 0, lambda n: qkT[:, n // 2 if n < 16 else 16 + (n - 16) // 2, :],
                      lambda n: qkT[:, 8 + n // 2 if n < 16 else 20 + (n - 16) // 2, :],
                      p_sb, pT, v1, lambda n: n < 16, beside=gates_beside)
            pe.wait_ge(at_d, 24)
            transpose(y, KD)
            transpose(oc[:, :, :, :].rearrange("p a b c -> p a (b c)"), 4)
            pe.wait_ge(t_low, nt[0])
            for u in range(4):
                pe.wait_ge(w_low, CH["bd"] + u + 1)
                n = UN["bd"] + u
                unit((CH["bd"] + u) % RING, n, n % 2, sh=odh, sl=odl).then_inc(c_done, 1)
            for c in range(CH["bc"], CH["bc"] + 2):
                pe.wait_ge(w_low, c + 1)
                for k in range(2):
                    n = UN["bc"] + 2 * (c - CH["bc"]) + k
                    last = unit(c % RING, n, n % 2, kt=4, at=k * 2 * 4 * P, sh=och, sl=ocl)
                last.then_inc(c_done, 1)
            pe.wait_ge(bt_done, 4)
            for k in range(4):
                acc_chunk(CH["out"] + k, CH["out"] + k, xh, xl, 2 * k, k == 0, k == 3)
            transpose(y, KD)
            for u in range(4):
                unit_chunk(CH["wq"] + u, CH["wq"] + u, UN["wq"] + u, UN["wq"] + u, fresh=u == 0)
            pe.wait_ge(u_free, 2 + UN["wq"] + 4)
            pe.wait_ge(keys_in, 16)
            for n in range(4):
                tt, k = n // 2, n % 2
                if n >= 2:
                    pe.wait_ge(sk_sb, n - 1)
                for s in range(2):
                    rows = slice(SUB * s, SUB * s + SUB)
                    for h in range(4):
                        last = pe.matmul(acc[:, 2 * k + s, h * NKEY:(h + 1) * NKEY],
                                         pqT[rows, 4 * k + h, tt * P:tt * P + P],
                                         keysT[rows, 4 * k + h, :], start=True, stop=True)
                last.then_inc(sk_ps, 1)
            CU, CV = CH["pu"], CH["pv"]

            def hidden_step(n, nmod):
                if not isinstance(n, int) or n >= 2:
                    pe.wait_ge(hd_g, n - 1)
                unit_chunk(n + CU, CU + nmod, None, nmod)

            def turn_indices(tt):
                pe.wait_ge(ix_in, tt + 1)
                srcs = (esel[:, 0, :], esel[:, 1, :], gate_t[:, :, :].rearrange("p h k -> p (h k)"))
                for k, src in enumerate(srcs):
                    last = pe.transpose(mb[:, tt, k * P:k * P + P], src, ident[:, :])
                last.then_inc(ix_ps, 1)

            def spread(n, b):
                pe.wait_ge(g_two, n + 1)
                if not isinstance(n, int) or n >= 2:
                    pe.wait_ge(g_sb, n - 1)
                for k in range(GT):
                    dst = mb[:, b, k * QW:k * QW + QW]
                    for part in range(3):
                        last = pe.matmul(dst, one1[:, b, :, k], g2[:, b, part, :, k],
                                         start=part == 0, stop=part == 2)
                last.then_inc(g_ps, 1)

            for n in range(16):
                hidden_step(n, n)
            hidden_step(16, 16)
            turn_indices(0)
            for n in range(17, TOPK_U):
                hidden_step(n, n)
            turn_indices(1)
            def gates_step(q, i, j):
                hidden_step(i * 4 + (TOPK_U + 16 * q + j), j)
                for g in range(2):
                    spread(i * 8 + (GROUPS * q + 2 * j + g), g)

            for j in range(4):
                gates_step(0, 0, j)
            for q in range(2):
                with pe.Fori(1 - q, 4) as i:
                    for j in range(4):
                        gates_step(q, i, j)

            def value_step(q, i, j, first=False, last=False):
                n = i * 4 + (16 * q + j)
                pe.wait_ge(a_l, n + 1)
                acc_chunk(n + CV, CV + j, ah[:, j % 2, :, :], al[:, j % 2, :, :], 0, first, last)
                if q in (1, 2):
                    for g in groups_at(i, j):
                        spread(i * 8 + (GROUPS * (q + 1) + g), g % 2)

            for q in range(QG):
                if q == 0:
                    for j in range(4):
                        value_step(0, 0, j, first=j == 0)
                with pe.Fori(1 if q == 0 else 0, 3) as i:
                    for j in range(4):
                        value_step(q, i, j)
                for j in range(4):
                    value_step(q, 3, j, last=q == QG - 1 and j == 3)

            def ffn(gu, dn, nf):
                transpose(y_again, KD)
                C, U = CH[gu], UN[gu]
                for j in range(2):
                    unit_chunk(C + j, C + j, U + j, U + j, fresh=j == 0)
                with pe.Fori(0, 5) as i:
                    for j in range(2, 6):
                        unit_chunk(i * 4 + (C + j), C + j, i * 4 + (U + j), U + j)
                pe.wait_ge(f_l, nf + FT)
                for k in range(11):
                    acc_chunk(CH[dn] + k, CH[dn] + k, fh, fl, 2 * k, k == 0, k == 10)

            ffn("gu1", "dn1", 0)
            transpose(y_again, KD)
            for u in range(6):
                unit_chunk(CH["in2"] + u, CH["in2"] + u, UN["in2"] + u, UN["in2"] + u, fresh=u == 0)
            c = CH["in2"] + 6
            pe.wait_ge(w_low, c + 1)
            unit(c % RING, UN["in2"] + 6, (UN["in2"] + 6) % 2, tiles=1)
            for tt in range(TT):
                for k in range(KD):
                    o = (KD + k) * P
                    tok = slice(tt * P, tt * P + P)
                    last = three(mb[:, tt, 0:P], (xh[:, k, tok], xl[:, k, tok]),
                                 (wh[:, c % RING, o:o + P], wl[:, c % RING, o:o + P]), k == 0, k == KD - 1)
            last.then_inc(c_done, 1)
            def lru_gates():
                pe.wait_ge(par2, 96)
                pe.wait_ge(v2_sb, 1)
                for t in range(LT):
                    pe.wait_ge(xc_ok, t + 1)
                    dst = (ub, mb)[t // 2][:, t % 2, :]
                    pe.matmul(dst[:, 0:T], bd[:, 0, t, :], xc[:, t, :], start=True, stop=True)
                    pe.matmul(dst[:, T:2 * T], bd[:, 1, t, :], xc[:, t, :], start=True, stop=True
                              ).then_inc(rg_ps, 1)
                pe.wait_ge(rg_sb, LT)

            pe.wait_ge(u_free, 2 + UN["in2"] + 7)
            attention(8, 24, lambda n: q2T[:, n // 2, :], lambda n: q2T[:, 4, :], p2_sb, p2T,
                      lambda n, kb, r, w: v2[:, kb, r * SUB:r * SUB + SUB], lambda n: False, first=lru_gates)
            pe.wait_ge(at_b, 32)
            pe.wait_ge(yq_ok, 1)
            for t in range(LT):
                last = pe.matmul(acc[:, 1, 0:T], ones[:, :], gr[:, t, :], start=t == 0, stop=t == LT - 1)
            last.then_inc(ss_ps, 1)
            pe.wait_ge(yl_ok, 1)
            pe.wait_ge(at_d, 32)
            for k in range(2):
                acc_chunk(CH["wo"] + k, CH["wo"] + k, xh, xl, 2 * k, k == 0, False)
            transpose(o2[:, :, :, :].rearrange("p a b c -> p a (b c)"), 4, bank=ub)
            pe.wait_ge(t_low, nt[0])
            for k in range(2, 4):
                acc_chunk(CH["wo"] + k, CH["wo"] + k, xh, xl, 2 * k, False, k == 3)
            ffn("gu2", "dn2", FT)


def layout(inputs):
    n = {k: np.asarray(a) for k, a in inputs.items()}

    def tiles(w):
        k, m = w.shape
        return w.reshape(k // P, P, m // P, P).transpose(2, 1, 0, 3)

    def chunks(t):
        per = CW // (t.shape[2] * P)
        return t.reshape(t.shape[0] // per, per, P, -1).transpose(0, 2, 1, 3).reshape(-1, P, CW)

    def wide(w):
        k, m = w.shape
        per = CW // m
        return w.reshape(k // P // per, per, P, m).transpose(0, 2, 1, 3).reshape(-1, P, CW)

    w_in = n["w_in"][0]
    s = np.split(w_in, [1024, 2048, 3072, 3584, 4096, 4608], axis=1)
    qd, kd, vd, qc, kc, vc, gates = s
    parts = {
        "qk": chunks(tiles(np.concatenate([qd, kd, qc, kc], axis=1))),
        "vd": wide(vd), "vc": wide(vc), "gate": chunks(tiles(gates)),
        "bd": chunks(tiles(n["w_branch_diff"][0])), "bc": chunks(tiles(n["w_branch_chunk"][0])),
        "out": wide(n["w_out"][0]), "wq": chunks(tiles(n["peer_wq"][0])),
    }
    u = n["peer_u"][0].reshape(NKEY, NKEY, KD, P).transpose(1, 3, 2, 0)
    u = u.reshape(NKEY // 2, 2, P, D).transpose(0, 2, 1, 3).reshape(NKEY // 2, P, CW)
    w = n["peer_v"][0].reshape(NKEY, NKEY // 2, 2 * D).transpose(1, 0, 2)
    parts["pu"], parts["pv"] = np.concatenate([u[4:], u[:4]], axis=0), w
    for name, b in (("1", "ffn1"), ("2", "ffn2")):
        gu = tiles(n[f"{b}_w_gu_2"][0]).reshape(2, FT, P, D).transpose(1, 2, 0, 3).reshape(FT, P, CW)
        parts["gu" + name] = gu
        parts["dn" + name] = wide(n[f"{b}_w_down_2"][0])
    w2 = n["w_in_2"][0]

    def by_pair(a, axis):
        shape = a.shape[:axis] + (2, 4, SUB) + a.shape[axis + 1:]
        return a.reshape(shape).swapaxes(axis, axis + 1).reshape(a.shape)

    w2 = np.concatenate([w2[:, :1024], by_pair(w2[:, 1024:1536], 1), w2[:, 1536:]], axis=1)
    parts["in2"] = chunks(tiles(w2))
    wo = n["w_o_2"][0]
    parts["wo"] = wide(np.concatenate([wo[:512], by_pair(wo[512:], 0)], axis=0))
    stream = np.concatenate([np.asarray(parts[name]) for name, _ in _sizes], axis=0)

    def columns(a):
        return np.ascontiguousarray(a.reshape(-1, P).T)

    rev = np.pad(n["chunk_rel_bias"][0][:, ::-1], ((0, 0), (P - 1, P - 1)), mode="edge")
    rel = np.stack([rev[:, P - 1 - q:P - 1 - q + T] for q in range(P)])
    A = {
        "wstream": stream, "x": n["x"][0],
        "lq": np.concatenate([n["diff_lq1"], n["diff_lk1"], n["diff_lq2"], n["diff_lk2"]], axis=1),
        "subln": n["diff_subln_w"], "b_gate": columns(n["b_gate"][0]), "rel": rel,
        "keys": n["peer_keys"][0].transpose(1, 3, 0, 2).reshape(P, PEER_H, NKEY),
        "sinks": n["sinks_2"].reshape(1, 2, 4).transpose(0, 2, 1).reshape(1, 8),
        "cols": np.stack([columns(n["conv_w_2"][0][k]) for k in range(CONV)]
                         + [columns(n[k][0]) for k in ("conv_b_2", "b_rg_2", "b_ig_2", "lru_lambda_2",
                                                       "g_lru_out_2")], axis=1),
        "w_rg": n["w_rg_2"][0].reshape(LT, 2, SUB, SUB).transpose(1, 2, 0, 3),
        "w_ig": n["w_ig_2"][0].reshape(LT, 2, SUB, SUB).transpose(1, 2, 0, 3),
        "g_attn": by_pair(n["g_attn_out_2"], 1),
    }
    for name in NORMS:
        if name not in A:
            A[name] = n[name].reshape(1, D)
    return {k: np.ascontiguousarray(a) for k, a in A.items()}


def kernel(**inputs):
    import concourse.bacc as _bacc
    from concourse.bass_utils import run_bass_kernel_spmd as _run

    arrays = layout(inputs)
    nc = _bacc.Bacc("TRN2", target_bir_lowering=False, num_devices=1)
    A = {k: nc.dram_tensor(f"in_{k}", a.shape, mybir.dt.from_np(a.dtype), kind="ExternalInput").ap()
         for k, a in arrays.items()}
    out = nc.dram_tensor("out_x", (T, D), F32, kind="ExternalOutput").ap()
    build_program(nc, A, out)
    r = _run(nc, [{f"in_{k}": a for k, a in arrays.items()}], core_ids=[0])
    return r.results[0]["out_x"].reshape(1, T, D)
```
